# Optimizing a Trainium2 kernel written in Bass

```python
import math
import jax, jax.numpy as jnp
from jax import lax
import numpy as np

D_MODEL = 1024
BATCH = 1
SEQ = 1024
DEPTH = 1

N_MIXERS = 2
N_HYENA_LAYERS = (DEPTH + N_MIXERS - 1) // N_MIXERS
N_NA_LAYERS = DEPTH // N_MIXERS
GRID_W = 64
RMS_EPS = 1e-6
HY_SHORT_CONV = 3
HY_EMB_DIM = 33
HY_N_BANDS = (HY_EMB_DIM - 1) // 2
HY_FILTER_WIDTH = 64
HY_FAST_DECAY_PCT = 0.3
HY_SLOW_DECAY_PCT = 1.5
HY_DECAY_TARGET = 1e-2
NA_HEADS = 16
NA_HEAD_DIM = D_MODEL // NA_HEADS
NA_KH = 8
NA_KW = 16
FFN_HIDDEN = -(-8 * D_MODEL // (3 * 256)) * 256


def rmsnorm(x, g):
    x32 = x.astype(jnp.float32)
    y = x32 * lax.rsqrt(jnp.mean(x32 * x32, axis=-1, keepdims=True) + RMS_EPS)
    return (y * g.astype(jnp.float32)).astype(x.dtype)

def short_conv(z, w, b):
    c = z.shape[-1]
    pad = HY_SHORT_CONV // 2
    y = lax.conv_general_dilated(
        z, w[:, None, :].astype(z.dtype), window_strides=(1,), padding=((pad, pad),),
        dimension_numbers=("NWC", "WIO", "NWC"), feature_group_count=c)
    return y + b

def hyena_filter(L, w1, b1, w2, b2, w3, b3, freq, w_out, decay):
    f32 = jnp.float32
    t = jnp.linspace(0.0, 1.0, L, dtype=f32)[:, None]
    w = 2.0 * math.pi * jnp.arange(L, dtype=f32)[:, None] / L
    bands = jnp.linspace(1e-4, HY_N_BANDS - 1, HY_N_BANDS, dtype=f32)[None, :]
    feat = jnp.concatenate([t, jnp.cos(bands * w), -jnp.sin(bands * w)], axis=-1)
    fr = freq.astype(f32)
    act = lambda a: jnp.sin(fr * a)
    h = act(feat @ w1.astype(f32) + b1.astype(f32))
    h = act(h @ w2.astype(f32) + b2.astype(f32))
    h = act(h @ w3.astype(f32) + b3.astype(f32))
    h = (h @ w_out.astype(f32)).reshape(L, 2, D_MODEL)
    h = h * jnp.exp(-t[:, :, None] * jnp.abs(decay.astype(f32)))
    g = jnp.concatenate([h[:, 0], jnp.zeros((1, D_MODEL), f32), jnp.flip(h[1:, 1], axis=0)], axis=0)
    return g / jnp.sum(jnp.abs(g), axis=0, keepdims=True)

def hyena_mixer(u, w_in, b_in, conv_w, conv_b, f_w1, f_b1, f_w2, f_b2, f_w3, f_b3,
                f_freq, f_wout, decay, skip, w_out, b_out):
    L = u.shape[1]
    z = short_conv(u @ w_in + b_in, conv_w, conv_b)
    x0, x1, v = jnp.split(z, 3, axis=-1)
    s = (v * x1).astype(jnp.float32)
    g = hyena_filter(L, f_w1, f_b1, f_w2, f_b2, f_w3, f_b3, f_freq, f_wout, decay)
    n = 2 * L
    y = jnp.fft.irfft(jnp.fft.rfft(s, n=n, axis=1) * jnp.fft.rfft(g, n=n, axis=0)[None],
                      n=n, axis=1)[:, :L]
    y = (y + s * skip.astype(jnp.float32)).astype(u.dtype) * x0
    return y @ w_out + b_out

def na_mixer(u, w_qkv, b_qkv, rpb, w_o, b_o):
    B_, L, D = u.shape
    rows = L // GRID_W
    kh = min(NA_KH, rows)
    kw = NA_KW
    qkv = u @ w_qkv + b_qkv
    q, k, v = [a.reshape(B_, rows, GRID_W, NA_HEADS, NA_HEAD_DIM) for a in jnp.split(qkv, 3, axis=-1)]
    q = q * (NA_HEAD_DIM ** -0.5)
    col = jnp.arange(GRID_W)
    col_start = jnp.clip(col - kw // 2, 0, GRID_W - kw)
    col_idx = col_start[:, None] + jnp.arange(kw)[None, :]
    col_off = col_idx - col[:, None] + (NA_KW - 1)

    def row_block(r):
        r_start = jnp.clip(r - kh // 2, 0, rows - kh)
        k_rows = lax.dynamic_slice_in_dim(k, r_start, kh, axis=1)
        v_rows = lax.dynamic_slice_in_dim(v, r_start, kh, axis=1)
        k_win = k_rows[:, :, col_idx]
        v_win = v_rows[:, :, col_idx]
        q_r = lax.dynamic_index_in_dim(q, r, axis=1, keepdims=False)
        s = jnp.einsum("bwhd,biwjhd->bhwij", q_r, k_win)
        row_off = r_start + jnp.arange(kh) - r + (NA_KH - 1)
        bias = rpb[:, row_off[None, :, None], col_off[:, None, :]]
        s = (s + bias[None]).astype(jnp.float32).reshape(B_, NA_HEADS, GRID_W, kh * kw)
        p = jax.nn.softmax(s, axis=-1).reshape(B_, NA_HEADS, GRID_W, kh, kw).astype(v.dtype)
        return jnp.einsum("bhwij,biwjhd->bwhd", p, v_win)

    out = lax.map(row_block, jnp.arange(rows))
    out = jnp.transpose(out, (1, 0, 2, 3, 4)).reshape(B_, L, D)
    return out @ w_o + b_o

def swiglu(x, w_gate, w_up, w_down):
    return (jax.nn.silu(x @ w_gate) * (x @ w_up)) @ w_down

def first_inputs(seed: int = 0) -> dict:
    key = jax.random.key(seed)
    ks = iter(jax.random.split(key, 40))
    nrm = lambda shape, scale: scale * jax.random.normal(next(ks), shape, jnp.float32)
    D, F, NH, NN = D_MODEL, FFN_HIDDEN, N_HYENA_LAYERS, N_NA_LAYERS
    base_decay = jnp.abs(jnp.linspace(math.log(HY_DECAY_TARGET) / HY_SLOW_DECAY_PCT,
                                      math.log(HY_DECAY_TARGET) / HY_FAST_DECAY_PCT, D, dtype=jnp.float32))
    return {
        "x": nrm((BATCH, SEQ, D), 1.0),
        "norm_mix": 1.0 + nrm((DEPTH, D), 0.02),
        "norm_ffn": 1.0 + nrm((DEPTH, D), 0.02),
        "norm_final": 1.0 + nrm((D,), 0.02),
        "hy_w_in": nrm((NH, D, 3 * D), D ** -0.5),
        "hy_b_in": nrm((NH, 3 * D), 0.02),
        "hy_conv_w": nrm((NH, HY_SHORT_CONV, 3 * D), HY_SHORT_CONV ** -0.5),
        "hy_conv_b": nrm((NH, 3 * D), 0.02),
        "hy_f_w1": nrm((NH, HY_EMB_DIM, HY_FILTER_WIDTH), HY_EMB_DIM ** -0.5),
        "hy_f_b1": nrm((NH, HY_FILTER_WIDTH), 0.02),
        "hy_f_w2": nrm((NH, HY_FILTER_WIDTH, HY_FILTER_WIDTH), HY_FILTER_WIDTH ** -0.5),
        "hy_f_b2": nrm((NH, HY_FILTER_WIDTH), 0.02),
        "hy_f_w3": nrm((NH, HY_FILTER_WIDTH, HY_FILTER_WIDTH), HY_FILTER_WIDTH ** -0.5),
        "hy_f_b3": nrm((NH, HY_FILTER_WIDTH), 0.02),
        "hy_f_freq": 1.0 + nrm((NH, HY_FILTER_WIDTH), 0.02),
        "hy_f_wout": nrm((NH, HY_FILTER_WIDTH, 2 * D), HY_FILTER_WIDTH ** -0.5),
        "hy_decay": base_decay * (1.0 + nrm((NH, 2, D), 0.05)),
        "hy_skip": nrm((NH, D), 0.5),
        "hy_w_out": nrm((NH, D, D), D ** -0.5),
        "hy_b_out": nrm((NH, D), 0.02),
        "na_w_qkv": nrm((NN, D, 3 * D), D ** -0.5),
        "na_b_qkv": nrm((NN, 3 * D), 0.02),
        "na_rpb": nrm((NN, NA_HEADS, 2 * NA_KH - 1, 2 * NA_KW - 1), 0.02),
        "na_w_o": nrm((NN, D, D), D ** -0.5),
        "na_b_o": nrm((NN, D), 0.02),
        "ffn_w_gate": nrm((DEPTH, D, F), D ** -0.5),
        "ffn_w_up": nrm((DEPTH, D, F), D ** -0.5),
        "ffn_w_down": nrm((DEPTH, F, D), F ** -0.5),
    }

def first_block(x, norm_mix, norm_ffn, norm_final,
              hy_w_in, hy_b_in, hy_conv_w, hy_conv_b, hy_f_w1, hy_f_b1, hy_f_w2, hy_f_b2,
              hy_f_w3, hy_f_b3, hy_f_freq, hy_f_wout, hy_decay, hy_skip, hy_w_out, hy_b_out,
              na_w_qkv, na_b_qkv, na_rpb, na_w_o, na_b_o,
              ffn_w_gate, ffn_w_up, ffn_w_down):
    for i in range(DEPTH):
        h = rmsnorm(x, norm_mix[i])
        j = i // N_MIXERS
        if i % N_MIXERS == 0:
            mixed = hyena_mixer(h, hy_w_in[j], hy_b_in[j], hy_conv_w[j], hy_conv_b[j],
                                hy_f_w1[j], hy_f_b1[j], hy_f_w2[j], hy_f_b2[j], hy_f_w3[j], hy_f_b3[j],
                                hy_f_freq[j], hy_f_wout[j], hy_decay[j], hy_skip[j],
                                hy_w_out[j], hy_b_out[j])
        else:
            mixed = na_mixer(h, na_w_qkv[j], na_b_qkv[j], na_rpb[j], na_w_o[j], na_b_o[j])
        x = x + mixed
        x = x + swiglu(rmsnorm(x, norm_ffn[i]), ffn_w_gate[i], ffn_w_up[i], ffn_w_down[i])
    return rmsnorm(x, norm_final)


CTX_LEN = 256

GLA_HEADS = 4
GLA_DK = 128
GLA_DV = 256
GLA_KW = GLA_HEADS * GLA_DK
GLA_VW = GLA_HEADS * GLA_DV
GATE_RANK = 16
GATE_NORM = 16.0
CHUNK = 64
ROPE_BASE = 10000.0

POOL_WINDOWS = (2, 4, 8, 16)
POOL_GROUPS = 4
POOL_W = D_MODEL
POOL_GW = POOL_W // POOL_GROUPS

EPS = 1e-6

IN_SPLITS = (GLA_KW, GLA_KW, GLA_VW, GLA_VW, GATE_RANK, GATE_RANK, POOL_W, POOL_W, D_MODEL, D_MODEL)
D_IN = 2 * GLA_KW + 2 * GLA_VW + 2 * GATE_RANK + 2 * POOL_W + 2 * D_MODEL


def rmsnorm_2(x, g):
    xf = x.astype(jnp.float32)
    y = xf * lax.rsqrt(jnp.mean(xf * xf, axis=-1, keepdims=True) + EPS)
    return (y * g.astype(jnp.float32)).astype(x.dtype)

def rope_2d(t, row, col):
    half = GLA_DK // 2
    nf = half // 2
    freqs = ROPE_BASE ** (-jnp.arange(nf, dtype=jnp.float32) / nf)

    def rot(xp, pos):
        ang = pos[:, None] * freqs
        cos = jnp.cos(ang)[None, :, None, :]
        sin = jnp.sin(ang)[None, :, None, :]
        xa, xb = xp[..., :nf], xp[..., nf:]
        return jnp.concatenate([xa * cos - xb * sin, xa * sin + xb * cos], axis=-1)

    return jnp.concatenate([rot(t[..., :half], row), rot(t[..., half:], col)], axis=-1)

def gla_chunked(q, k, v, log_a, s0, with_output):
    B, L, H, DK = q.shape
    n = L // CHUNK

    def to_chunks(t):
        return t.astype(jnp.float32).reshape(B, n, CHUNK, H, t.shape[-1]).transpose(1, 0, 3, 2, 4)

    tri = jnp.tril(jnp.ones((CHUNK, CHUNK), dtype=bool))

    def step(S, inp):
        qc, kc, vc, ac = inp
        b = jnp.cumsum(ac, axis=2)
        bC = b[:, :, -1:, :]
        S_new = jnp.exp(bC[:, :, 0, :, None]) * S + jnp.einsum(
            'bhjd,bhjv->bhdv', kc * jnp.exp(bC - b), vc)
        if not with_output:
            return S_new, None
        diff = b[:, :, :, None, :] - b[:, :, None, :, :]
        decay = jnp.exp(jnp.where(tri[:, :, None], diff, -jnp.inf))
        scores = jnp.einsum('bhid,bhjd,bhijd->bhij', qc, kc, decay)
        o = jnp.einsum('bhij,bhjv->bhiv', scores, vc) + jnp.einsum(
            'bhid,bhdv->bhiv', qc * jnp.exp(b), S)
        return S_new, o

    S, o = lax.scan(step, s0, (to_chunks(q), to_chunks(k), to_chunks(v), to_chunks(log_a)))
    if not with_output:
        return None, S
    o = o.transpose(1, 0, 3, 2, 4).reshape(B, L, H, v.shape[-1])
    return o, S

def gla_bidir(q, k, v, la_f, la_b, s0_f, s0_b, with_output):
    flip = lambda t: t[:, ::-1]
    o_f, s_f = gla_chunked(q, k, v, la_f, s0_f, with_output)
    o_b, s_b = gla_chunked(flip(q), flip(k), flip(v), flip(la_b), s0_b, with_output)
    o = o_f + flip(o_b) if with_output else None
    return o, s_f, s_b

def gla_log_decay(lowrank, w_up, b):
    B, L, _ = lowrank.shape
    gk = (lowrank @ w_up + b).astype(jnp.float32)
    return (jax.nn.log_sigmoid(gk) / GATE_NORM).reshape(B, L, GLA_HEADS, GLA_DK)

def mixer_inputs(h, w_in, w_up_f, b_f, w_up_b, b_b, row, col):
    B, L, _ = h.shape
    p = h @ w_in
    idx = np.cumsum(IN_SPLITS)[:-1].tolist()
    pq, pk, pv, zA, lr_f, lr_b, uB, zB, gA, gB = jnp.split(p, idx, axis=-1)
    q = pq.reshape(B, L, GLA_HEADS, GLA_DK) * (GLA_DK ** -0.5)
    k = pk.reshape(B, L, GLA_HEADS, GLA_DK)
    if row is not None:
        q = rope_2d(q, row, col)
        k = rope_2d(k, row, col)
    v = pv.reshape(B, L, GLA_HEADS, GLA_DV)
    la_f = gla_log_decay(lr_f, w_up_f, b_f)
    la_b = gla_log_decay(lr_b, w_up_b, b_b)
    return q, k, v, la_f, la_b, zA, uB, zB, gA, gB

def multiscale_pool(u, w_pool, pool_scale):
    B, L, _ = u.shape
    uf = u.astype(jnp.float32)
    cs = jnp.concatenate([jnp.zeros_like(uf[:, :1]), jnp.cumsum(uf, axis=1)], axis=1)
    t = jnp.arange(L)
    parts = []
    for g, w in enumerate(POOL_WINDOWS):
        lo = jnp.clip(t - w // 2, 0, L - 1)
        hi = jnp.clip(t + (w - 1 - w // 2), 0, L - 1)
        sl = slice(g * POOL_GW, (g + 1) * POOL_GW)
        csg = cs[..., sl]
        cnt = (hi - lo + 1).astype(jnp.float32)[:, None]
        parts.append((csg[:, hi + 1] - csg[:, lo]) / cnt - uf[..., sl])
    d = jnp.stack(parts, axis=2)
    y = jnp.einsum('blgc,gcd->blgd', d, w_pool.astype(jnp.float32)).reshape(B, L, POOL_W)
    return (y * pool_scale.astype(jnp.float32)).astype(u.dtype)

def branch_out(o, zA, uB, zB, gA, gB, gla_norm_g, w_pool, pool_scale, w_branch_a, w_branch_b, w_out):
    B, L, _ = zA.shape
    o_n = rmsnorm_2(o, gla_norm_g).astype(zA.dtype).reshape(B, L, GLA_VW)
    yA = (o_n * jax.nn.silu(zA)) @ w_branch_a
    yB = (multiscale_pool(uB, w_pool, pool_scale) * jax.nn.silu(zB)) @ w_branch_b
    merged = jax.nn.sigmoid(gA) * yA + jax.nn.sigmoid(gB) * yB
    return merged @ w_out

def second_inputs(seed: int = 0) -> dict:
    key = jax.random.key(seed)
    ks = jax.random.split(key, 24)
    f32 = jnp.float32
    nrm = lambda k, s, sc: jax.random.normal(k, s, f32) * sc
    return {
        "x": nrm(ks[0], (BATCH, SEQ, D_MODEL), 1.0),
        "c": nrm(ks[1], (BATCH, D_MODEL), 1.0),
        "ctx": nrm(ks[2], (BATCH, CTX_LEN, D_MODEL), 1.0),
        "c_ctx": nrm(ks[3], (D_MODEL,), 1.0),
        "w_mod": nrm(ks[4], (DEPTH, D_MODEL, 3 * D_MODEL), D_MODEL ** -0.5),
        "b_mod": nrm(ks[5], (DEPTH, 3 * D_MODEL), 0.01),
        "norm_g": 1.0 + nrm(ks[6], (DEPTH, D_MODEL), 0.1),
        "w_in": nrm(ks[7], (DEPTH, D_MODEL, D_IN), D_MODEL ** -0.5),
        "w_gate_up_f": nrm(ks[8], (DEPTH, GATE_RANK, GLA_KW), GATE_RANK ** -0.5),
        "b_gate_f": jax.random.uniform(ks[9], (DEPTH, GLA_KW), f32, 1.0, 5.0),
        "w_gate_up_b": nrm(ks[10], (DEPTH, GATE_RANK, GLA_KW), GATE_RANK ** -0.5),
        "b_gate_b": jax.random.uniform(ks[11], (DEPTH, GLA_KW), f32, 1.0, 5.0),
        "gla_norm_g": 1.0 + nrm(ks[12], (DEPTH, GLA_DV), 0.1),
        "w_pool": nrm(ks[13], (DEPTH, POOL_GROUPS, POOL_GW, POOL_GW), POOL_GW ** -0.5),
        "pool_scale": 1.0 + nrm(ks[14], (DEPTH, POOL_W), 0.1),
        "w_branch_a": nrm(ks[15], (DEPTH, GLA_VW, D_MODEL), GLA_VW ** -0.5),
        "w_branch_b": nrm(ks[16], (DEPTH, POOL_W, D_MODEL), POOL_W ** -0.5),
        "w_out": nrm(ks[17], (DEPTH, D_MODEL, D_MODEL), D_MODEL ** -0.5),
        "final_norm_g": 1.0 + nrm(ks[18], (D_MODEL,), 0.1),
    }

def second_block(x, c, ctx, c_ctx, w_mod, b_mod, norm_g, w_in, w_gate_up_f, b_gate_f,
              w_gate_up_b, b_gate_b, gla_norm_g, w_pool, pool_scale, w_branch_a,
              w_branch_b, w_out, final_norm_g):
    B, L, _ = x.shape
    ROWS = L // GRID_W
    t = jnp.arange(ROWS * GRID_W)
    row = (t // GRID_W).astype(jnp.float32)
    col = (t % GRID_W).astype(jnp.float32)

    for l in range(DEPTH):
        last = l == DEPTH - 1
        shift_x, scale_x, gate_x = jnp.split(jax.nn.silu(c) @ w_mod[l] + b_mod[l], 3, axis=-1)
        shift_x, scale_x, gate_x = shift_x[:, None], scale_x[:, None], gate_x[:, None]
        shift_c, scale_c, gate_c = jnp.split(jax.nn.silu(c_ctx) @ w_mod[l] + b_mod[l], 3, axis=-1)

        hc = rmsnorm_2(ctx, norm_g[l]) * (1.0 + scale_c) + shift_c
        qc, kc, vc, laf_c, lab_c, zAc, uBc, zBc, gAc, gBc = mixer_inputs(
            hc, w_in[l], w_gate_up_f[l], b_gate_f[l], w_gate_up_b[l], b_gate_b[l], None, None)
        s_zero = jnp.zeros((B, GLA_HEADS, GLA_DK, GLA_DV), jnp.float32)
        oc, s_f, s_b = gla_bidir(qc, kc, vc, laf_c, lab_c, s_zero, s_zero, not last)

        hx = rmsnorm_2(x, norm_g[l]) * (1.0 + scale_x) + shift_x
        q, k, v, la_f, la_b, zA, uB, zB, gA, gB = mixer_inputs(
            hx, w_in[l], w_gate_up_f[l], b_gate_f[l], w_gate_up_b[l], b_gate_b[l], row, col)
        ox, _, _ = gla_bidir(q, k, v, la_f, la_b, s_f, s_b, True)
        y = branch_out(ox.astype(x.dtype), zA, uB, zB, gA, gB, gla_norm_g[l], w_pool[l],
                       pool_scale[l], w_branch_a[l], w_branch_b[l], w_out[l])
        x_new = x + gate_x * y

        if not last:
            yc = branch_out(oc.astype(ctx.dtype), zAc, uBc, zBc, gAc, gBc, gla_norm_g[l], w_pool[l],
                            pool_scale[l], w_branch_a[l], w_branch_b[l], w_out[l])
            ctx = ctx + gate_c * yc
        x = x_new

    return rmsnorm_2(x, final_norm_g)


def setup_inputs(seed=0):
    out = dict(first_inputs(seed))
    for name, value in second_inputs(seed + 1).items():
        if name != "x":
            out[name + "_2"] = value
    return out


def reference(
    x, norm_mix, norm_ffn, norm_final, hy_w_in, hy_b_in, hy_conv_w, hy_conv_b, hy_f_w1, hy_f_b1,
    hy_f_w2, hy_f_b2, hy_f_w3, hy_f_b3, hy_f_freq, hy_f_wout, hy_decay, hy_skip, hy_w_out,
    hy_b_out, na_w_qkv, na_b_qkv, na_rpb, na_w_o, na_b_o, ffn_w_gate, ffn_w_up, ffn_w_down, c_2,
    ctx_2, c_ctx_2, w_mod_2, b_mod_2, norm_g_2, w_in_2, w_gate_up_f_2, b_gate_f_2,
    w_gate_up_b_2, b_gate_b_2, gla_norm_g_2, w_pool_2, pool_scale_2, w_branch_a_2, w_branch_b_2,
    w_out_2, final_norm_g_2,
):
    x = first_block(
        x, norm_mix, norm_ffn, norm_final, hy_w_in, hy_b_in, hy_conv_w, hy_conv_b, hy_f_w1,
        hy_f_b1, hy_f_w2, hy_f_b2, hy_f_w3, hy_f_b3, hy_f_freq, hy_f_wout, hy_decay, hy_skip,
        hy_w_out, hy_b_out, na_w_qkv, na_b_qkv, na_rpb, na_w_o, na_b_o, ffn_w_gate, ffn_w_up,
        ffn_w_down,
    )
    return second_block(
        x, c_2, ctx_2, c_ctx_2, w_mod_2, b_mod_2, norm_g_2, w_in_2, w_gate_up_f_2, b_gate_f_2,
        w_gate_up_b_2, b_gate_b_2, gla_norm_g_2, w_pool_2, pool_scale_2, w_branch_a_2,
        w_branch_b_2, w_out_2, final_norm_g_2,
    )


_drawn_inputs = setup_inputs


def setup_inputs(seed=0):
    import zlib

    import numpy as np

    out = dict(_drawn_inputs(seed))
    spreads = {}
    factors = {'norm_mix': 2.866,
     'norm_ffn': 10.955,
     'norm_final': 7.892,
     'hy_b_in': 3.208,
     'hy_conv_b': 3.071,
     'hy_f_b1': 8.0,
     'hy_f_b2': 8.0,
     'hy_f_b3': 8.0,
     'hy_f_freq': 8.0,
     'hy_decay': 3.054,
     'b_mod_2': 4.713,
     'hy_b_out': 8.0,
     'ctx_2': 3.375,
     'gla_norm_g_2': 5.334,
     'pool_scale_2': 5.01}
    for name, (base, spread) in spreads.items():
        noise = np.random.default_rng([zlib.crc32(name.encode()), seed]).standard_normal(out[name].shape)
        drawn = base * np.exp(spread * noise) if base else spread * noise
        out[name] = __import__('jax').numpy.asarray(drawn.astype(out[name].dtype))
    for name, factor in factors.items():
        out[name] = (out[name] * factor).astype(out[name].dtype)
    return out
```

```python
from contextlib import ExitStack

import numpy as np
import concourse.bass as bass
from concourse import mybir

F32 = mybir.dt.float32
F32R = mybir.dt.float32r
ACT = mybir.ActivationFunctionType
ALU = mybir.AluOpType
ds = bass.ds

P = 128
D = 1024
T = 1024
KT = D // P
TC = 256
F = 2816
FPARTS = (8, 8, 6)
EPS = 1e-6
HEADS, DK, DV = 4, 128, 256
CH = 128
NCH = T // CH
NCC = TC // CH
GATE_NORM = 16.0
CLAMP = 40.0 * GATE_NORM
N1, N2 = 128, 16
HALF = N1 // 2
GROUPS = 16
POOL_WINDOWS = (2, 4, 8, 16)
PAD = 8
MAGIC = 1.5 * 2.0 ** 23
C1 = 6.28125
C2 = float(np.float32(np.round((2 * np.pi - C1) * 2 ** 20) / 2 ** 20))
C3 = float(np.float32(2 * np.pi - C1 - C2))
PI_LOW = 3.1415925

VEC = {}
_c = 0
for _n, _w in (("norm_mix", 8), ("norm_ffn", 8), ("norm_final", 8), ("b_in", 24), ("cw0", 24), ("cw1", 24),
               ("cw2", 24), ("cb", 24), ("skip", 8), ("b_out", 8), ("norm2", 8), ("b_mod", 24), ("b_gf", 4),
               ("b_gb", 4), ("gla_g", 2), ("pool_scale", 8), ("final2", 8), ("f_b1", 1), ("f_b2", 1),
               ("f_b3", 1), ("f_freq", 1), ("c", 8), ("c_ctx", 8)):
    VEC[_n] = _c
    _c += _w
NVEC = _c
CST = {}
_c = 0
for _n, _w in (("ident", 128), ("ones", 128), ("mask_f", 128), ("mask_b", 128), ("perm", 128), ("dft_g", 128),
               ("dft_s", 128), ("idft", 64), ("tneg", 16), ("tmask", 16)):
    CST[_n] = _c
    _c += _w
NCST = _c

PHASES = [("norm1", 1, 0), ("mlp", 3, 0), ("taps", 32, 0), ("tapnorm", 1, 0), ("zin", 24, 24), ("sfwd", 32, 0),
          ("mod", 1, 0), ("inv", 8, 0), ("wout", 8, 8), ("norm2", 1, 0)]
for _p, _n in enumerate(FPARTS):
    PHASES += [(f"up{_p}", 2 * _n, 2 * _n), (f"down{_p}", 8, 8)]
PHASES += [("normf", 1, 0), ("norm3", 1, 0), ("normc", 1, 0), ("lr", 2, 1), ("heads", 24 * HEADS, 4 * HEADS), ("za", 8, 8),
           ("mixa", 16, 16), ("pool", 24, 16), ("mixb", 16, 16), ("wout2", 8, 8), ("norm4", 1, 0)]
J0, N0, A0 = {}, {}, {}
_j = _n_ = 0
for _name, _jobs, _pan in PHASES:
    J0[_name], N0[_name] = _j, _n_
    _j += _jobs
    _n_ += _pan
NPANELS = _n_
_a = 0
AUX = {"norm1": 1, "mlp": 3, "taps": 32, "tapnorm": 1, "sfwd": 32, "inv": 8, "norm2": 1, "normf": 1, "norm3": 1,
       "normc": 1, "lr": 1, "heads": 21 * HEADS, "pool": 8, "norm4": 1}
for _name, _, _ in PHASES:
    A0[_name] = _a
    _a += AUX.get(_name, 0)


class Steps:

    def __init__(self, eng, sem):
        self.eng, self.sem, self.n, self.base = eng, sem, 0, 0

    def do(self, ins):
        ins.then_inc(self.sem, 1)
        self.n += 1

    def wait(self):
        self.eng.wait_ge(self.sem, self.base + self.n)

    def link(self, ins):
        self.do(ins)
        self.wait()

    def enter(self, i, per):
        self.base, self.start = i * per, self.n

    def leave(self, trips, per):
        assert self.n - self.start == per, (self.n - self.start, per)
        self.base, self.n = 0, self.start + trips * per


def program(nc, d, out):
    ctx = ExitStack()
    with ctx:
        base = -(-nc.sbuf_base // 64) * 64

        def at(name, shape, offset, dt=F32):
            return nc.alloc_sbuf_tensor_at(name, shape, dt, offset=offset)

        def sem(name):
            return ctx.enter_context(nc.semaphore(name))

        o_vec = base
        o_cst = o_vec + NVEC * 4 + 8
        o_small = o_cst + NCST * 4
        o_raw = base + 5312
        o_wh = o_raw + 8192
        o_wl = o_wh + 8192
        RH = o_wl + 8192
        RA = RH + 65536
        RX = RA + 65536
        RT = RX + 32768
        assert o_small + 88 * 4 <= o_raw and RT + 19104 <= nc.sbuf_usable_end
        K = 1024
        vec = at("vec", [P, NVEC], o_vec)
        cst = at("cst", [P, NCST], o_cst)
        rn = at("rn", [P, 8], o_small)
        mod = at("mod", [P, 24, 2], o_small + 32)
        mgs = at("mgs", [P, 8, 2], o_small + 224)
        sc = at("sc", [P, 2, 8], o_small + 288)
        wraw = at("wraw", [P, 2, 8, P], o_raw)
        whi = at("whi", [P, 2, 8, P], o_wh, F32R)
        wlo = at("wlo", [P, 2, 8, P], o_wl, F32R)
        H = at("H", [P, 2, KT, T], RH, F32R)
        A = at("A", [P, 2, KT, T], RA, F32R)
        X = at("X", [P, KT, T], RX)
        TT = [at(f"T{i}", [P, T], RT + 4 * K * i) for i in range(4)]
        feat = at("feat", [66, T], RA)
        fw1 = at("fw1", [66, P], RA + 4 * K)
        fw2 = at("fw2", [P, P], RA + 4 * K + 512)
        fw3 = at("fw3", [P, P], RA + 5 * K)
        wtap = at("wtap", [P, T], RA + 6 * K)
        dec = at("dec", [P, T], RA + 10 * K)
        fa = at("fa", [P, T], RA + 14 * K)
        fu = at("fu", [P, T], RA + 18 * K)
        fh = at("fh", [P, T], RA + 22 * K)
        hb = at("hb", [P, N2, N1], RA + 26 * K)
        hbs = [at(f"hbs{u}", [P, N1], RA + 34 * K + 512 * u) for u in range(2)]
        dk_ = [at(f"decay{u}", [P, T], RA + 35 * K + 4 * K * u) for u in range(2)]
        tap = [at(f"tap{u}", [P, T], RA + 43 * K + 4 * K * u) for u in range(2)]
        gsp = [at(f"gsp{u}", [P, T], RA + 51 * K + 4 * K * u) for u in range(2)]
        gacc = at("gacc", [P, T], RA + 59 * K)
        S = at("S", [P, KT, T], RA)
        G0 = at("G0", [P, KT, T], RA + 32 * K)
        zp = [at(f"zp{u}", [P, T + 2], RT + 4128 * u) for u in range(2)]
        ca = at("ca", [P, T], RT + 8256)
        cb_ = at("cb_", [P, T], RT + 8256 + 4 * K)
        sn = [at(f"sn{u}", [P, KT, HALF], RH + 2 * K * u) for u in range(2)]
        st_ = [at(f"st{u}", [HALF, T], RH + 4 * K + 4 * K * u) for u in range(2)]
        sa = [at(f"sa{u}", [P, T], RH + 12 * K + 4 * K * u) for u in range(2)]
        mraw = at("mraw", [P, 2, 8, P], RH + 20 * K)
        kf = [at(f"kf{u}", [P, 5, P], RX + 2560 * u) for u in range(2)]
        bs = [at(f"bs{u}", [P, T], RX + 5 * K + 4 * K * u) for u in range(2)]
        bg = [at(f"bg{u}", [P, T], RX + 13 * K + 4 * K * u) for u in range(2)]
        ga = [at(f"ga{u}", [P, 512], RX + 21 * K + 2 * K * u) for u in range(2)]
        gb = [at(f"gb{u}", [P, 512], RX + 25 * K + 2 * K * u) for u in range(2)]
        t1 = [at(f"t1_{u}", [P, 512], RT + 2 * K * u) for u in range(2)]
        t2 = [at(f"t2_{u}", [P, 512], RT + 4 * K + 2 * K * u) for u in range(2)]
        yy = [at(f"yy{u}", [P, 512], RT + 8 * K + 2 * K * u) for u in range(2)]
        yi = [at(f"yi{u}", [P, 512], RT + 12 * K + 2 * K * u) for u in range(2)]
        YB = at("YB", [P, N2, T], RH)
        CX = at("CX", [P, KT, TC], RA)
        HC = at("HC", [P, 2, KT, TC], RX, F32R)
        SR = [at("SRF", [P, NCH, DV], RX + 16 * K), at("SRB", [P, NCH, DV], RX + 24 * K)]
        QT = at("QT", [P, T], RA)
        KTt = at("KT", [P, T], RA + 4 * K)
        BB = [at("BF", [P, T], RA + 8 * K), at("BB", [P, T], RA + 12 * K)]
        QD = [at("QF", [P, T], RA + 16 * K), QT]
        KD = [at("KF", [P, T], RA + 20 * K), KTt]
        V = at("V", [P, NCH, DV], RA + 24 * K)
        VC = at("VC", [P, NCC, DV], RA + 32 * K)
        KDT = [at("KFT", [P, NCH, P], RA + 34 * K), at("KBT", [P, NCH, P], RA + 38 * K)]
        SCO = TT[0:2]
        ROT = [at("ROTQ", [P, T], RA + 34 * K), at("ROTK", [P, T], RA + 38 * K)]
        KDTC = at("KDTC", [P, 2, NCC, P], RA + 42 * K)
        KC = at("KC", [P, TC], RA + 44 * K)
        BBC = at("BBC", [P, 2, TC], RA + 45 * K)
        KDC = at("KDC", [P, 2, TC], RA + 47 * K)
        COS = at("COS", [P, T], RA + 49 * K)
        SIN = at("SIN", [P, T], RA + 53 * K)
        LRT = at("LRT", [48, T + TC], RA + 57 * K)
        WUP = at("WUP", [48, HEADS * DK], RA + 62 * K)
        wup_h = at("wup_h", [48, DK], o_cst + CST["dft_g"] * 4)
        SS = [at("SF", [P, DV], RT + 16 * K), at("SB", [P, DV], RT + 17 * K)]
        o_col = RT + 18 * K
        col = [at("colf", [P, 40], o_col), at("colb", [P, 40], o_col + 160)]
        dcol = [at("dcolf", [P, 10], o_col + 320), at("dcolb", [P, 10], o_col + 384)]
        on = [at(f"on{u}", [P, T], RX + 4 * K * u) for u in range(2)]
        W_U = T + 2 * PAD
        up = [at(f"up{u}", [P, W_U], RX + 4224 * u) for u in range(2)]
        wa = at("wa", [P, W_U], RX + 8448)
        wb = at("wb", [P, W_U], RX + 12672)
        pd = [at(f"pd{u}", [P, T], RX + 16896 + 4 * K * u) for u in range(2)]
        icnt = at("icnt", [P, T], RX + 16896 + 8 * K)
        wpl = at("wpl", [P, 2, 256], RX + 16896 + 12 * K)
        assert 16896 + 14 * K <= 32 * K
        XN = at("XN", [P, KT, T], RA)

        ps = [ctx.enter_context(nc.psum_tensor(f"ps{s}", [P, 2 * 512], F32)) for s in range(4)]

        def dram(name, shape):
            return nc.dram_tensor(name, shape, F32, kind="Internal").ap()

        g1 = dram("g1", [P, N2, T])
        s1 = dram("s1", [P, N2, T])
        xs = dram("xs", [D, T])
        ond = dram("ond", [KT, P, T])
        mad = dram("mad", [KT, P, T])

        const_in, x_in, filt_in = sem("const_in"), sem("x_in"), sem("filt_in")
        raw_in = [sem("raw_in0"), sem("raw_in1")]
        hi_made, split_made = sem("hi_made"), sem("split_made")
        panel_done, aux_done = sem("panel_done"), sem("aux_done")
        evac = [sem(f"evac{s}") for s in range(4)]
        act_chain, dve_chain = sem("act_chain"), sem("dve_chain")
        ended = {e: sem(f"ended_{e}") for e in ("pe", "act", "dve")}

        def slot(phase, u):
            return (J0[phase] + u) % 4

        def turn(phase, u, i=0, per=0):
            return (J0[phase] + u) // 4 + i * (per // 4)

        def barrier(eng, name, p):
            eng.drain().then_inc(ended[name], 1)
            for other in ("pe", "act", "dve"):
                if other != name:
                    eng.wait_ge(ended[other], p)

        waited = sem("waited")

        def steady(eng):
            eng.sem_inc(waited, 1)

        class NormSems:
            def __init__(self, tag):
                self.sq, self.acc = sem(f"sq_{tag}"), sem(f"acc_{tag}")
                self.var, self.r0 = sem(f"var_{tag}"), sem(f"r0_{tag}")
                self.h, self.hi, self.lo = (sem(f"{x}_{tag}") for x in ("h", "hi", "lo"))

        n1, n2, nf1, n3, ncx, n4 = (NormSems(t) for t in ("mix", "ffn", "fin", "x2", "ctx", "fin2"))
        arg_made, sin_made, hb_zero, dec_abs = sem("arg_made"), sem("sin_made"), sem("hb_zero"), sem("dec_abs")
        hbs_made, decay_made, tap_sum = sem("hbs_made"), sem("decay_made"), sem("tap_sum")
        g1_out = [sem("g1_out0"), sem("g1_out1")]
        zpad_zero, z_used, s_made = sem("zpad_zero"), sem("z_used"), sem("s_made")
        sn_made = sem("sn_made")
        s1_out = [sem("s1_out0"), sem("s1_out1")]
        silu_c = sem("silu_c")
        mod_in = [sem("mod_in0"), sem("mod_in1")]
        mod_used = sem("mod_used")
        spec_in = [sem("spec_in0"), sem("spec_in1")]
        spec_mm, spec_g, spec_y, spec_inv, spec_ev = (sem(f"spec_{x}") for x in ("mm", "g", "y", "inv", "ev"))
        yb_in = [sem("yb_in0"), sem("yb_in1")]
        sp1_hi, sp1_lo = sem("y_hi"), sem("y_lo")
        xr_in = sem("xr_in")
        ff_hi, ff_lo, xdown = sem("ff_hi"), sem("ff_lo"), sem("xdown")
        x_spilled, blk2_in, cx_in = sem("x_spilled"), sem("blk2_in"), sem("cx_in")
        gate_abs, gate_ln, wup_made = sem("gate_abs"), sem("gate_ln"), sem("wup_made")
        dif_made, exp_made, qk_made = sem("dif_made"), sem("exp_made"), sem("qk_made")
        kdc_made, colexp = sem("kdc_made"), sem("colexp")
        state_made, sco_made = sem("state_made"), sem("sco_made")
        osq, osum, orsq = (sem(x) for x in ("osq", "osum", "orsq"))
        on_out = [sem("on_out0"), sem("on_out1")]
        on_in = [sem(f"on_in{k}") for k in range(4)]
        za_hi, za_lo, za_prod = sem("za_hi"), sem("za_lo"), sem("za_prod")
        ma_out = sem("ma_out")
        ma_in = [sem(f"ma_in{k}") for k in range(4)]
        pool_in, pool_pad, pd_made, pb_hi, pb_lo = (
            sem(x) for x in ("pool_in", "pool_pad", "pd_made", "pb_hi", "pb_lo"))
        mb_made, m_hi, m_lo = sem("mb_made"), sem("m_hi"), sem("m_lo")
        xr2_in = sem("xr2_in")
        out_st = [sem("out_st0"), sem("out_st1")]

        def vcol(name, j=0):
            return vec[:, ds(VEC[name] + j, 1)]

        def cc(name, rows=P):
            w = {"idft": 64, "tneg": 16, "tmask": 16}.get(name, 128)
            return cst[0:rows, CST[name]:CST[name] + w]

        ident, ones = cc("ident"), cc("ones")

        def chunk(t, c):
            return t[:, c * CH:(c + 1) * CH]

        HJ = 24
        HA = 21

        def aux_at(h, a):
            return h * HA + (A0["heads"] + a)

        def evac_at(h, u):
            return h * (HJ // 4) + (turn("heads", u) + 1)

        def heads_pe(pe, h, free, panel_mm):
            mm = nc.tensor.matmul

            def p(u):
                return ps[slot("heads", u)]

            def begin(u):
                free("heads", u, h, HJ)

            n0 = N0["heads"]
            pe.wait_ge(wup_made, h * 2 + 2)
            for u in range(2):
                begin(u)
                for c in range(2):
                    last = mm(p(u)[:, c * 512:(c + 1) * 512], wup_h[32 * u:32 * u + 16, :],
                              LRT[32 * u:32 * u + 16, c * 512:(c + 1) * 512], start=True, stop=True)
                last.then_inc(aux_done, 1)
            begin(2)
            for u in range(2):
                last = mm(p(2)[:, u * 512:u * 512 + TC], wup_h[32 * u:32 * u + 16, :],
                          LRT[32 * u:32 * u + 16, T:T + TC], start=True, stop=True)
            last.then_inc(aux_done, 1)
            pe.wait_ge(split_made, h * 4 + (n0 + 1))
            begin(3)
            panel_mm(p(3), n0 % 2, H, T, 8).then_inc(panel_done, 1)
            pe.wait_ge(split_made, h * 4 + (n0 + 2))
            begin(4)
            panel_mm(p(4), (n0 + 1) % 2, H, T, 8).then_inc(aux_done, 1)
            begin(5)
            panel_mm(p(5), (n0 + 1) % 2, HC, TC, 8).then_inc(panel_done, 1)

            def rotate(u, src, ready):
                begin(u)
                pe.wait_ge(*ready)
                for c in range(2):
                    last = mm(p(u)[:, c * 512:(c + 1) * 512], cc("perm"), src[:, c * 512:(c + 1) * 512],
                              start=True, stop=True)
                last.then_inc(aux_done, 1)

            def values(u, act, tiles, t0):
                begin(u)
                for t in range(tiles):
                    q = 0
                    for k in range(KT):
                        for a, w in ((0, whi), (1, whi), (0, wlo)):
                            last = mm(p(u)[:, t * DV:(t + 1) * DV], act[:, a, k, (t0 + t) * P:(t0 + t + 1) * P],
                                      w[:, :, k, :], start=(q == 0), stop=(q == 23))
                            q += 1
                return last

            rotate(6, QT, (evac[slot("heads", 3)], evac_at(h, 3)))
            pe.wait_ge(split_made, h * 4 + (n0 + 4))
            values(7, H, 4, 0).then_inc(aux_done, 1)
            rotate(8, KTt, (evac[slot("heads", 4)], evac_at(h, 4)))
            values(9, H, 4, 4).then_inc(aux_done, 1)
            values(10, HC, 2, 0).then_inc(panel_done, 2)
            begin(11)
            pe.wait_ge(kdc_made, h + 1)
            for dr in range(2):
                for c in range(NCC):
                    last = nc.tensor.transpose(p(11)[:, dr * 512 + c * CH:dr * 512 + (c + 1) * CH],
                                               chunk(KDC[:, dr, :], c), ident)
            last.then_inc(aux_done, 1)
            for dr in range(2):
                begin(12 + dr)
                pe.wait_ge(qk_made, h * 4 + 2 * dr + 2)
                for c in range(NCH):
                    last = nc.tensor.transpose(chunk(p(12 + dr), c), chunk(KD[dr], c), ident)
                last.then_inc(aux_done, 1)
            for dr in range(2):
                begin(14 + dr)
                for c in range(NCH):
                    last = mm(chunk(p(14 + dr), c), chunk(KD[dr], c), chunk(QD[dr], c), start=True, stop=True)
                last.then_inc(aux_done, 1)
            for u in (10, 11):
                pe.wait_ge(evac[slot("heads", u)], evac_at(h, u))
            begin(16)
            for dr in range(2):
                for c in range(NCC):
                    last = mm(p(16)[:, dr * 512 + c * DV:dr * 512 + (c + 1) * DV], KDTC[:, dr, c, :], VC[:, c, :],
                              start=True, stop=True)
            last.then_inc(aux_done, 1)
            pe.wait_ge(evac[slot("heads", 7)], evac_at(h, 7))
            for dr in range(2):
                pe.wait_ge(evac[slot("heads", 12 + dr)], evac_at(h, 12 + dr))
                for j in range(2):
                    u = 17 + 2 * dr + j
                    begin(u)
                    for c in range(4 * j, 4 * j + 4):
                        if c != (NCH - 1, 0)[dr]:
                            last = mm(p(u)[:, (c % 4) * DV:(c % 4 + 1) * DV], KDT[dr][:, c, :], V[:, c, :],
                                      start=True, stop=True)
                    last.then_inc(aux_done, 1)
            pe.wait_ge(sco_made, h + 1)
            pe.wait_ge(state_made, h + 1)
            for e in range(2):
                begin(21 + e)
                for c in range(NCH):
                    o = chunk(p(21 + e), c)
                    mm(o, V[:, c, e * P:(e + 1) * P], chunk(SCO[0], c), start=True, stop=False)
                    mm(o, SR[0][:, c, e * P:(e + 1) * P], chunk(QD[0], c), start=False, stop=False)
                    last = mm(o, SR[1][:, c, e * P:(e + 1) * P], chunk(QD[1], c), start=False, stop=True)
                last.then_inc(aux_done, 1)
            begin(23)
            pe.wait_ge(osum, h + 1)
            for c in range(2):
                last = mm(p(23)[:, c * 512:(c + 1) * 512], ones, TT[2][:, c * 512:(c + 1) * 512], start=True, stop=True)
            last.then_inc(aux_done, 1)


        def heads_act(act, h, ch):
            A_ = nc.scalar.activation
            inv = 1.0 / GATE_NORM

            def p(u):
                return ps[slot("heads", u)]

            def copied(u, out_, in_, **kw):
                A_(out_, in_, ACT.Copy, **kw).then_inc(evac[slot("heads", u)], 1)

            act.wait_ge(aux_done, aux_at(h, 0))
            steady(act)
            for r in (0, 32):
                A_(wup_h[r:r + 16, :], WUP[r:r + 16, ds(h * DK, DK)], ACT.Copy).then_inc(wup_made, 1)
            for u in range(2):
                act.wait_ge(on_out[u], h * 16 + 16)
            for u, t in ((0, TT[0]), (1, TT[2])):
                act.wait_ge(aux_done, aux_at(h, u + 1))
                steady(act)
                A_(t[:, :], p(u)[:, :], ACT.Abs, bias=vcol(("b_gf", "b_gb")[u], h)).then_inc(gate_abs, 1)
                act.wait_ge(gate_abs, h * 4 + u + 1)
                ch.link(A_(t[:, :], t[:, :], ACT.Exp, scale=-1.0))
                A_(t[:, :], t[:, :], ACT.Ln, bias=1.0).then_inc(gate_ln, 1)
            act.wait_ge(aux_done, aux_at(h, 3))
            steady(act)
            for u in range(2):
                A_(KDC[:, u, :], p(2)[:, u * 512:u * 512 + TC], ACT.Abs, bias=vcol(("b_gf", "b_gb")[u], h)
                   ).then_inc(gate_abs, 1)
            act.wait_ge(gate_abs, h * 4 + 4)
            ch.link(A_(KDC[:, :, :], KDC[:, :, :], ACT.Exp, scale=-1.0))
            A_(KDC[:, :, :], KDC[:, :, :], ACT.Ln, bias=1.0).then_inc(gate_ln, 1)
            act.wait_ge(panel_done, h * 4 + (N0["heads"] + 1))
            copied(3, QT[:, :], p(3)[:, :], scale=DK ** -0.5)
            act.wait_ge(aux_done, aux_at(h, 4))
            copied(4, KTt[:, :], p(4)[:, :])
            act.wait_ge(panel_done, h * 4 + (N0["heads"] + 2))
            copied(5, KC[:, :], p(5)[:, 0:TC])
            act.wait_ge(dif_made, h * 4 + 1)
            A_(TT[1][:, :], TT[0][:, :], ACT.Exp, scale=inv).then_inc(exp_made, 1)
            A_(TT[2][:, :], TT[0][:, :], ACT.Exp, scale=-inv).then_inc(exp_made, 1)
            act.wait_ge(exp_made, h * 5 + 2)
            act.wait_ge(dif_made, h * 4 + 2)
            A_(TT[0][:, :], TT[3][:, :], ACT.Exp, scale=inv).then_inc(exp_made, 1)
            act.wait_ge(exp_made, h * 5 + 3)
            A_(TT[3][:, :], TT[3][:, :], ACT.Exp, scale=-inv).then_inc(exp_made, 1)
            act.wait_ge(dif_made, h * 4 + 3)
            A_(KDC[:, :, :], KDC[:, :, :], ACT.Exp, scale=-inv).then_inc(exp_made, 1)
            act.wait_ge(dif_made, h * 4 + 4)
            for dr in range(2):
                mid, end = ((CH // 2 - 1, CH - 1), (CH // 2, 0))[dr]
                A_(col[dr][:, 10:18], BB[dr][:, mid::CH], ACT.Exp, scale=inv).then_inc(colexp, 1)
                A_(col[dr][:, 20:28], BB[dr][:, end::CH], ACT.Exp, scale=inv).then_inc(colexp, 1)
                A_(col[dr][:, 28:30], BBC[:, dr, end::CH], ACT.Exp, scale=inv).then_inc(colexp, 1)
                A_(col[dr][:, 30:40], dcol[dr][:, :], ACT.Exp, scale=inv).then_inc(colexp, 1)
            act.wait_ge(aux_done, aux_at(h, 6))
            copied(7, V[:, 0:4, :].rearrange("p c v -> p (c v)"), p(7)[:, :])
            act.wait_ge(aux_done, aux_at(h, 8))
            copied(9, V[:, 4:8, :].rearrange("p c v -> p (c v)"), p(9)[:, :])
            act.wait_ge(panel_done, h * 4 + (N0["heads"] + 4))
            copied(10, VC[:, :, :].rearrange("p c v -> p (c v)"), p(10)[:, 0:2 * DV])
            act.wait_ge(aux_done, aux_at(h, 9))
            copied(11, KDTC[:, :, :, :].rearrange("p a c k -> p a (c k)"),
                   p(11)[:, :].rearrange("p (a b) -> p a b", a=2)[:, :, 0:TC])
            for dr in range(2):
                act.wait_ge(aux_done, aux_at(h, 10 + dr))
                copied(12 + dr, KDT[dr][:, :, :].rearrange("p c k -> p (c k)"), p(12 + dr)[:, :])
            for e in range(2):
                act.wait_ge(aux_done, aux_at(h, 19 + e))
                if e == 0:
                    act.wait_ge(state_made, h + 1)
                A_(TT[2 + e][:, :], p(21 + e)[:, :], ACT.Square).then_inc(osq, 1)
            act.wait_ge(evac[slot("heads", 23)], evac_at(h, 23))
            ch.link(A_(TT[2][:, :], TT[3][:, :], ACT.Ln))
            ch.link(A_(TT[2][:, :], TT[2][:, :], ACT.Exp, scale=-0.5))
            A_(TT[1][:, :], TT[2][:, :], ACT.Square).then_inc(orsq, 1)
            for e in range(2):
                act.wait_ge(evac[slot("heads", 21 + e)], evac_at(h, 21 + e))
                act.dma_start(ond[ds(h * 2 + e, 1), :, :].rearrange("k p t -> (k p) t"), TT[e][:, :]
                              ).then_inc(on_out[e], 16)

        HEAD_STEPS = 87
        HEAD_ACT_STEPS = 5

        def heads_dve(dve, h, ch):
            V_ = nc.vector

            def p(u):
                return ps[slot("heads", u)]

            def ev(u):
                return evac[slot("heads", u)]

            def by_chunk(t):
                return t.rearrange("p (c j) -> p c j", j=CH)

            def at_col(t, j):
                v = by_chunk(t)
                return v[:, :, j:j + 1].to_broadcast([P, v.shape[1], CH])

            dve.wait_ge(gate_abs, h * 4 + 1)
            V_.tensor_scalar(TT[1][:, :], p(0)[:, :], vcol("b_gf", h), 0.0, ALU.add, ALU.min).then_inc(ev(0), 1)
            dve.wait_ge(ev(0), evac_at(h, 0))
            dve.wait_ge(gate_ln, h * 3 + 1)
            ch.link(V_.tensor_tensor(TT[1][:, :], TT[1][:, :], TT[0][:, :], ALU.subtract))
            for c in range(NCH):
                ch.do(V_.tensor_tensor_scan(chunk(BB[0], c), ones, chunk(TT[1], c), 0.0, ALU.mult, ALU.add))
            dve.wait_ge(gate_abs, h * 4 + 2)
            V_.tensor_scalar(TT[3][:, :], p(1)[:, :], vcol("b_gb", h), 0.0, ALU.add, ALU.min).then_inc(ev(1), 1)
            dve.wait_ge(ev(1), evac_at(h, 1))
            dve.wait_ge(gate_ln, h * 3 + 2)
            ch.link(V_.tensor_tensor(TT[3][:, :], TT[3][:, :], TT[2][:, :], ALU.subtract))
            for c in range(NCH):
                ch.do(V_.tensor_tensor_scan(chunk(TT[2], c), ones, chunk(TT[3], c), 0.0, ALU.mult, ALU.add))
            ch.wait()
            ch.link(V_.tensor_tensor(TT[3][:, :], TT[3][:, :], TT[2][:, :], ALU.subtract))
            ch.link(V_.tensor_tensor(by_chunk(BB[1][:, :]), by_chunk(TT[3][:, :]), at_col(TT[2][:, :], CH - 1), ALU.add))
            dve.wait_ge(gate_abs, h * 4 + 4)
            for u in range(2):
                i_ = V_.tensor_scalar(BBC[:, u, :], p(2)[:, u * 512:u * 512 + TC], vcol(("b_gf", "b_gb")[u], h), 0.0,
                                      ALU.add, ALU.min)
                if u:
                    i_.then_inc(ev(2), 1)
            dve.wait_ge(ev(2), evac_at(h, 2))
            dve.wait_ge(gate_ln, h * 3 + 3)
            ch.link(V_.tensor_tensor(BBC[:, :, :], BBC[:, :, :], KDC[:, :, :], ALU.subtract))
            for u in range(2):
                for c in range(NCC):
                    ch.do(V_.tensor_tensor_scan(chunk(KDC[:, u, :], c), ones, chunk(BBC[:, u, :], c), 0.0,
                                                ALU.mult, ALU.add))
            ch.wait()
            ch.do(V_.tensor_copy(BBC[:, 0, :], KDC[:, 0, :]))
            ch.link(V_.tensor_tensor(BBC[:, 1, :], BBC[:, 1, :], KDC[:, 1, :], ALU.subtract))
            ch.link(V_.tensor_tensor(by_chunk(BBC[:, 1, :]), by_chunk(BBC[:, 1, :]), at_col(KDC[:, 1, :], CH - 1), ALU.add))
            mids = (CH // 2 - 1, CH // 2)
            ends = (CH - 1, 0)
            for dr, t in ((0, TT[0]), (1, TT[3])):
                ch.link(V_.tensor_tensor(by_chunk(t[:, :]), by_chunk(BB[dr][:, :]), at_col(BB[dr][:, :], mids[dr]),
                                         ALU.subtract))
                V_.tensor_scalar(t[:, :], t[:, :], CLAMP, -CLAMP, ALU.min, ALU.max).then_inc(dif_made, 1)
            for dr in range(2):
                ch.do(V_.tensor_tensor(by_chunk(KDC[:, dr, :]), by_chunk(BBC[:, dr, :]), at_col(BBC[:, dr, :], mids[dr]),
                                       ALU.subtract))
            ch.wait()
            V_.tensor_scalar(KDC[:, :, :], KDC[:, :, :], CLAMP, -CLAMP, ALU.min, ALU.max).then_inc(dif_made, 1)
            for dr in range(2):
                ch.do(V_.tensor_tensor(dcol[dr][:, 0:8], BB[dr][:, ends[dr]::CH], BB[dr][:, mids[dr]::CH], ALU.subtract))
                i_ = V_.tensor_tensor(dcol[dr][:, 8:10], BBC[:, dr, ends[dr]::CH], BBC[:, dr, mids[dr]::CH], ALU.subtract)
                if dr == 0:
                    ch.do(i_)
                else:
                    i_.then_inc(dif_made, 1)
            def rotate(u, t, tmp, a):
                dve.wait_ge(aux_done, aux_at(h, a))
                V_.tensor_tensor(tmp[:, :], p(u)[:, :], SIN[:, :], ALU.mult).then_inc(ev(u), 1)
                ch.link(V_.tensor_tensor(t[:, :], t[:, :], COS[:, :], ALU.mult))
                dve.wait_ge(ev(u), evac_at(h, u))
                ch.link(V_.tensor_tensor(t[:, :], t[:, :], tmp[:, :], ALU.add))

            dve.wait_ge(exp_made, h * 5 + 5)
            dve.wait_ge(ev(5), evac_at(h, 5))
            ch.link(V_.tensor_tensor(KDC[:, 0, :], KDC[:, 0, :], KC[:, :], ALU.mult))
            V_.tensor_tensor(KDC[:, 1, :], KDC[:, 1, :], KC[:, :], ALU.mult).then_inc(kdc_made, 1)
            rotate(6, QT, ROT[0], 5)
            V_.tensor_tensor(QD[0][:, :], QT[:, :], TT[1][:, :], ALU.mult).then_inc(qk_made, 1)
            rotate(8, KTt, ROT[1], 7)
            V_.tensor_tensor(KD[0][:, :], KTt[:, :], TT[2][:, :], ALU.mult).then_inc(qk_made, 1)
            dve.wait_ge(qk_made, h * 4 + 2)
            V_.tensor_tensor(QD[1][:, :], QT[:, :], TT[0][:, :], ALU.mult).then_inc(qk_made, 1)
            V_.tensor_tensor(KD[1][:, :], KTt[:, :], TT[3][:, :], ALU.mult).then_inc(qk_made, 1)
            masks = [cc(m).unsqueeze(1).to_broadcast([P, NCH, CH]) for m in ("mask_f", "mask_b")]
            dve.wait_ge(qk_made, h * 4 + 4)
            for dr in range(2):
                dve.wait_ge(aux_done, aux_at(h, 12 + dr))
                V_.tensor_tensor(by_chunk(SCO[dr][:, :]), by_chunk(p(14 + dr)[:, :]), masks[dr], ALU.mult
                                 ).then_inc(ev(14 + dr), 1)
                dve.wait_ge(ev(14 + dr), evac_at(h, 14 + dr))
            V_.tensor_tensor(SCO[0][:, :], SCO[0][:, :], SCO[1][:, :], ALU.add).then_inc(sco_made, 1)
            dve.wait_ge(colexp, h * 8 + 8)
            dve.wait_ge(aux_done, aux_at(h, 14))
            for dr in range(2):
                S_, cl, tmp = SS[dr], col[dr], TT[2 + dr][:, 0:DV]
                for q, c in enumerate(((0, 1), (1, 0))[dr]):
                    U = p(16)[:, dr * 512 + c * DV:dr * 512 + (c + 1) * DV]
                    if q == 0:
                        ch.link(V_.tensor_scalar(S_[:, :], U, cl[:, 38 + c:39 + c], None, ALU.mult))
                    else:
                        i_ = V_.tensor_scalar(tmp, U, cl[:, 38 + c:39 + c], None, ALU.mult)
                        if dr:
                            i_.then_inc(ev(16), 1)
                            dve.wait_ge(ev(16), evac_at(h, 16))
                        else:
                            ch.link(i_)
                        ch.link(V_.scalar_tensor_tensor(out=S_[:, :], in0=S_[:, :], scalar=cl[:, 28 + c:29 + c], in1=tmp,
                                                        op0=ALU.mult, op1=ALU.add))
            dve.wait_ge(aux_done, aux_at(h, 18))
            for q in range(NCH):
                for dr in range(2):
                    c = (q, NCH - 1 - q)[dr]
                    S_, cl, tmp = SS[dr], col[dr], TT[2 + dr][:, 0:DV]
                    i_ = V_.tensor_scalar(SR[dr][:, c, :], S_[:, :], cl[:, 10 + c:11 + c], None, ALU.mult)
                    if q == NCH - 1 and dr == 1:
                        i_.then_inc(state_made, 1)
                    else:
                        ch.link(i_)
                    if q == NCH - 1:
                        continue
                    u = 17 + 2 * dr + c // 4
                    i_ = V_.tensor_scalar(tmp, p(u)[:, (c % 4) * DV:(c % 4 + 1) * DV], cl[:, 30 + c:31 + c], None, ALU.mult)
                    if (dr, c) in ((0, 3), (0, 6), (1, 4), (1, 1)):
                        i_.then_inc(ev(u), 1)
                        dve.wait_ge(ev(u), evac_at(h, u))
                    else:
                        ch.link(i_)
                    ch.link(V_.scalar_tensor_tensor(out=S_[:, :], in0=S_[:, :], scalar=cl[:, 20 + c:21 + c], in1=tmp,
                                                    op0=ALU.mult, op1=ALU.add))
            dve.wait_ge(osq, h * 2 + 2)
            V_.tensor_tensor(TT[2][:, :], TT[2][:, :], TT[3][:, :], ALU.add).then_inc(osum, 1)
            dve.wait_ge(aux_done, aux_at(h, 21))
            V_.tensor_scalar(TT[3][:, :], p(23)[:, :], 1.0 / DV, EPS, ALU.mult, ALU.add).then_inc(ev(23), 1)
            dve.wait_ge(orsq, h + 1)
            ch.link(V_.tensor_tensor(TT[1][:, :], TT[1][:, :], TT[3][:, :], ALU.mult))
            ch.link(V_.tensor_scalar(TT[1][:, :], TT[1][:, :], -0.5, 1.5, ALU.mult, ALU.add))
            ch.link(V_.tensor_tensor(TT[2][:, :], TT[2][:, :], TT[1][:, :], ALU.mult))
            for e in range(2):
                V_.scalar_tensor_tensor(out=TT[e][:, :], in0=p(21 + e)[:, :], scalar=vec[:, VEC["gla_g"] + e:VEC["gla_g"] + e + 1],
                                        in1=TT[2][:, :], op0=ALU.mult, op1=ALU.mult).then_inc(ev(21 + e), 1)
                dve.wait_ge(ev(21 + e), evac_at(h, 21 + e))

        block = ctx.enter_context(nc.Block())

        @block.sync
        def _(sp):
            sp.dma_start(vec[:, :], d["vec"]).then_inc(const_in, 16)
            sp.dma_start(cst[:, :], d["cst"]).then_inc(const_in, 16)
            for t, n in ((feat, "feat"), (fw1, "fw1"), (fw2, "fw2"), (fw3, "fw3"), (wtap, "wtap"), (dec, "dec")):
                sp.dma_start(t[:, :], d[n]).then_inc(filt_in, 16)
            xv = d["xT"].rearrange("(k p) t -> p k t", p=P)
            sp.dma_start(X[:, :, :], xv).then_inc(x_in, 16)

            def panel(n, s):
                sp.dma_start(wraw[:, s, :, :], d["panels"][ds(n, 1), :, :].rearrange("a p (k m) -> (a p) k m", k=8)
                             ).then_inc(raw_in[s], 16)

            def panels(lo, hi):
                assert lo >= 2 and (hi - lo) % 2 == 0
                with sp.Fori(0, (hi - lo) // 2) as i:
                    for u in range(2):
                        n = lo + u + i * 2
                        sp.wait_ge(split_made, n - 1)
                        panel(n, (lo + u) % 2)

            panel(0, 0)
            panel(1, 1)
            panels(2, 4)
            with sp.Fori(0, N2 // 2) as i:
                for u in range(2):
                    s = slot("taps", 2 + u)
                    sp.wait_ge(evac[s], turn("taps", 2 + u, i, 4) + 1)
                    sp.dma_start(g1[:, ds(i * 2 + u, 1), :], gsp[u][:, :].unsqueeze(1)).then_inc(g1_out[u], 16)
            panels(4, 24)
            with sp.Fori(0, N2 // 2) as i:
                for u in range(2):
                    s = slot("sfwd", 2 + u)
                    sp.wait_ge(evac[s], turn("sfwd", 2 + u, i, 4) + 1)
                    sp.dma_start(s1[:, ds(i * 2 + u, 1), :], sa[u][:, :].unsqueeze(1)).then_inc(s1_out[u], 16)
            def modp(n, s):
                sp.dma_start(mraw[:, s, :, :], d["modp"][ds(n, 1), :, :].rearrange("a p (k m) -> (a p) k m", k=8)
                             ).then_inc(mod_in[s], 16)
            modp(0, 0)
            modp(1, 1)
            with sp.Fori(0, 11) as i:
                for u in range(2):
                    sp.wait_ge(mod_used, i * 2 + u + 1)
                    modp(i * 2 + u + 2, u)
            for u in range(2):
                sp.wait_ge(g1_out[u], 16 * (N2 // 2 + 1))
                sp.wait_ge(s1_out[u], 16 * (N2 // 2 + 1))
            sp.wait_ge(ended["pe"], 4)
            sp.wait_ge(ended["act"], 4)
            g1r = g1.rearrange("p n t -> (p n) t")
            s1r = s1.rearrange("p n t -> (p n) t")

            def spec_load(g):
                u = g % 2
                if g >= 2:
                    sp.wait_ge(spec_inv, 2 * (g - 1))
                for t, src in ((kf[u][:, :, :].rearrange("p a m -> p (a m)"), d["kfft"][g, :, :]),
                               (bg[u][:, :], g1r[g * P:(g + 1) * P, :]), (bs[u][:, :], s1r[g * P:(g + 1) * P, :])):
                    sp.dma_start(t, src).then_inc(spec_in[u], 16)

            spec_load(0)
            spec_load(1)
            for g in range(GROUPS):
                for c in range(2):
                    sp.wait_ge(spec_ev, 2 * g + c + 1)
                    sp.dma_start(YB[8 * g:8 * g + 8, :, 512 * c:512 * c + 512], yi[c][:, :]).then_inc(yb_in[c], 16)
                if g + 2 < GROUPS:
                    spec_load(g + 2)
            sp.wait_ge(ended["pe"], 5)
            sp.wait_ge(ended["act"], 5)
            sp.wait_ge(ended["dve"], 5)
            sp.dma_start(X[:, :, :], xv).then_inc(xr_in, 16)
            panels(24, N0["lr"])
            sp.wait_ge(nf1.h, KT)
            xsv = xs.rearrange("(k p) t -> p k t", p=P)
            sp.dma_start(xsv, X[:, :, :]).then_inc(x_spilled, 16)
            sp.wait_ge(ended["pe"], 8)
            sp.dma_start(CX[:, :, :], d["ctxT"].rearrange("(k p) t -> p k t", p=P)).then_inc(cx_in, 16)
            for t, n in ((COS, "cos"), (SIN, "sin"), (WUP, "wup")):
                sp.dma_start(t[:, :], d[n]).then_inc(blk2_in, 16)
            sp.wait_ge(split_made, N0["lr"] - 1)
            panel(N0["lr"], N0["lr"] % 2)
            panels(N0["heads"], NPANELS - 8)
            sp.wait_ge(ended["pe"], 16)
            sp.dma_start(XN[:, :, :], xsv).then_inc(xr2_in, 16)
            panels(NPANELS - 8, NPANELS)

        @block.gpsimd
        def _(pool):
            for s in range(2):
                pool.wait_ge(raw_in[s], 16)
                nc.gpsimd.tensor_copy(whi[:, s, :, :], wraw[:, s, :, :]).then_inc(hi_made, 1)
                pool.wait_ge(hi_made, s + 1)
                nc.gpsimd.tensor_tensor(wlo[:, s, :, :], wraw[:, s, :, :], whi[:, s, :, :].bitcast(F32), ALU.subtract
                                        ).then_inc(split_made, 1)

            def rest(pairs_lo, pairs_hi):
                with pool.Fori(pairs_lo, pairs_hi) as i:
                    for s in range(2):
                        pool.wait_ge(raw_in[s], i * 16 + 16)
                        pool.wait_ge(panel_done, i * 2 + s - 1)
                        steady(pool)
                        nc.gpsimd.tensor_copy(whi[:, s, :, :], wraw[:, s, :, :]).then_inc(hi_made, 1)
                        pool.wait_ge(hi_made, i * 2 + s + 1)
                        nc.gpsimd.tensor_tensor(wlo[:, s, :, :], wraw[:, s, :, :], whi[:, s, :, :].bitcast(F32),
                                                ALU.subtract).then_inc(split_made, 1)

            rest(1, NPANELS // 2)
            if NPANELS % 2:
                n = NPANELS - 1
                pool.wait_ge(raw_in[0], (n // 2 + 1) * 16)
                pool.wait_ge(panel_done, n - 1)
                nc.gpsimd.tensor_copy(whi[:, 0, :, :], wraw[:, 0, :, :]).then_inc(hi_made, 1)
                pool.wait_ge(hi_made, n + 1)
                nc.gpsimd.tensor_tensor(wlo[:, 0, :, :], wraw[:, 0, :, :], whi[:, 0, :, :].bitcast(F32), ALU.subtract
                                        ).then_inc(split_made, 1)

        @block.tensor
        def _(pe):
            mm = nc.tensor.matmul

            def free(phase, u, i=0, per=0):
                q = turn(phase, u, i, per)
                if not (isinstance(q, int) and q == 0):
                    pe.wait_ge(evac[slot(phase, u)], q)

            def panel_mm(p, ws, act, width, nk, ready=None):
                last = None
                step = min(512, width)
                for k in range(nk):
                    if ready is not None:
                        pe.wait_ge(ready[0], ready[1] + k + 1)
                    for w, a in ((whi, 0), (whi, 1), (wlo, 0)):
                        for c in range(width // step):
                            last = mm(p[:, c * step:(c + 1) * step], w[:, ws, k, :],
                                      act[:, a, k, c * step:(c + 1) * step],
                                      start=(k == 0 and w is whi and a == 0), stop=(k == nk - 1 and w is wlo))
                return last

            def panel_jobs(phase, trips, act, nk=8, ready=None, per=4):
                n0 = N0[phase]
                with pe.Fori(0, trips) as i:
                    for u in range(per):
                        pe.wait_ge(split_made, i * per + (n0 + u + 1))
                        free(phase, u, i, per)
                        a = act[u] if isinstance(act, list) else act
                        r = ready[u] if isinstance(ready, list) else ready
                        panel_mm(ps[slot(phase, u)], (n0 + u) % 2, a, T, nk, r).then_inc(panel_done, 1)

            def sum_partitions(phase, u, src, ready, width=T, i=0, per=0):
                free(phase, u, i, per)
                pe.wait_ge(*ready)
                step = min(512, width)
                for c in range(width // step):
                    last = mm(ps[slot(phase, u)][:, c * step:(c + 1) * step], ones, src[:, c * step:(c + 1) * step],
                              start=True, stop=True)
                last.then_inc(aux_done, 1)

            pe.wait_ge(const_in, 32)
            sum_partitions("norm1", 0, TT[2], (n1.acc, 8))
            pe.wait_ge(filt_in, 96)
            for l, (w, src) in enumerate(((fw1, feat), (fw2, fh), (fw3, fh))):
                if l:
                    pe.wait_ge(sin_made, l)
                free("mlp", l)
                for c in range(2):
                    last = mm(ps[slot("mlp", l)][:, c * 512:(c + 1) * 512], w[:, :], src[:, c * 512:(c + 1) * 512],
                              start=True, stop=True)
                last.then_inc(aux_done, 1)
            with pe.Fori(0, N2 // 2) as i:
                for u in range(2):
                    free("taps", u, i, 4)
                    pe.wait_ge(hbs_made, i * 2 + u + 1)
                    for c in range(2):
                        last = mm(ps[slot("taps", u)][:, c * 512:(c + 1) * 512], hbs[u][:, :],
                                  wtap[:, c * 512:(c + 1) * 512], start=True, stop=True)
                    last.then_inc(aux_done, 1)
                for u in range(2):
                    free("taps", 2 + u, i, 4)
                    pe.wait_ge(evac[slot("taps", u)], turn("taps", u, i, 4) + 1)
                    for c in range(2):
                        last = mm(ps[slot("taps", 2 + u)][:, c * 512:(c + 1) * 512], cc("dft_g"),
                                  tap[u][:, c * 512:(c + 1) * 512], start=True, stop=True)
                    last.then_inc(aux_done, 1)
            free("tapnorm", 0)
            pe.wait_ge(tap_sum, N2)
            for e in range(KT):
                last = mm(ps[slot("tapnorm", 0)][:, e:e + 1], gacc[:, e * P:(e + 1) * P], ones[:, 0:1],
                          start=True, stop=True)
            last.then_inc(aux_done, 1)
            barrier(pe, "pe", 1)
            panel_jobs("zin", 6, H, ready=(n1.lo, 0))
            barrier(pe, "pe", 2)
            with pe.Fori(0, N2 // 2) as i:
                for u in range(2):
                    free("sfwd", u, i, 4)
                    pe.wait_ge(sn_made, i * 2 + u + 1)
                    steady(pe)
                    for e in range(KT):
                        last = nc.tensor.transpose(ps[slot("sfwd", u)][0:HALF, e * P:(e + 1) * P], sn[u][:, e, :], ident)
                    last.then_inc(aux_done, 1)
                for u in range(2):
                    free("sfwd", 2 + u, i, 4)
                    pe.wait_ge(evac[slot("sfwd", u)], turn("sfwd", u, i, 4) + 1)
                    for c in range(2):
                        last = mm(ps[slot("sfwd", 2 + u)][:, c * 512:(c + 1) * 512], cc("dft_s", HALF),
                                  st_[u][:, c * 512:(c + 1) * 512], start=True, stop=True)
                    last.then_inc(aux_done, 1)
            barrier(pe, "pe", 3)
            free("mod", 0)
            pe.wait_ge(silu_c, 1)
            with pe.Fori(0, 12) as i:
                for u in range(2):
                    pe.wait_ge(mod_in[u], i * 16 + 16)
                    for k in range(KT):
                        last = mm(ps[slot("mod", 0)][:, ds(i * 4 + 2 * u, 2)], mraw[:, u, k, :], sc[:, :, k],
                                  start=(k == 0), stop=(k == KT - 1))
                    last.then_inc(mod_used, 1)
            barrier(pe, "pe", 4)
            def bank(c, b):
                s = 2 * c + b // 2
                return ps[s][:, (b % 2) * 512:(b % 2) * 512 + 512]

            def inverse(n):
                g, c = n // 2, n % 2
                pe.wait_ge(spec_y, n + 1)
                mm(bank(c, 0), kf[g % 2][:, 4, :], yy[c][:, :], start=True, stop=True).then_inc(spec_inv, 1)

            for n in range(2 * GROUPS):
                g, c = n // 2, n % 2
                u = g % 2
                if c == 0:
                    pe.wait_ge(spec_in[u], 48 * (g // 2 + 1))
                for m, b, src in ((2, 2, bg), (3, 3, bg), (1, 1, bs), (0, 0, bs)):
                    if b == 0 and n >= 2:
                        pe.wait_ge(spec_ev, n - 1)
                    last = mm(bank(c, b), kf[u][:, m, :], src[u][:, c * 512:(c + 1) * 512], start=True, stop=True)
                last.then_inc(spec_mm, 1)
                if n:
                    inverse(n - 1)
            inverse(2 * GROUPS - 1)
            barrier(pe, "pe", 5)
            for u in range(2):
                pe.wait_ge(yb_in[u], 16 * GROUPS)
            for e in range(KT):
                free("inv", e)
                for m in range(N2):
                    last = mm(ps[slot("inv", e)][:, m * HALF:(m + 1) * HALF], YB[:, m, e * P:(e + 1) * P], cc("idft"),
                              start=True, stop=True)
                last.then_inc(aux_done, 1)
            barrier(pe, "pe", 6)
            panel_jobs("wout", 2, H, ready=(sp1_lo, 0))
            barrier(pe, "pe", 7)
            sum_partitions("norm2", 0, TT[2], (n2.acc, 8))
            f0 = 0
            for p, nf in enumerate(FPARTS):
                panel_jobs(f"up{p}", nf // 2, H, ready=(n2.lo, 0))
                panel_jobs(f"down{p}", 2, A, nk=nf, ready=(ff_lo, f0))
                f0 += nf
            sum_partitions("normf", 0, TT[2], (nf1.acc, 8))
            barrier(pe, "pe", 8)
            sum_partitions("norm3", 0, TT[2], (n3.acc, 8))
            barrier(pe, "pe", 9)
            sum_partitions("normc", 0, TT[2], (ncx.acc, 8), TC)
            barrier(pe, "pe", 10)
            pe.wait_ge(split_made, N0["lr"] + 1)
            free("lr", 0)
            free("lr", 1)
            ws = N0["lr"] % 2
            panel_mm(ps[slot("lr", 0)], ws, H, T, 8).then_inc(aux_done, 1)
            panel_mm(ps[slot("lr", 1)], ws, HC, TC, 8).then_inc(panel_done, 1)
            barrier(pe, "pe", 11)
            with pe.Fori(0, HEADS) as h:
                heads_pe(pe, h, free, panel_mm)
            barrier(pe, "pe", 12)
            panel_jobs("za", 2, H)
            barrier(pe, "pe", 13)
            panel_jobs("mixa", 4, [H, A, H, A])
            barrier(pe, "pe", 14)
            for g in range(4):
                for u in range(4):
                    n = N0["pool"] + 4 * g + u
                    pe.wait_ge(split_made, n + 1)
                    free("pool", 6 * g + u)
                    panel_mm(ps[slot("pool", 6 * g + u)], n % 2, H, T, 8).then_inc(panel_done, 1)
                pe.wait_ge(pool_in, 32 * (g + 1))
                for m in range(2):
                    free("pool", 6 * g + 4 + m)
                    for k in range(2):
                        pe.wait_ge(pd_made, 2 * g + k + 1)
                        for c in range(2):
                            last = mm(ps[slot("pool", 6 * g + 4 + m)][:, c * 512:(c + 1) * 512],
                                      wpl[:, k, m * P:(m + 1) * P], pd[k][:, c * 512:(c + 1) * 512],
                                      start=(k == 0), stop=(k == 1))
                    last.then_inc(aux_done, 1)
            barrier(pe, "pe", 15)
            panel_jobs("mixb", 4, [H, A, H, A])
            barrier(pe, "pe", 16)
            panel_jobs("wout2", 2, H, ready=(m_lo, 0))
            barrier(pe, "pe", 17)
            sum_partitions("norm4", 0, TT[2], (n4.acc, 8))

        @block.scalar
        def _(act):
            A_ = nc.scalar.activation
            ch = Steps(act, act_chain)

            def norm_act(n, src, width=T, shift=None, hi=None):
                for k in range(KT):
                    if k >= 2:
                        act.wait_ge(n.acc, k - 1)
                    A_(TT[k % 2][:, 0:width], src[:, k, :], ACT.Square).then_inc(n.sq, 1)
                act.wait_ge(n.var, 1)
                ch.link(A_(TT[2][:, 0:width], TT[3][:, 0:width], ACT.Ln))
                ch.link(A_(TT[2][:, 0:width], TT[2][:, 0:width], ACT.Exp, scale=-0.5))
                A_(TT[1][:, 0:width], TT[2][:, 0:width], ACT.Square).then_inc(n.r0, 1)
                if hi is None:
                    return
                for k in range(KT):
                    act.wait_ge(n.h, k + 1)
                    if shift is None:
                        A_(hi[:, 0, k, :], TT[k % 2][:, 0:width], ACT.Copy).then_inc(n.hi, 1)
                    else:
                        A_(hi[:, 0, k, :], TT[k % 2][:, 0:width], ACT.Identity, bias=shift(k)).then_inc(n.hi, 1)

            act.wait_ge(const_in, 32)
            act.wait_ge(x_in, 16)
            norm_act(n1, X, hi=H)
            act.wait_ge(filt_in, 96)
            A_(dec[:, :], dec[:, :], ACT.Abs).then_inc(dec_abs, 1)
            for l in range(2):
                act.wait_ge(arg_made, l + 1)
                if l:
                    act.wait_ge(aux_done, A0["mlp"] + 2)
                A_(fh[:, :], fu[:, :], ACT.Sin).then_inc(sin_made, 1)
            act.wait_ge(arg_made, 3)
            act.wait_ge(hb_zero, 1)
            for r, half in ((0, 0), (HALF, HALF)):
                ch.do(A_(hb[r:r + HALF, :, half:half + HALF],
                         fu[r:r + HALF, :].rearrange("p (a b) -> p a b", b=HALF), ACT.Sin))
            ch.wait()
            act.wait_ge(dec_abs, 1)

            def decays(n2, u):
                A_(hbs[u][:, :], hb[:, ds(n2, 1), :].rearrange("p a b -> p (a b)"), ACT.Copy).then_inc(hbs_made, 1)
                A_(dk_[u][:, :], dec[:, :], ACT.Exp, scale=cst[:, ds(n2 + CST["tneg"], 1)],
                   bias=cst[:, ds(n2 + CST["tmask"], 1)]).then_inc(decay_made, 1)

            for u in range(2):
                act.sem_inc(g1_out[u], 16)
                act.sem_inc(s1_out[u], 16)
                decays(u, u)

            def tap_spectra(i):
                for u in range(2):
                    act.wait_ge(aux_done, i * 4 + (A0["taps"] + 3 + u))
                    act.wait_ge(g1_out[u], i * 16 + 16)
                    A_(gsp[u][:, :], ps[slot("taps", 2 + u)][:, :], ACT.Copy).then_inc(evac[slot("taps", 2 + u)], 1)

            with act.Fori(0, N2 // 2 - 1) as i:
                for u in range(2):
                    act.wait_ge(evac[slot("taps", u)], turn("taps", u, i, 4) + 1)
                    steady(act)
                    decays(i * 2 + u + 2, u)
                tap_spectra(i)
            tap_spectra(N2 // 2 - 1)
            for u in range(2):
                act.wait_ge(g1_out[u], 16 * (N2 // 2 + 1))
            barrier(act, "act", 1)
            act.wait_ge(zpad_zero, 1)

            def z_tile(n, u, f):
                act.wait_ge(panel_done, n + 1)
                act.wait_ge(z_used, n + 1)
                steady(act)
                A_(zp[u % 2][:, 1:T + 1], ps[slot("zin", u)][:, :], ACT.Identity, bias=vcol("b_in", f)
                   ).then_inc(evac[slot("zin", u)], 1)

            with act.Fori(0, 2) as i:
                for u in range(4):
                    z_tile(i * 4 + u, u, i * 4 + u)
            with act.Fori(0, 4) as i:
                for u in range(4):
                    z_tile(i * 4 + 8 + u, u, i * 2 + (8 + 8 * (u % 2) + u // 2))
            barrier(act, "act", 2)
            Sv = S[:, :, :].rearrange("p k (a b) -> p k a b", b=N2)

            def gather(n, u):
                A_(sn[u][:, :, :], Sv[:, :, :, ds(n, 1)].rearrange("p k a b -> p k (a b)"), ACT.Copy
                   ).then_inc(sn_made, 1)

            def transposed(i):
                for u in range(2):
                    act.wait_ge(aux_done, i * 4 + (A0["sfwd"] + 1 + u))
                    A_(st_[u][:, :], ps[slot("sfwd", u)][0:HALF, :], ACT.Copy).then_inc(evac[slot("sfwd", u)], 1)

            gather(0, 0)
            gather(1, 1)
            with act.Fori(0, N2 // 2 - 1) as i:
                transposed(i)
                for u in range(2):
                    gather(i * 2 + u + 2, u)
            transposed(N2 // 2 - 1)
            A_(sc[:, :, :].rearrange("p w k -> p (w k)"), vec[:, VEC["c"]:VEC["c"] + 16], ACT.Silu).then_inc(silu_c, 1)
            barrier(act, "act", 3)
            barrier(act, "act", 4)

            def spec_inverse(n):
                c = n % 2
                act.wait_ge(spec_inv, n + 1)
                if n >= 2:
                    act.wait_ge(yb_in[c], 16 * (n // 2))
                A_(yi[c][:, :], ps[2 * c][:, 0:512], ACT.Copy).then_inc(spec_ev, 1)

            for n in range(2 * GROUPS):
                c = n % 2
                act.wait_ge(spec_mm, n + 1)
                if n >= 2:
                    act.wait_ge(spec_y, n - 1)
                A_(ga[c][:, :], ps[2 * c + 1][:, 0:512], ACT.Copy).then_inc(spec_g, 1)
                A_(gb[c][:, :], ps[2 * c + 1][:, 512:1024], ACT.Copy).then_inc(spec_g, 1)
                if n:
                    spec_inverse(n - 1)
            spec_inverse(2 * GROUPS - 1)
            barrier(act, "act", 5)
            barrier(act, "act", 6)

            def split_act(src, dst, hi):
                for k in range(KT):
                    A_(dst[:, 0, k, :], src[:, k, :], ACT.Copy).then_inc(hi, 1)

            split_act(G0, H, sp1_hi)
            barrier(act, "act", 7)
            norm_act(n2, X, hi=H)
            f0 = 0
            for p, nf in enumerate(FPARTS):
                ph = f"up{p}"
                with act.Fori(0, nf // 2) as i:
                    for u in range(2):
                        g, v = slot(ph, 2 * u), slot(ph, 2 * u + 1)
                        act.wait_ge(panel_done, i * 4 + (N0[ph] + 2 * u + 1))
                        A_(TT[0][:, :], ps[g][:, :], ACT.Silu).then_inc(evac[g], 1)
                        act.wait_ge(evac[v], turn(ph, 2 * u + 1, i, 4) + 1)
                        steady(act)
                        A_(A[:, 0, ds(i * 2 + u, 1), :], TT[2][:, :], ACT.Copy).then_inc(ff_hi, 1)
                f0 += nf
            act.wait_ge(xdown, 8 * len(FPARTS))
            norm_act(nf1, X)
            barrier(act, "act", 8)
            norm_act(n3, X, shift=lambda k: mod[:, k, 0:1], hi=H)
            barrier(act, "act", 9)
            act.wait_ge(cx_in, 16)
            act.wait_ge(x_spilled, 16)
            norm_act(ncx, CX, TC, shift=lambda k: mod[:, k, 1:2], hi=HC)
            barrier(act, "act", 10)
            act.wait_ge(aux_done, A0["lr"] + 1)
            A_(LRT[0:48, 0:T], ps[slot("lr", 0)][0:48, :], ACT.Copy).then_inc(evac[slot("lr", 0)], 1)
            act.wait_ge(panel_done, N0["lr"] + 1)
            A_(LRT[0:48, T:T + TC], ps[slot("lr", 1)][0:48, 0:TC], ACT.Copy).then_inc(evac[slot("lr", 1)], 1)
            barrier(act, "act", 11)
            act.wait_ge(blk2_in, 48)
            for u in range(2):
                act.sem_inc(on_out[u], 16)
            with act.Fori(0, HEADS) as h:
                ch.enter(h, HEAD_ACT_STEPS)
                heads_act(act, h, ch)
                ch.leave(HEADS, HEAD_ACT_STEPS)
            for u in range(2):
                act.wait_ge(on_out[u], 16 * (HEADS + 1))
            barrier(act, "act", 12)
            for k in range(4):
                act.dma_start(X[:, 2 * k:2 * k + 2, :], ond[2 * k:2 * k + 2, :, :].rearrange("k p t -> p k t")
                              ).then_inc(on_in[k], 16)
            with act.Fori(0, 2) as i:
                for u in range(4):
                    e = i * 4 + u
                    act.wait_ge(panel_done, e + (N0["za"] + 1))
                    A_(TT[0][:, :], ps[slot("za", u)][:, :], ACT.Silu).then_inc(evac[slot("za", u)], 1)
                    act.wait_ge(za_prod, e + 1)
                    steady(act)
                    A_(A[:, 0, ds(e, 1), :], TT[1][:, :], ACT.Copy).then_inc(za_hi, 1)
            barrier(act, "act", 13)
            act.sem_inc(ma_out, 16)
            with act.Fori(0, 4) as i:
                for u in range(2):
                    g, v = slot("mixa", 2 * u), slot("mixa", 2 * u + 1)
                    act.wait_ge(panel_done, i * 4 + (N0["mixa"] + 2 * u + 1))
                    A_(TT[0][:, :], ps[g][:, :], ACT.Sigmoid).then_inc(evac[g], 1)
                    act.wait_ge(evac[v], turn("mixa", 2 * u + 1, i, 4) + 1)
                    act.dma_start(mad[ds(i * 2 + u, 1), :, :].rearrange("k p t -> (k p) t"), TT[1][:, :]
                                  ).then_inc(ma_out, 16)
            act.wait_ge(ma_out, 16 * (KT + 1))
            barrier(act, "act", 14)
            act.wait_ge(pool_pad, 1)
            for g in range(4):
                if g:
                    act.wait_ge(aux_done, A0["pool"] + 2 * g)
                act.dma_start(wpl[:, :, :], d["wpool"][g].rearrange("p (k m) -> p k m", k=2)).then_inc(pool_in, 16)
                act.dma_start(icnt[:, :], d["icnt"][g]).then_inc(pool_in, 16)
                for u in range(2):
                    s = slot("pool", 6 * g + u)
                    act.wait_ge(panel_done, N0["pool"] + 4 * g + u + 1)
                    A_(up[u][:, PAD:PAD + T], ps[s][:, :], ACT.Copy).then_inc(evac[s], 1)
                for m in range(2):
                    s = slot("pool", 6 * g + 2 + m)
                    act.wait_ge(panel_done, N0["pool"] + 4 * g + 2 + m + 1)
                    A_(TT[m][:, :], ps[s][:, :], ACT.Silu).then_inc(evac[s], 1)
                for m in range(2):
                    act.wait_ge(evac[slot("pool", 6 * g + 4 + m)], turn("pool", 6 * g + 4 + m) + 1)
                    A_(A[:, 0, 2 * g + m, :], TT[2 + m][:, :], ACT.Copy).then_inc(pb_hi, 1)
            barrier(act, "act", 15)
            for k in range(4):
                act.dma_start(X[:, 2 * k:2 * k + 2, :], mad[2 * k:2 * k + 2, :, :].rearrange("k p t -> p k t")
                              ).then_inc(ma_in[k], 16)
            with act.Fori(0, 4) as i:
                for u in range(2):
                    g = slot("mixb", 2 * u)
                    act.wait_ge(panel_done, i * 4 + (N0["mixb"] + 2 * u + 1))
                    act.wait_ge(mb_made, i * 2 + u + 1)
                    A_(TT[0][:, :], ps[g][:, :], ACT.Sigmoid).then_inc(evac[g], 1)
            barrier(act, "act", 16)
            split_act(X, H, m_hi)
            barrier(act, "act", 17)
            norm_act(n4, XN)
            for k in range(KT):
                act.wait_ge(n4.h, k + 1)
                act.dma_start(out[k * P:(k + 1) * P, :], TT[k % 2][:, :]).then_inc(out_st[k % 2], 16)
            for u in range(2):
                act.wait_ge(out_st[u], 16 * (KT // 2))

        @block.vector
        def _(dve):
            V_ = nc.vector
            ch = Steps(dve, dve_chain)

            def norm_dve(n, phase, src, gain, width=T, shift=None, dst=None, in_place=False):
                sl = slot(phase, 0)
                acc, v, r, q = (TT[x][:, 0:width] for x in (2, 3, 2, 1))
                for k in range(KT):
                    dve.wait_ge(n.sq, k + 1)
                    if k == 0:
                        V_.tensor_copy(acc, TT[0][:, 0:width]).then_inc(n.acc, 1)
                    else:
                        dve.wait_ge(n.acc, k)
                        V_.tensor_tensor(acc, acc, TT[k % 2][:, 0:width], ALU.add).then_inc(n.acc, 1)
                dve.wait_ge(aux_done, A0[phase] + 1)
                dve_evac = V_.tensor_scalar(v, ps[sl][:, 0:width], 1.0 / D, EPS, ALU.mult, ALU.add)
                dve_evac.then_inc(evac[sl], 1)
                dve.wait_ge(evac[sl], turn(phase, 0) + 1)
                dve.sem_inc(n.var, 1)
                dve.wait_ge(n.r0, 1)
                ch.link(V_.tensor_tensor(q, q, v, ALU.mult))
                ch.link(V_.tensor_scalar(q, q, -0.5, 1.5, ALU.mult, ALU.add))
                ch.link(V_.tensor_tensor(r, r, q, ALU.mult))

                def low(k):
                    dve.wait_ge(n.hi, k + 1)
                    if shift is None:
                        V_.tensor_tensor(dst[:, 1, k, :], TT[k % 2][:, 0:width], dst[:, 0, k, :].bitcast(F32),
                                         ALU.subtract).then_inc(n.lo, 1)
                    else:
                        V_.scalar_tensor_tensor(out=dst[:, 1, k, :], in0=TT[k % 2][:, 0:width], scalar=shift(k),
                                                in1=dst[:, 0, k, :].bitcast(F32), op0=ALU.add, op1=ALU.subtract
                                                ).then_inc(n.lo, 1)

                for k in range(KT):
                    if k >= 2:
                        if dst is not None:
                            dve.wait_ge(n.lo, k - 1)
                        elif not in_place:
                            dve.wait_ge(out_st[k % 2], 16 * (k // 2))
                    V_.scalar_tensor_tensor(out=src[:, k, :] if in_place else TT[k % 2][:, 0:width], in0=src[:, k, :], scalar=gain(k), in1=r,
                                            op0=ALU.mult, op1=ALU.mult).then_inc(n.h, 1)
                    if k and dst is not None:
                        low(k - 1)
                if dst is not None:
                    low(KT - 1)

            dve.wait_ge(const_in, 32)
            dve.wait_ge(x_in, 16)
            V_.memset(hb[:, :, :], 0.0).then_inc(hb_zero, 1)
            norm_dve(n1, "norm1", X, lambda k: vcol("norm_mix", k), dst=H)
            ch.link(V_.memset(gacc[:, :], 0.0))
            for l in range(3):
                s = slot("mlp", l)
                dve.wait_ge(aux_done, A0["mlp"] + l + 1)
                if l:
                    dve.wait_ge(sin_made, l)
                V_.tensor_scalar(fa[:, :], ps[s][:, :], vcol(f"f_b{l + 1}"), vcol("f_freq"), ALU.add, ALU.mult
                                 ).then_inc(evac[s], 1)
                dve.wait_ge(evac[s], turn("mlp", l) + 1)
                ch.link(V_.tensor_scalar(fu[:, :], fa[:, :], 1.0 / (2 * np.pi), MAGIC, ALU.mult, ALU.add))
                ch.link(V_.tensor_scalar(fu[:, :], fu[:, :], MAGIC, None, ALU.subtract))
                for cst_ in (C1, C2, C3):
                    ch.link(V_.scalar_tensor_tensor(out=fa[:, :], in0=fu[:, :], scalar=-cst_, in1=fa[:, :],
                                                    op0=ALU.mult, op1=ALU.add))
                V_.tensor_scalar(fu[:, :], fa[:, :], PI_LOW, -PI_LOW, ALU.min, ALU.max).then_inc(arg_made, 1)
            with dve.Fori(0, N2 // 2) as i:
                ch.enter(i, 2)
                for u in range(2):
                    s = slot("taps", u)
                    dve.wait_ge(aux_done, i * 4 + (A0["taps"] + 1 + u))
                    dve.wait_ge(decay_made, i * 2 + u + 1)
                    if u:
                        dve.wait_ge(tap_sum, i * 2 + 1)
                    V_.tensor_tensor(tap[u][:, :], ps[s][:, :], dk_[u][:, :], ALU.mult).then_inc(evac[s], 1)
                    dve.wait_ge(evac[s], turn("taps", u, i, 4) + 1)
                    ch.link(V_.scalar_tensor_tensor(out=fa[:, :], in0=tap[u][:, :], scalar=-1.0, in1=tap[u][:, :],
                                                    op0=ALU.mult, op1=ALU.max))
                    V_.tensor_tensor(gacc[:, :], fa[:, :], gacc[:, :], ALU.add).then_inc(tap_sum, 1)
                dve.wait_ge(tap_sum, i * 2 + 2)
                ch.leave(N2 // 2, 2)
            s = slot("tapnorm", 0)
            dve.wait_ge(aux_done, A0["tapnorm"] + 1)
            V_.reciprocal(rn[:, :], ps[s][:, 0:8]).then_inc(evac[s], 1)
            barrier(dve, "dve", 1)
            for z in zp:
                ch.do(V_.memset(z[:, 0:1], 0.0))
                ch.do(V_.memset(z[:, T + 1:T + 2], 0.0))
            ch.wait()
            dve.sem_inc(zpad_zero, 1)
            dve.sem_inc(z_used, 2)

            def conv(z, f, tmp, dst):
                ch.link(V_.tensor_scalar(tmp, z[:, 1:T + 1], vcol("cw1", f), vcol("cb", f), ALU.mult, ALU.add))
                ch.link(V_.scalar_tensor_tensor(out=tmp, in0=z[:, 0:T], scalar=vcol("cw0", f), in1=tmp,
                                                op0=ALU.mult, op1=ALU.add))
                V_.scalar_tensor_tensor(out=dst, in0=z[:, 2:T + 2], scalar=vcol("cw2", f), in1=tmp,
                                        op0=ALU.mult, op1=ALU.add).then_inc(z_used, 1)

            with dve.Fori(0, 2) as i:
                ch.enter(i, 8)
                for u in range(4):
                    dve.wait_ge(evac[slot("zin", u)], turn("zin", u, i, 4) + 1)
                    conv(zp[u % 2], i * 4 + u, ca[:, :], G0[:, ds(i * 4 + u, 1), :].rearrange("p a t -> p (a t)"))
                    dve.wait_ge(z_used, i * 4 + u + 3)
                ch.leave(2, 8)
            with dve.Fori(0, 4) as i:
                ch.enter(i, 8)
                for u in range(4):
                    dve.wait_ge(evac[slot("zin", u)], turn("zin", 8 + u, i, 4) + 1)
                    t = (ca, cb_)[u % 2]
                    conv(zp[u % 2], i * 2 + (8 + 8 * (u % 2) + u // 2), t[:, :], t[:, :])
                    dve.wait_ge(z_used, i * 4 + 8 + u + 3)
                    if u % 2:
                        V_.tensor_tensor(S[:, ds(i * 2 + u // 2, 1), :].rearrange("p a t -> p (a t)"), ca[:, :], cb_[:, :],
                                         ALU.mult).then_inc(s_made, 1)
                        dve.wait_ge(s_made, i * 2 + u // 2 + 1)
                ch.leave(4, 8)
            barrier(dve, "dve", 2)
            with dve.Fori(0, N2 // 2) as i:
                for u in range(2):
                    s = slot("sfwd", 2 + u)
                    dve.wait_ge(aux_done, i * 4 + (A0["sfwd"] + 3 + u))
                    dve.wait_ge(s1_out[u], i * 16 + 16)
                    V_.tensor_copy(sa[u][:, :], ps[s][:, :]).then_inc(evac[s], 1)
            for u in range(2):
                dve.wait_ge(s1_out[u], 16 * (N2 // 2 + 1))
            barrier(dve, "dve", 3)
            s = slot("mod", 0)
            dve.wait_ge(mod_used, 24)
            V_.tensor_tensor(mod[:, :, :], ps[s][:, 0:48].rearrange("p (f w) -> p f w", w=2),
                             vec[:, VEC["b_mod"]:VEC["b_mod"] + 24].unsqueeze(2).to_broadcast([P, 24, 2]), ALU.add
                             ).then_inc(evac[s], 1)
            dve.wait_ge(evac[s], turn("mod", 0) + 1)
            ch.link(V_.tensor_scalar(mgs[:, :, :], mod[:, 8:16, :], 1.0, None, ALU.add))
            ch.link(V_.tensor_tensor(mgs[:, :, :], mgs[:, :, :],
                                     vec[:, VEC["norm2"]:VEC["norm2"] + 8].unsqueeze(2).to_broadcast([P, 8, 2]), ALU.mult))
            barrier(dve, "dve", 4)
            for n in range(2 * GROUPS):
                c = n % 2
                dve.wait_ge(spec_mm, n + 1)
                dve.wait_ge(spec_g, 2 * n + 1)
                ch.do(V_.tensor_tensor(t1[c][:, :], ps[2 * c][:, 0:512], ga[c][:, :], ALU.mult))
                dve.wait_ge(spec_g, 2 * n + 2)
                ch.link(V_.tensor_tensor(t2[c][:, :], ps[2 * c][:, 512:1024], gb[c][:, :], ALU.mult))
                V_.tensor_tensor(yy[c][:, :], t1[c][:, :], t2[c][:, :], ALU.add).then_inc(spec_y, 1)
                if n:
                    dve.wait_ge(spec_y, n)
            barrier(dve, "dve", 5)
            for e in range(KT):
                s = slot("inv", e)
                ch.do(V_.tensor_scalar(TT[0][:, :], S[:, e, :], vcol("skip", e), None, ALU.mult))
                ch.wait()
                dve.wait_ge(aux_done, A0["inv"] + e + 1)
                V_.scalar_tensor_tensor(out=TT[1][:, :].rearrange("p (a b) -> p a b", b=N2),
                                        in0=ps[s][:, :].rearrange("p (b a) -> p a b", a=HALF),
                                        scalar=rn[:, e:e + 1], in1=TT[0][:, :].rearrange("p (a b) -> p a b", b=N2),
                                        op0=ALU.mult, op1=ALU.add).then_inc(evac[s], 1)
                dve.wait_ge(evac[s], turn("inv", e) + 1)
                ch.link(V_.tensor_tensor(G0[:, e, :], TT[1][:, :], G0[:, e, :], ALU.mult))
            barrier(dve, "dve", 6)

            def split_dve(src, dst, hi, lo):
                for k in range(KT):
                    dve.wait_ge(hi, k + 1)
                    V_.tensor_tensor(dst[:, 1, k, :], src[:, k, :], dst[:, 0, k, :].bitcast(F32), ALU.subtract
                                     ).then_inc(lo, 1)

            split_dve(G0, H, sp1_hi, sp1_lo)
            dve.wait_ge(xr_in, 16)
            with dve.Fori(0, 2) as i:
                for u in range(4):
                    e = i * 4 + u
                    dve.wait_ge(panel_done, e + (N0["wout"] + 1))
                    x = X[:, ds(e, 1), :].rearrange("p a t -> p (a t)")
                    V_.scalar_tensor_tensor(out=x, in0=ps[slot("wout", u)][:, :], scalar=vcol("b_out", e), in1=x,
                                            op0=ALU.add, op1=ALU.add).then_inc(evac[slot("wout", u)], 1)
            barrier(dve, "dve", 7)
            norm_dve(n2, "norm2", X, lambda k: vcol("norm_ffn", k), dst=H)
            f0 = 0
            for p, nf in enumerate(FPARTS):
                ph = f"up{p}"
                with dve.Fori(0, nf // 2) as i:
                    for u in range(2):
                        g, v = slot(ph, 2 * u), slot(ph, 2 * u + 1)
                        f = i * 2 + (f0 + u)
                        dve.wait_ge(panel_done, i * 4 + (N0[ph] + 2 * u + 2))
                        dve.wait_ge(evac[g], turn(ph, 2 * u, i, 4) + 1)
                        V_.tensor_tensor(TT[2][:, :], TT[0][:, :], ps[v][:, :], ALU.mult).then_inc(evac[v], 1)
                        dve.wait_ge(ff_hi, f + 1)
                        V_.tensor_tensor(A[:, 1, ds(i * 2 + u, 1), :].rearrange("p a t -> p (a t)"), TT[2][:, :],
                                         A[:, 0, ds(i * 2 + u, 1), :].rearrange("p a t -> p (a t)").bitcast(F32),
                                         ALU.subtract).then_inc(ff_lo, 1)
                        dve.wait_ge(ff_lo, f + 1)
                f0 += nf
                ph = f"down{p}"
                with dve.Fori(0, 2) as i:
                    for u in range(4):
                        e = i * 4 + u
                        dve.wait_ge(panel_done, e + (N0[ph] + 1))
                        x = X[:, ds(e, 1), :].rearrange("p a t -> p (a t)")
                        V_.tensor_tensor(x, ps[slot(ph, u)][:, :], x, ALU.add).then_inc(evac[slot(ph, u)], 1)
                        dve.wait_ge(evac[slot(ph, u)], turn(ph, u, i, 4) + 1)
            dve.sem_inc(xdown, 8 * len(FPARTS))
            norm_dve(nf1, "normf", X, lambda k: vcol("norm_final", k), in_place=True)
            barrier(dve, "dve", 8)
            norm_dve(n3, "norm3", X, lambda k: mgs[:, k, 0:1], shift=lambda k: mod[:, k, 0:1], dst=H)
            barrier(dve, "dve", 9)
            dve.wait_ge(cx_in, 16)
            dve.wait_ge(x_spilled, 16)
            norm_dve(ncx, "normc", CX, lambda k: mgs[:, k, 1:2], TC, shift=lambda k: mod[:, k, 1:2], dst=HC)
            barrier(dve, "dve", 10)
            barrier(dve, "dve", 11)
            dve.wait_ge(blk2_in, 48)
            with dve.Fori(0, HEADS) as h:
                ch.enter(h, HEAD_STEPS)
                heads_dve(dve, h, ch)
                ch.leave(HEADS, HEAD_STEPS)
            barrier(dve, "dve", 12)
            with dve.Fori(0, 2) as i:
                for u in range(4):
                    e = i * 4 + u
                    for k in range(4):
                        dve.wait_ge(on_in[k], 16)
                    dve.wait_ge(evac[slot("za", u)], turn("za", u, i, 4) + 1)
                    V_.tensor_tensor(TT[1][:, :], TT[0][:, :], X[:, ds(e, 1), :].rearrange("p a t -> p (a t)"), ALU.mult
                                     ).then_inc(za_prod, 1)
                    dve.wait_ge(za_hi, e + 1)
                    V_.tensor_tensor(A[:, 1, ds(e, 1), :].rearrange("p a t -> p (a t)"), TT[1][:, :],
                                     A[:, 0, ds(e, 1), :].rearrange("p a t -> p (a t)").bitcast(F32), ALU.subtract
                                     ).then_inc(za_lo, 1)
                    dve.wait_ge(za_lo, e + 1)
            barrier(dve, "dve", 13)
            with dve.Fori(0, 4) as i:
                for u in range(2):
                    g, v = slot("mixa", 2 * u), slot("mixa", 2 * u + 1)
                    dve.wait_ge(panel_done, i * 4 + (N0["mixa"] + 2 * u + 2))
                    dve.wait_ge(evac[g], turn("mixa", 2 * u, i, 4) + 1)
                    dve.wait_ge(ma_out, i * 32 + 16 * u + 16)
                    V_.tensor_tensor(TT[1][:, :], TT[0][:, :], ps[v][:, :], ALU.mult).then_inc(evac[v], 1)
            barrier(dve, "dve", 14)
            for t in up:
                ch.do(V_.memset(t[:, 0:PAD], 0.0))
                ch.do(V_.memset(t[:, PAD + T:W_U], 0.0))
            ch.wait()
            dve.sem_inc(pool_pad, 1)
            for g, w in enumerate(POOL_WINDOWS):
                dve.wait_ge(pool_in, 32 * (g + 1))
                for u in range(2):
                    s = slot("pool", 6 * g + u)
                    dve.wait_ge(evac[s], turn("pool", 6 * g + u) + 1)
                    src, span, width, q = up[u], 1, W_U, 0
                    while span < w:
                        width -= span
                        dst = (wa, wb)[q % 2]
                        ch.link(V_.tensor_tensor(dst[:, 0:width], src[:, 0:width], src[:, span:span + width], ALU.add))
                        src, span, q = dst, span * 2, q + 1
                    lo = PAD - w // 2
                    ch.link(V_.tensor_tensor(pd[u][:, :], src[:, lo:lo + T], icnt[:, :], ALU.mult))
                    V_.tensor_tensor(pd[u][:, :], pd[u][:, :], up[u][:, PAD:PAD + T], ALU.subtract).then_inc(pd_made, 1)
                    dve.wait_ge(pd_made, 2 * g + u + 1)
                for m in range(2):
                    s = slot("pool", 6 * g + 4 + m)
                    dve.wait_ge(aux_done, A0["pool"] + 2 * g + m + 1)
                    dve.wait_ge(evac[slot("pool", 6 * g + 2 + m)], turn("pool", 6 * g + 2 + m) + 1)
                    V_.scalar_tensor_tensor(out=TT[2 + m][:, :], in0=ps[s][:, :], scalar=vcol("pool_scale", 2 * g + m),
                                            in1=TT[m][:, :], op0=ALU.mult, op1=ALU.mult).then_inc(evac[s], 1)
                    dve.wait_ge(pb_hi, 2 * g + m + 1)
                    V_.tensor_tensor(A[:, 1, 2 * g + m, :], TT[2 + m][:, :], A[:, 0, 2 * g + m, :].bitcast(F32),
                                     ALU.subtract).then_inc(pb_lo, 1)
                    dve.wait_ge(pb_lo, 2 * g + m + 1)
            barrier(dve, "dve", 15)
            for k in range(4):
                dve.wait_ge(ma_in[k], 16)
            dve.sem_inc(mb_made, 1)
            with dve.Fori(0, 4) as i:
                for u in range(2):
                    g, v = slot("mixb", 2 * u), slot("mixb", 2 * u + 1)
                    e = i * 2 + u
                    dve.wait_ge(panel_done, i * 4 + (N0["mixb"] + 2 * u + 2))
                    dve.wait_ge(evac[g], turn("mixb", 2 * u, i, 4) + 1)
                    V_.tensor_tensor(TT[0][:, :], TT[0][:, :], ps[v][:, :], ALU.mult).then_inc(evac[v], 1)
                    dve.wait_ge(evac[v], turn("mixb", 2 * u + 1, i, 4) + 1)
                    x = X[:, ds(e, 1), :].rearrange("p a t -> p (a t)")
                    V_.tensor_tensor(x, x, TT[0][:, :], ALU.add).then_inc(mb_made, 1)
                    dve.wait_ge(mb_made, e + 2)
            barrier(dve, "dve", 16)
            split_dve(X, H, m_hi, m_lo)
            dve.wait_ge(xr2_in, 16)
            with dve.Fori(0, 2) as i:
                for u in range(4):
                    e = i * 4 + u
                    dve.wait_ge(panel_done, e + (N0["wout2"] + 1))
                    x = XN[:, ds(e, 1), :].rearrange("p a t -> p (a t)")
                    V_.scalar_tensor_tensor(out=x, in0=ps[slot("wout2", u)][:, :],
                                            scalar=mod[:, ds(e + 16, 1), 0:1].rearrange("p a b -> p (a b)"), in1=x,
                                            op0=ALU.mult, op1=ALU.add).then_inc(evac[slot("wout2", u)], 1)
            barrier(dve, "dve", 17)
            norm_dve(n4, "norm4", XN, lambda k: vcol("final2", k))



def _constants():
    f8 = np.float64
    cst = np.zeros((P, NCST), np.float32)

    def put(name, a):
        cst[:a.shape[0], CST[name]:CST[name] + a.shape[1]] = a

    put("ident", np.eye(P))
    put("ones", np.ones((P, P)))
    j, i = np.meshgrid(np.arange(P), np.arange(P), indexing="ij")
    put("mask_f", (j <= i) * 1.0)
    put("mask_b", (j >= i) * 1.0)
    m = np.arange(P)
    swap = np.where(m % 64 < 32, m + 32, m - 32)
    perm = np.zeros((P, P))
    perm[swap, m] = 1
    put("perm", perm)
    n1, k1 = np.arange(N1, dtype=f8)[:, None], np.arange(HALF, dtype=f8)[None, :]
    th = 2 * np.pi * n1 * (k1 + 0.5) / N1
    dft = np.stack([np.cos(th), -np.sin(th)], -1).reshape(N1, P)
    put("dft_s", dft[:HALF])
    put("dft_g", dft * np.where(np.arange(N1) < HALF, 1.0, -1.0)[:, None])
    inv = np.stack([np.cos(th[:HALF]), -np.sin(th[:HALF])], -1).reshape(HALF, P).T / (N1 * N2 / 2)
    put("idft", inv)
    r, n2 = np.arange(P)[:, None], np.arange(N2)[None, :]
    tok = np.where(r < HALF, N2 * r + n2, N2 * (N1 - r) - n2)
    none = tok >= T
    tok = np.where(none, 0, tok)
    t = np.linspace(0.0, 1.0, T, dtype=np.float32)
    put("tneg", -t[tok])
    put("tmask", np.where(none, -1e30, 0.0))
    w = (np.float32(2.0 * np.pi) * np.arange(T, dtype=np.float32) / np.float32(T))[:, None]
    bands = np.linspace(1e-4, 15, 16, dtype=np.float32)[None, :]
    arg = (bands * w).astype(f8)
    ft = np.concatenate([t[:, None], np.cos(arg), -np.sin(arg)], -1).astype(np.float32)
    cols = tok.reshape(2, HALF, N2).transpose(0, 2, 1).reshape(2, T)
    feat = np.concatenate([ft[cols[0]].T, ft[cols[1]].T], 0)
    kf = np.zeros((GROUPS, P, 5, P))
    a, b = np.arange(N2, dtype=f8)[:, None], np.arange(N2, dtype=f8)[None, :]
    for k in range(HALF):
        g, o = k // 4, (k % 4) * 32
        th = 2 * np.pi * (a * (k + 0.5) / (N1 * N2) + a * b / N2)
        c, s = np.cos(th), np.sin(th)
        re, im = np.concatenate([c, s], 0), np.concatenate([-s, c], 0)
        blk = kf[g, o:o + 32]
        blk[:, 0, o:o + 32] = np.concatenate([re, im], 1)
        blk[:, 1, o:o + 32] = np.concatenate([im, re], 1)
        blk[:, 2, o:o + 32] = np.concatenate([re, re], 1)
        blk[:, 3, o:o + 32] = np.concatenate([-im, im], 1)
        blk[:, 4, o:o + 32] = np.block([[c.T, s.T], [-s.T, c.T]])
    tt = np.arange(T)
    fr = np.float32(10000.0) ** (-np.arange(32, dtype=np.float32) / np.float32(32))
    cos, sin = np.zeros((P, T)), np.zeros((P, T))
    for p in range(P):
        pos = (tt // 64 if p < 64 else tt % 64).astype(np.float32)
        an = (pos * fr[p % 32]).astype(f8)
        cos[p] = np.cos(an)
        sin[p] = np.sin(an) * (-1 if p % 64 < 32 else 1)
    icnt = np.zeros((4, P, T))
    for g, wd in enumerate(POOL_WINDOWS):
        lo = np.clip(tt - wd // 2, 0, T - 1)
        hi = np.clip(tt + (wd - 1 - wd // 2), 0, T - 1)
        icnt[g] = 1.0 / (hi - lo + 1)
    f4 = lambda x: np.ascontiguousarray(x, np.float32)
    return {"cst": cst, "feat": f4(feat), "kfft": f4(kf.reshape(GROUPS, P, 5 * P)), "cos": f4(cos), "sin": f4(sin),
            "icnt": f4(icnt)}


def _layout(x):
    g = {k: np.asarray(v) for k, v in x.items()}
    cols = lambda a: np.asarray(a).reshape(-1, P).T
    vec = np.zeros((P, NVEC), np.float32)
    for name, a in (("norm_mix", g["norm_mix"]), ("norm_ffn", g["norm_ffn"]), ("norm_final", g["norm_final"]),
                    ("b_in", g["hy_b_in"]), ("cw0", g["hy_conv_w"][0, 0]), ("cw1", g["hy_conv_w"][0, 1]),
                    ("cw2", g["hy_conv_w"][0, 2]), ("cb", g["hy_conv_b"]), ("skip", g["hy_skip"]),
                    ("b_out", g["hy_b_out"]), ("norm2", g["norm_g_2"]), ("b_mod", g["b_mod_2"]),
                    ("b_gf", g["b_gate_f_2"]), ("b_gb", g["b_gate_b_2"]), ("gla_g", g["gla_norm_g_2"]),
                    ("pool_scale", g["pool_scale_2"]), ("final2", g["final_norm_g_2"]), ("c", g["c_2"]),
                    ("c_ctx", g["c_ctx_2"])):
        a = cols(a)
        vec[:, VEC[name]:VEC[name] + a.shape[1]] = a
    for name, key in (("f_b1", "hy_f_b1"), ("f_b2", "hy_f_b2"), ("f_b3", "hy_f_b3"), ("f_freq", "hy_f_freq")):
        vec[:HALF, VEC[name]] = vec[HALF:, VEC[name]] = g[key][0]
    w1, w2, w3, wo = g["hy_f_w1"][0], g["hy_f_w2"][0], g["hy_f_w3"][0], g["hy_f_wout"][0]

    def twice(w):
        a = np.zeros((2 * w.shape[0], 2 * w.shape[1]), np.float32)
        a[:w.shape[0], :w.shape[1]] = w
        a[w.shape[0]:, w.shape[1]:] = w
        return a

    wtap = np.concatenate([wo[:, :D], wo[:, D:]], 0)
    dec = np.concatenate([np.repeat(g["hy_decay"][0, :1], HALF, 0), np.repeat(g["hy_decay"][0, 1:], HALF, 0)], 0)

    def panel(w):
        a = np.zeros((D, P), np.float32)
        a[:w.shape[0], :w.shape[1]] = w
        return a.reshape(8, P, P).transpose(1, 0, 2).reshape(P, D)

    out = []

    def add(w, f, rows=slice(None)):
        out.append(panel(w[rows, f * P:(f + 1) * P]))

    win, wi2 = g["hy_w_in"][0], g["w_in_2"][0]
    q_, k_, v_, za, lr, ub, zb, ga, gb = np.cumsum([0, 512, 512, 1024, 1024, 32, 1024, 1024, 1024])
    for f in range(8):
        add(win, f)
    for f in range(8):
        add(win, 8 + f)
        add(win, 16 + f)
    for f in range(8):
        add(g["hy_w_out"][0], f)
    f0 = 0
    for nf in FPARTS:
        for f in range(f0, f0 + nf):
            add(g["ffn_w_gate"][0], f)
            add(g["ffn_w_up"][0], f)
        for f in range(8):
            add(g["ffn_w_down"][0], f, slice(f0 * P, (f0 + nf) * P))
        f0 += nf
    low = np.zeros((D, 48), np.float32)
    low[:, 0:16] = wi2[:, lr:lr + 16]
    low[:, 32:48] = wi2[:, lr + 16:lr + 32]
    out.append(panel(low))
    for h in range(HEADS):
        add(wi2[:, q_:k_], h)
        add(wi2[:, k_:v_], h)
        first = (N0["heads"] + 2) % 2
        for e in (first, 1 - first):
            add(wi2[:, v_:za], 2 * h + e)
    for f in range(8):
        add(wi2[:, za:lr], f)
    for f in range(8):
        add(wi2[:, ga:gb], f)
        add(g["w_branch_a_2"][0], f)
    for q in range(4):
        for w0 in (ub, zb):
            for u in range(2):
                add(wi2[:, w0:w0 + D], 2 * q + u)
    for f in range(8):
        add(wi2[:, gb:], f)
        add(g["w_branch_b_2"][0], f)
    for f in range(8):
        add(g["w_out_2"][0], f)
    assert len(out) == NPANELS
    modp = np.stack([panel(g["w_mod_2"][0][:, f * P:(f + 1) * P]) for f in range(24)])
    wup = np.zeros((48, HEADS * DK), np.float32)
    wup[0:16] = g["w_gate_up_f_2"][0]
    wup[32:48] = g["w_gate_up_b_2"][0]
    wpool = g["w_pool_2"][0].reshape(4, 2, P, 256).transpose(0, 2, 1, 3).reshape(4, P, 512)
    c = np.ascontiguousarray
    return {"vec": vec, "xT": c(g["x"][0].T), "ctxT": c(g["ctx_2"][0].T), "panels": np.stack(out), "modp": modp,
            "fw1": twice(w1), "fw2": twice(w2), "fw3": twice(w3), "wtap": c(wtap), "dec": c(dec), "wup": wup,
            "wpool": c(wpool)}


def kernel(**inputs):
    import concourse.bacc as _bacc
    from concourse.bass_utils import run_bass_kernel_spmd as _run

    arrays = {**_layout(inputs), **_constants()}
    nc = _bacc.Bacc("TRN2", target_bir_lowering=False, num_devices=1)
    args = {n: nc.dram_tensor(f"in_{n}", a.shape, F32, kind="ExternalInput").ap() for n, a in arrays.items()}
    out = nc.dram_tensor("out_T", (D, T), F32, kind="ExternalOutput").ap()
    program(nc, args, out)
    r = _run(nc, [{f"in_{n}": a for n, a in arrays.items()}], core_ids=[0])
    return np.ascontiguousarray(r.results[0]["out_T"].T)[None]
```

```python
from contextlib import ExitStack

import numpy as np
import concourse.bass as bass
from concourse import mybir

F32 = mybir.dt.float32
F32R = mybir.dt.float32r
ACT = mybir.ActivationFunctionType
ALU = mybir.AluOpType
ds = bass.ds

P = 128
D = 1024
T = 1024
KT = D // P
TC = 256
F = 2816
FPARTS = (8, 8, 6)
EPS = 1e-6
HEADS, DK, DV = 4, 128, 256
CH = 128
NCH = T // CH
NCC = TC // CH
GATE_NORM = 16.0
CLAMP = 40.0 * GATE_NORM
N1, N2 = 128, 16
HALF = N1 // 2
GROUPS = 16
POOL_WINDOWS = (2, 4, 8, 16)
PAD = 8
MAGIC = 1.5 * 2.0 ** 23
C1 = 6.28125
C2 = float(np.float32(np.round((2 * np.pi - C1) * 2 ** 20) / 2 ** 20))
C3 = float(np.float32(2 * np.pi - C1 - C2))
PI_LOW = 3.1415925

VEC = {}
_c = 0
for _n, _w in (("norm_mix", 8), ("norm_ffn", 8), ("norm_final", 8), ("b_in", 24), ("cw0", 24), ("cw1", 24),
               ("cw2", 24), ("cb", 24), ("skip", 8), ("b_out", 8), ("norm2", 8), ("b_mod", 24), ("b_gf", 4),
               ("b_gb", 4), ("gla_g", 2), ("pool_scale", 8), ("final2", 8), ("f_b1", 1), ("f_b2", 1),
               ("f_b3", 1), ("f_freq", 1)):
    VEC[_n] = _c
    _c += _w
NVEC = _c
CST = {}
_c = 0
for _n, _w in (("ident", 128), ("ones", 128), ("mask_f", 128), ("mask_b", 128), ("perm", 128), ("dft_g", 128),
               ("dft_s", 128), ("idft", 64), ("tneg", 16), ("tmask", 16)):
    CST[_n] = _c
    _c += _w
NCST = _c

PHASES = [("mlp0", 1, 0), ("norm1", 1, 0), ("zin0", 1, 1), ("mlp1", 1, 0), ("zin1", 1, 1), ("mlp2", 1, 0),
          ("zin2", 2, 2), ("zin3", 12, 12), ("mix", 40, 8), ("sfwd", 32, 0), ("tapnorm", 1, 0), ("inv", 8, 0),
          ("wout", 8, 8), ("norm2", 1, 0)]
UPS = [[(f"up{_p}", _n // 2)] for _p, _n in enumerate(FPARTS)]
UPS[-1] = [("up2", 1), ("up2b", FPARTS[-1] // 2 - 1)]
for _p, _ups in enumerate(UPS):
    for _u, (_name, _trips) in enumerate(_ups):
        PHASES += [(_name, 4 * _trips, 4 * _trips)]
        if len(_ups) > 1:
            PHASES += [(("normc", "normcb")[_u], 1, 0)]
    PHASES += [(f"down{_p}", 8, 8)]
HJ, HP, HA = 28, 8, 21
PHASES += [("normf", 1, 0), ("norm3", 1, 0), ("lr", 2, 1), ("heads", HJ * HEADS, HP * HEADS), ("mixa", 8, 8),
           ("pool", 24, 16), ("gb", 8, 8), ("mixb", 8, 8), ("wout2", 8, 8), ("norm4", 1, 0)]
J0, N0, A0 = {}, {}, {}
_j = _n_ = 0
for _name, _jobs, _pan in PHASES:
    J0[_name], N0[_name] = _j, _n_
    _j += _jobs
    _n_ += _pan
NPANELS = _n_
_a = 0
AUX = {"norm1": 1, "mlp0": 1, "mlp1": 1, "mlp2": 1, "mix": 32, "tapnorm": 1, "sfwd": 32, "inv": 8, "norm2": 1, "normf": 1, "normc": 1, "lr": 1,
       "heads": HA * HEADS, "pool": 8, "norm4": 1}
for _name, _, _ in PHASES:
    A0[_name] = _a
    _a += AUX.get(_name, 0)


class Steps:

    def __init__(self, eng, sem):
        self.eng, self.sem, self.n, self.base = eng, sem, 0, 0

    def do(self, ins):
        ins.then_inc(self.sem, 1)
        self.n += 1

    def wait(self, but=0):
        self.eng.wait_ge(self.sem, self.base + (self.n - but))

    def link(self, ins):
        self.do(ins)
        self.wait()

    def enter(self, i, per):
        self.base, self.start = i * per, self.n

    def leave(self, trips, per):
        assert self.n - self.start == per, (self.n - self.start, per)
        self.base, self.n = 0, self.start + trips * per


def program(nc, d, out):
    ctx = ExitStack()
    with ctx:
        base = -(-nc.sbuf_base // 64) * 64

        def at(name, shape, offset, dt=F32):
            return nc.alloc_sbuf_tensor_at(name, shape, dt, offset=offset)

        def sem(name):
            return ctx.enter_context(nc.semaphore(name))

        o_vec = base
        o_cst = o_vec + NVEC * 4 + 8
        o_small = o_cst + NCST * 4
        o_raw = base + 5504
        o_wh = o_raw + 8192
        o_wl = o_wh + 8192
        RH = o_wl + 8192
        RA = RH + 65536
        RX = RA + 65536
        RT = RX + 32768
        assert o_small + 568 <= o_raw and RT + 18880 <= nc.sbuf_usable_end
        K = 1024
        vec = at("vec", [P, NVEC], o_vec)
        cst = at("cst", [P, NCST], o_cst)
        rn = at("rn", [P, 8], o_small)
        mod = at("mod", [P, 24, 2], o_small + 32)
        mgs = at("mgs", [P, 8, 2], o_small + 224)
        macc = at("macc", [P, 8, 2], o_small + 288)
        nv, nr, nq = (at(f"n{x}", [P, 16], o_small + 352 + 64 * k) for k, x in enumerate("vrq"))
        nc_ = at("nctx", [P, 3, 2], o_small + 544)
        cv, cr, cq = (nc_[:, k, :] for k in range(3))
        gfm = at("gfm", [P, 8], o_small)
        wraw = at("wraw", [P, 2, 8, P], o_raw)
        whi = at("whi", [P, 2, 8, P], o_wh, F32R)
        wlo = at("wlo", [P, 2, 8, P], o_wl, F32R)
        H = at("H", [P, 2, KT, T], RH, F32R)
        A = at("A", [P, 2, KT, T], RA, F32R)
        X = at("X", [P, KT, T], RX)
        TT = [at(f"T{i}", [P, T], RT + 4 * K * i) for i in range(4)]
        feat = at("feat", [66, T], RA + 32 * K)
        fa = at("fa", [P, T], RA + 36 * K)
        fu = at("fu", [P, T], RA + 40 * K)
        fh = at("fh", [P, T], RA + 44 * K)
        fw1 = at("fw1", [66, P], RA + 8 * K)
        fw2 = at("fw2", [P, P], RA + 8 * K + 512)
        fw3 = at("fw3", [P, P], RA + 9 * K)
        crep = at("crep", [P, 2 * D], RX + 12 * K)
        mw = [at(f"mw{m}", [P, D], RA + 48 * K + 4 * K * m) for m in range(4)]
        mprod = at("mprod", [P, D], RX + 28 * K)
        wtap = at("wtap", [P, T], RX)
        dec = at("dec", [P, T], RX + 4 * K)
        hb = at("hb", [P, N2, HALF], RX + 8 * K)
        tap = [at(f"tap{u}", [P, T], RX + 12 * K + 4 * K * u) for u in range(2)]
        gsp = [at(f"gsp{u}", [P, T], RX + 20 * K + 4 * K * u) for u in range(2)]
        gacc = at("gacc", [P, T], RX + 28 * K)
        hbs = [at(f"hbs{u}", [P, N1], RT + 16896 + 512 * u) for u in range(2)]
        S = at("S", [P, KT, T], RA)
        G0 = at("G0", [P, KT, T], RA + 32 * K)
        zp = [at(f"zp{u}", [P, T + 2], RT + 4128 * u) for u in range(2)]
        ca = at("ca", [P, T], RT + 8256)
        cb_ = at("cb_", [P, T], RT + 8256 + 4 * K)
        tabs = at("tabs", [P, T], RT + 8256 + 4 * K)
        sn = [at(f"sn{u}", [P, KT, HALF], RH + 2 * K * u) for u in range(2)]
        st_ = [at(f"st{u}", [HALF, T], RH + 4 * K + 4 * K * u) for u in range(2)]
        sa = [at(f"sa{u}", [P, T], RH + 12 * K + 4 * K * u) for u in range(2)]
        kf = [at(f"kf{u}", [P, 5, P], RX + 2560 * u) for u in range(3)]
        bs = [at(f"bs{u}", [P, T], RX + 8 * K + 4 * K * u) for u in range(2)]
        bg = [at(f"bg{u}", [P, T], RX + 16 * K + 4 * K * u) for u in range(2)]
        ga = [at(f"ga{u}", [P, 512], RX + 24 * K + 2 * K * u) for u in range(2)]
        gb = [at(f"gb{u}", [P, 512], RX + 28 * K + 2 * K * u) for u in range(2)]
        ya = [at(f"ya{u}", [P, 512], RT + 2 * K * u) for u in range(2)]
        yb = [at(f"yb{u}", [P, 512], RT + 4 * K + 2 * K * u) for u in range(2)]
        yi = [at(f"yi{u}", [P, 512], RT + 12 * K + 2 * K * u) for u in range(2)]
        YB = at("YB", [P, N2, T], RH)
        CX = [at(f"CX{u}", [P, 4, TC], RT + 4 * K + 8 * K * u) for u in range(2)]
        cxacc = at("cxacc", [P, TC], RA + 63 * K)
        HC = [at("HCH", [P, KT, TC], RA + 24 * K, F32R), at("HCL", [P, KT, TC], RA + 56 * K, F32R)]
        QT = at("QT", [P, T], RA)
        KTt = at("KT", [P, T], RA + 4 * K)
        BB = [at("BF", [P, T], RA + 8 * K), at("BB", [P, T], RA + 12 * K)]
        QD = [at("QF", [P, T], RA + 16 * K), QT]
        KD = [at("KF", [P, T], RA + 20 * K), KTt]
        KDT = [at("KFT", [P, NCH, P], RA + 32 * K), at("KBT", [P, NCH, P], RA + 36 * K)]
        ROT = [at("ROTQ", [P, T], RA + 32 * K), at("ROTK", [P, T], RA + 36 * K)]
        KDTC = at("KDTC", [P, 2, NCC, P], RA + 40 * K)
        KC = at("KC", [P, TC], RA + 42 * K)
        BBC = at("BBC", [P, 2, TC], RA + 43 * K)
        KDC = at("KDC", [P, 2, TC], RA + 45 * K)
        COS = at("COS", [P, T], RA + 47 * K)
        LRT = at("LRT", [48, T + TC], RA + 51 * K)
        wup_h = at("wup_h", [48, DK], o_cst + CST["dft_g"] * 4)
        SIN = at("SIN", [P, T], RX)
        V = at("V", [P, NCH, DV], RX + 4 * K)
        VC = at("VC", [P, NCC, DV], RX + 12 * K)
        SR = [at("SRF", [P, NCH, DV], RX + 16 * K), at("SRB", [P, NCH, DV], RX + 24 * K)]
        SCO = TT[0:2]
        OE, SZA, SGA = [KD[0], KD[1]], BB, ROT
        SS = [at("SF", [P, DV], RT + 16 * K), at("SB", [P, DV], RT + 17 * K)]
        o_col = RT + 18 * K
        col = [at("colf", [P, 40], o_col), at("colb", [P, 40], o_col + 160)]
        dcol = [at("dcolf", [P, 10], o_col + 320), at("dcolb", [P, 10], o_col + 384)]
        W_U = T + 2 * PAD
        up = [at(f"up{u}", [P, W_U], RX + 4224 * u) for u in range(2)]
        wa = at("wa", [P, W_U], RX + 8448)
        wb = at("wb", [P, W_U], RX + 12672)
        pd = [at(f"pd{u}", [P, T], RX + 16896 + 4 * K * u) for u in range(2)]
        icnt = at("icnt", [P, T], RX + 16896 + 8 * K)
        wpl = at("wpl", [P, 2, 256], RX + 16896 + 12 * K)
        assert 16896 + 14 * K <= 32 * K
        XN = at("XN", [P, KT, T], RA)

        ps = [ctx.enter_context(nc.psum_tensor(f"ps{s}", [P, 2 * 512], F32)) for s in range(4)]

        def dram(name, shape):
            return nc.dram_tensor(name, shape, F32, kind="Internal").ap()

        g1 = dram("g1", [P, N2, T])
        s1 = dram("s1", [P, N2, T])
        xs = dram("xs", [D, T])
        ond = dram("ond", [KT, P, T])
        gad = dram("gad", [KT, P, T])
        mad = dram("mad", [KT, P, T])

        const_in, vec_in, feat_in, filt_in = (sem(f"{x}_in") for x in ("const", "vec", "feat", "filt"))
        x_in = [sem(f"x_in{k}") for k in range(4)]
        raw_in = [sem("raw_in0"), sem("raw_in1")]
        hi_made, split_made = sem("hi_made"), sem("split_made")
        panel_done, aux_done = sem("panel_done"), sem("aux_done")
        evac = [sem(f"evac{s}") for s in range(4)]
        act_chain, dve_chain = sem("act_chain"), sem("dve_chain")
        ended = {e: sem(f"ended_{e}") for e in ("pe", "act", "dve")}

        def slot(phase, u):
            return (J0[phase] + u) % 4

        def turn(phase, u, i=0, per=0):
            return (J0[phase] + u) // 4 + i * (per // 4)

        def barrier(eng, name, p):
            eng.drain().then_inc(ended[name], 1)
            for other in ("pe", "act", "dve"):
                if other != name:
                    eng.wait_ge(ended[other], p)

        waited = sem("waited")

        def steady(eng):
            eng.sem_inc(waited, 1)

        class NormSems:

            def __init__(self, tag, chain=True, split=True):
                self.sq, self.acc, self.r, self.rb, self.h = (sem(f"{x}_{tag}") for x in ("sq", "acc", "r", "rb", "h"))
                if chain:
                    self.var, self.r0 = sem(f"var_{tag}"), sem(f"r0_{tag}")
                if split:
                    self.hi, self.lo = sem(f"hi_{tag}"), sem(f"lo_{tag}")

        n1, n2, n3, ncx = (NormSems(t) for t in ("mix", "ffn", "x2", "ctx"))
        n4, nf1 = NormSems("fin2", split=False), NormSems("fin", chain=False, split=False)
        arg_made, sin_made, hb_zero = sem("arg_made"), sem("sin_made"), sem("hb_zero")
        hbs_made, decay_made, tap_sum = sem("hbs_made"), sem("decay_made"), sem("tap_sum")
        g1_out = [sem("g1_out0"), sem("g1_out1")]
        zpad_zero, z_used, s_made = sem("zpad_zero"), sem("z_used"), sem("s_made")
        sn_made = sem("sn_made")
        s1_out = [sem("s1_out0"), sem("s1_out1")]
        silu_c = sem("silu_c")
        mod_in = [sem(f"mod_in{m}") for m in range(4)]
        mod_used = sem("mod_used")
        spec_in = [sem("spec_in0"), sem("spec_in1")]
        spec_gm, spec_xm, spec_g, spec_y, spec_inv, spec_ev = (
            sem(f"spec_{x}") for x in ("gm", "xm", "g", "y", "inv", "ev"))
        yb_in = [sem("yb_in0"), sem("yb_in1")]
        kf_in = [sem(f"kf_in{u}") for u in range(3)]
        skip_made, y_made, y_hi, y_lo = sem("skip_made"), sem("y_made"), sem("y_hi"), sem("y_lo")
        xr_in = sem("xr_in")
        ff_hi, ff_lo = sem("ff_hi"), sem("ff_lo")
        x_spilled, rot_in, cx_in = sem("x_spilled"), sem("rot_in"), sem("cx_in")
        gate_abs, gate_ln, wup_in = sem("gate_abs"), sem("gate_ln"), sem("wup_in")
        dif_made, exp_made, qk_made = sem("dif_made"), sem("exp_made"), sem("qk_made")
        kdc_made, colexp = sem("kdc_made"), sem("colexp")
        state_made, sco_made = sem("state_made"), sem("sco_made")
        osq, osum, o_var, o_r0, o_r, o_rb, on_made = (
            sem(x) for x in ("osq", "osum", "o_var", "o_r0", "o_r", "o_rb", "on_made"))
        on_out = [sem("on_out0"), sem("on_out1")]
        ga_out = [sem("ga_out0"), sem("ga_out1")]
        on_in = [sem(f"on_in{k}") for k in range(4)]
        ga_in = sem("ga_in")
        za_hi, za_lo = sem("za_hi"), sem("za_lo")
        ma_out, ma_made = sem("ma_out"), sem("ma_made")
        ma_in = [sem(f"ma_in{k}") for k in range(2)]
        pool_in, pool_pad, pd_made, pb_hi, pb_lo = (
            sem(x) for x in ("pool_in", "pool_pad", "pd_made", "pb_hi", "pb_lo"))
        mb_made, m_hi, m_lo = sem("mb_made"), sem("m_hi"), sem("m_lo")
        xr2_in = sem("xr2_in")
        out_st = sem("out_st")

        def vcol(name, j=0):
            return vec[:, ds(VEC[name] + j, 1)]

        def cc(name, rows=P):
            w = {"idft": 64, "tneg": 16, "tmask": 16}.get(name, 128)
            return cst[0:rows, CST[name]:CST[name] + w]

        ident, ones = cc("ident"), cc("ones")

        def operand(act, a, k, t0, w):
            return act[a][:, k, t0:t0 + w] if isinstance(act, list) else act[:, a, k, t0:t0 + w]

        def chunk(t, c):
            return t[:, c * CH:(c + 1) * CH]


        def aux_at(h, a):
            return h * HA + (A0["heads"] + a)

        def evac_at(h, u):
            return h * (HJ // 4) + (turn("heads", u) + 1)

        O_ORDER = (0, 2, 3, 4, 7, 6, 1, 5)
        STATE_JOBS = ((17, 0, range(0, 4)), (18, 1, range(4, NCH)), (19, 0, range(4, NCH - 1)), (20, 1, range(1, 4)))

        def heads_pe(pe, h, free, panel_mm):
            mm = nc.tensor.matmul

            def p(u):
                return ps[slot("heads", u)]

            def begin(u):
                free("heads", u, h, HJ)

            n0 = N0["heads"]
            pe.wait_ge(wup_in, h * 16 + 16)
            for u in range(2):
                begin(u)
                for c in range(2):
                    last = mm(p(u)[:, c * 512:(c + 1) * 512], wup_h[32 * u:32 * u + 16, :],
                              LRT[32 * u:32 * u + 16, c * 512:(c + 1) * 512], start=True, stop=True)
                last.then_inc(aux_done, 1)
            begin(2)
            for u in range(2):
                last = mm(p(2)[:, u * 512:u * 512 + TC], wup_h[32 * u:32 * u + 16, :],
                          LRT[32 * u:32 * u + 16, T:T + TC], start=True, stop=True)
            last.then_inc(aux_done, 1)
            pe.wait_ge(split_made, h * HP + (n0 + 1))
            begin(3)
            panel_mm(p(3), n0 % 2, H, T, 8).then_inc(panel_done, 1)
            pe.wait_ge(split_made, h * HP + (n0 + 2))
            begin(4)
            panel_mm(p(4), (n0 + 1) % 2, H, T, 8).then_inc(aux_done, 1)
            begin(5)
            panel_mm(p(5), (n0 + 1) % 2, HC, TC, 8).then_inc(panel_done, 1)

            def rotate(u, src, ready):
                begin(u)
                pe.wait_ge(*ready)
                for c in range(2):
                    last = mm(p(u)[:, c * 512:(c + 1) * 512], cc("perm"), src[:, c * 512:(c + 1) * 512],
                              start=True, stop=True)
                last.then_inc(aux_done, 1)

            def values(u, act, tiles, t0):
                begin(u)
                for t in range(tiles):
                    q = 0
                    for k in range(KT):
                        for a, w in ((0, whi), (1, whi), (0, wlo)):
                            last = mm(p(u)[:, t * DV:(t + 1) * DV], operand(act, a, k, (t0 + t) * P, P),
                                      w[:, :, k, :], start=(q == 0), stop=(q == 23))
                            q += 1
                return last

            rotate(6, QT, (evac[slot("heads", 3)], evac_at(h, 3)))
            pe.wait_ge(split_made, h * HP + (n0 + 4))
            values(7, H, 4, 0).then_inc(aux_done, 1)
            rotate(8, KTt, (evac[slot("heads", 4)], evac_at(h, 4)))
            values(9, H, 4, 4).then_inc(aux_done, 1)
            values(10, HC, 2, 0).then_inc(panel_done, 2)
            begin(11)
            pe.wait_ge(kdc_made, h + 1)
            for dr in range(2):
                for c in range(NCC):
                    last = nc.tensor.transpose(p(11)[:, dr * 512 + c * CH:dr * 512 + (c + 1) * CH],
                                               chunk(KDC[:, dr, :], c), ident)
            last.then_inc(aux_done, 1)
            for dr in range(2):
                begin(12 + dr)
                pe.wait_ge(qk_made, h * 4 + 2 * dr + 2)
                for c in range(NCH):
                    last = nc.tensor.transpose(chunk(p(12 + dr), c), chunk(KD[dr], c), ident)
                last.then_inc(aux_done, 1)
            for dr in range(2):
                begin(14 + dr)
                for c in range(NCH):
                    last = mm(chunk(p(14 + dr), c), chunk(KD[dr], c), chunk(QD[dr], c), start=True, stop=True)
                last.then_inc(aux_done, 1)
            for u in (10, 11):
                pe.wait_ge(evac[slot("heads", u)], evac_at(h, u))
            begin(16)
            for dr in range(2):
                for c in range(NCC):
                    last = mm(p(16)[:, dr * 512 + c * DV:dr * 512 + (c + 1) * DV], KDTC[:, dr, c, :], VC[:, c, :],
                              start=True, stop=True)
            last.then_inc(aux_done, 1)
            pe.wait_ge(evac[slot("heads", 7)], evac_at(h, 7))
            pe.wait_ge(evac[slot("heads", 12)], evac_at(h, 12))
            for u, dr, chunks in STATE_JOBS:
                begin(u)
                if u == 18:
                    pe.wait_ge(evac[slot("heads", 13)], evac_at(h, 13))
                for c in chunks:
                    last = mm(p(u)[:, (c % 4) * DV:(c % 4 + 1) * DV], KDT[dr][:, c, :], V[:, c, :],
                              start=True, stop=True)
                last.then_inc(aux_done, 1)

            def projection(u, n):
                pe.wait_ge(split_made, h * HP + (n0 + n + 1))
                begin(u)
                panel_mm(p(u), (n0 + n) % 2, H, T, 8).then_inc(panel_done, 1)

            projection(21, 4)
            projection(22, 5)
            pe.wait_ge(sco_made, h + 1)
            pe.wait_ge(state_made, h + 1)
            for e in range(2):
                begin(23 + e)
                for c in range(NCH):
                    o = chunk(p(23 + e), c)
                    mm(o, V[:, c, e * P:(e + 1) * P], chunk(SCO[0], c), start=True, stop=False)
                    mm(o, SR[0][:, c, e * P:(e + 1) * P], chunk(QD[0], c), start=False, stop=False)
                    last = mm(o, SR[1][:, c, e * P:(e + 1) * P], chunk(QD[1], c), start=False, stop=True)
                last.then_inc(aux_done, 1)
            projection(25, 6)
            begin(26)
            pe.wait_ge(osum, h + 1)
            for c in range(NCH):
                last = mm(p(26)[:, c:c + 1], chunk(TT[2], c), ones[:, 0:1], start=True, stop=True)
            last.then_inc(aux_done, 1)
            projection(27, 7)
            pe.wait_ge(o_r, h + 1)
            for c in range(NCH):
                last = mm(chunk(p(26), c), nr[:, c:c + 1].to_broadcast([P, P]), ident, start=True, stop=True)
            last.then_inc(o_rb, 1)

        def heads_act(act, h, ch):
            A_ = nc.scalar.activation
            inv = 1.0 / GATE_NORM

            def p(u):
                return ps[slot("heads", u)]

            def copied(u, out_, in_, **kw):
                A_(out_, in_, ACT.Copy, **kw).then_inc(evac[slot("heads", u)], 1)

            for u, t in ((0, TT[0]), (1, TT[2])):
                act.wait_ge(aux_done, aux_at(h, u + 1))
                steady(act)
                A_(t[:, :], p(u)[:, :], ACT.Abs, bias=vcol(("b_gf", "b_gb")[u], h)).then_inc(gate_abs, 1)
                act.wait_ge(gate_abs, h * 4 + u + 1)
                ch.link(A_(t[:, :], t[:, :], ACT.Exp, scale=-1.0))
                A_(t[:, :], t[:, :], ACT.Ln, bias=1.0).then_inc(gate_ln, 1)
            act.wait_ge(aux_done, aux_at(h, 3))
            steady(act)
            for u in range(2):
                A_(KDC[:, u, :], p(2)[:, u * 512:u * 512 + TC], ACT.Abs, bias=vcol(("b_gf", "b_gb")[u], h)
                   ).then_inc(gate_abs, 1)
            act.wait_ge(gate_abs, h * 4 + 4)
            ch.link(A_(KDC[:, :, :], KDC[:, :, :], ACT.Exp, scale=-1.0))
            A_(KDC[:, :, :], KDC[:, :, :], ACT.Ln, bias=1.0).then_inc(gate_ln, 1)
            act.wait_ge(panel_done, h * HP + (N0["heads"] + 1))
            copied(3, QT[:, :], p(3)[:, :], scale=DK ** -0.5)
            act.wait_ge(aux_done, aux_at(h, 4))
            act.wait_ge(on_out[1], h * 16 + 16)
            copied(4, KTt[:, :], p(4)[:, :])
            act.wait_ge(panel_done, h * HP + (N0["heads"] + 2))
            copied(5, KC[:, :], p(5)[:, 0:TC])
            act.wait_ge(dif_made, h * 4 + 1)
            A_(TT[1][:, :], TT[0][:, :], ACT.Exp, scale=inv).then_inc(exp_made, 1)
            A_(TT[2][:, :], TT[0][:, :], ACT.Exp, scale=-inv).then_inc(exp_made, 1)
            act.wait_ge(exp_made, h * 5 + 2)
            act.wait_ge(dif_made, h * 4 + 2)
            A_(TT[0][:, :], TT[3][:, :], ACT.Exp, scale=inv).then_inc(exp_made, 1)
            act.wait_ge(exp_made, h * 5 + 3)
            A_(TT[3][:, :], TT[3][:, :], ACT.Exp, scale=-inv).then_inc(exp_made, 1)
            act.wait_ge(dif_made, h * 4 + 3)
            A_(KDC[:, :, :], KDC[:, :, :], ACT.Exp, scale=-inv).then_inc(exp_made, 1)
            act.wait_ge(dif_made, h * 4 + 4)
            for dr in range(2):
                mid, end = ((CH // 2 - 1, CH - 1), (CH // 2, 0))[dr]
                A_(col[dr][:, 10:18], BB[dr][:, mid::CH], ACT.Exp, scale=inv).then_inc(colexp, 1)
                A_(col[dr][:, 20:28], BB[dr][:, end::CH], ACT.Exp, scale=inv).then_inc(colexp, 1)
                A_(col[dr][:, 28:30], BBC[:, dr, end::CH], ACT.Exp, scale=inv).then_inc(colexp, 1)
                A_(col[dr][:, 30:40], dcol[dr][:, :], ACT.Exp, scale=inv).then_inc(colexp, 1)
            act.wait_ge(aux_done, aux_at(h, 6))
            copied(7, V[:, 0:4, :].rearrange("p c v -> p (c v)"), p(7)[:, :])
            act.wait_ge(aux_done, aux_at(h, 8))
            copied(9, V[:, 4:8, :].rearrange("p c v -> p (c v)"), p(9)[:, :])
            act.wait_ge(panel_done, h * HP + (N0["heads"] + 4))
            copied(10, VC[:, :, :].rearrange("p c v -> p (c v)"), p(10)[:, 0:2 * DV])
            act.wait_ge(aux_done, aux_at(h, 9))
            copied(11, KDTC[:, :, :, :].rearrange("p a c k -> p a (c k)"),
                   p(11)[:, :].rearrange("p (a b) -> p a b", a=2)[:, :, 0:TC])
            for dr in range(2):
                act.wait_ge(aux_done, aux_at(h, 10 + dr))
                copied(12 + dr, KDT[dr][:, :, :].rearrange("p c k -> p (c k)"), p(12 + dr)[:, :])
            for u, dr, chunks in STATE_JOBS:
                act.wait_ge(aux_done, aux_at(h, u - 2))
                for c in chunks:
                    i_ = A_(SR[dr][:, c + (1, -1)[dr], :], p(u)[:, (c % 4) * DV:(c % 4 + 1) * DV], ACT.Copy,
                            scale=col[dr][:, 30 + c:31 + c])
                i_.then_inc(evac[slot("heads", u)], 1)
            for e in range(2):
                act.wait_ge(panel_done, h * HP + (N0["heads"] + 5 + e))
                A_(SZA[e][:, :], p(21 + e)[:, :], ACT.Silu).then_inc(evac[slot("heads", 21 + e)], 1)
            for e in range(2):
                act.wait_ge(aux_done, aux_at(h, 19 + e))
                if e == 0:
                    act.wait_ge(state_made, h + 1)
                A_(TT[2 + e][:, :], p(23 + e)[:, :], ACT.Square).then_inc(osq, 1)
                copied(23 + e, OE[e][:, :], p(23 + e)[:, :])

            def gate_a(e):
                u = 25 + 2 * e
                act.wait_ge(panel_done, h * HP + (N0["heads"] + 7 + e))
                A_(SGA[e][:, :], p(u)[:, :], ACT.Sigmoid).then_inc(evac[slot("heads", u)], 1)
                act.wait_ge(evac[slot("heads", u)], evac_at(h, u))
                act.dma_start(gad[ds(h * 2 + e, 1), :, :].rearrange("k p t -> (k p) t"), SGA[e][:, :]
                              ).then_inc(ga_out[e], 16)

            gate_a(0)
            act.wait_ge(o_var, h + 1)
            ch.link(A_(nr[:, 0:8], nv[:, 0:8], ACT.Ln))
            A_(nr[:, 0:8], nr[:, 0:8], ACT.Exp, scale=-0.5).then_inc(o_r0, 1)
            gate_a(1)
            for e in range(2):
                act.wait_ge(on_made, h * 2 + e + 1)
                act.dma_start(ond[ds(h * 2 + e, 1), :, :].rearrange("k p t -> (k p) t"), OE[e][:, :]
                              ).then_inc(on_out[e], 16)

        HEAD_STEPS = 78
        HEAD_ACT_STEPS = 4

        def heads_dve(dve, h, ch):
            V_ = nc.vector

            def p(u):
                return ps[slot("heads", u)]

            def ev(u):
                return evac[slot("heads", u)]

            def by_chunk(t):
                return t.rearrange("p (c j) -> p c j", j=CH)

            def at_col(t, j):
                v = by_chunk(t)
                return v[:, :, j:j + 1].to_broadcast([P, v.shape[1], CH])

            dve.wait_ge(gate_abs, h * 4 + 1)
            V_.tensor_scalar(TT[1][:, :], p(0)[:, :], vcol("b_gf", h), 0.0, ALU.add, ALU.min).then_inc(ev(0), 1)
            dve.wait_ge(ev(0), evac_at(h, 0))
            dve.wait_ge(gate_ln, h * 3 + 1)
            ch.link(V_.tensor_tensor(TT[1][:, :], TT[1][:, :], TT[0][:, :], ALU.subtract))
            for c in range(NCH):
                ch.do(V_.tensor_tensor_scan(chunk(BB[0], c), ones, chunk(TT[1], c), 0.0, ALU.mult, ALU.add))
            dve.wait_ge(gate_abs, h * 4 + 2)
            V_.tensor_scalar(TT[3][:, :], p(1)[:, :], vcol("b_gb", h), 0.0, ALU.add, ALU.min).then_inc(ev(1), 1)
            dve.wait_ge(ev(1), evac_at(h, 1))
            dve.wait_ge(gate_ln, h * 3 + 2)
            ch.link(V_.tensor_tensor(TT[3][:, :], TT[3][:, :], TT[2][:, :], ALU.subtract))
            for c in range(NCH):
                ch.do(V_.tensor_tensor_scan(chunk(TT[2], c), ones, chunk(TT[3], c), 0.0, ALU.mult, ALU.add))
            ch.wait()
            ch.link(V_.tensor_tensor(TT[3][:, :], TT[3][:, :], TT[2][:, :], ALU.subtract))
            ch.link(V_.tensor_tensor(by_chunk(BB[1][:, :]), by_chunk(TT[3][:, :]), at_col(TT[2][:, :], CH - 1), ALU.add))
            dve.wait_ge(gate_abs, h * 4 + 4)
            for u in range(2):
                i_ = V_.tensor_scalar(BBC[:, u, :], p(2)[:, u * 512:u * 512 + TC], vcol(("b_gf", "b_gb")[u], h), 0.0,
                                      ALU.add, ALU.min)
                if u:
                    i_.then_inc(ev(2), 1)
            dve.wait_ge(ev(2), evac_at(h, 2))
            dve.wait_ge(gate_ln, h * 3 + 3)
            ch.link(V_.tensor_tensor(BBC[:, :, :], BBC[:, :, :], KDC[:, :, :], ALU.subtract))
            for u in range(2):
                for c in range(NCC):
                    ch.do(V_.tensor_tensor_scan(chunk(KDC[:, u, :], c), ones, chunk(BBC[:, u, :], c), 0.0,
                                                ALU.mult, ALU.add))
            ch.wait()
            ch.do(V_.tensor_copy(BBC[:, 0, :], KDC[:, 0, :]))
            ch.link(V_.tensor_tensor(BBC[:, 1, :], BBC[:, 1, :], KDC[:, 1, :], ALU.subtract))
            ch.link(V_.tensor_tensor(by_chunk(BBC[:, 1, :]), by_chunk(BBC[:, 1, :]), at_col(KDC[:, 1, :], CH - 1), ALU.add))
            mids = (CH // 2 - 1, CH // 2)
            ends = (CH - 1, 0)
            for dr, t in ((0, TT[0]), (1, TT[3])):
                ch.link(V_.tensor_tensor(by_chunk(t[:, :]), by_chunk(BB[dr][:, :]), at_col(BB[dr][:, :], mids[dr]),
                                         ALU.subtract))
                V_.tensor_scalar(t[:, :], t[:, :], CLAMP, -CLAMP, ALU.min, ALU.max).then_inc(dif_made, 1)
            for dr in range(2):
                ch.do(V_.tensor_tensor(by_chunk(KDC[:, dr, :]), by_chunk(BBC[:, dr, :]), at_col(BBC[:, dr, :], mids[dr]),
                                       ALU.subtract))
            ch.wait()
            V_.tensor_scalar(KDC[:, :, :], KDC[:, :, :], CLAMP, -CLAMP, ALU.min, ALU.max).then_inc(dif_made, 1)
            for dr in range(2):
                ch.do(V_.tensor_tensor(dcol[dr][:, 0:8], BB[dr][:, ends[dr]::CH], BB[dr][:, mids[dr]::CH], ALU.subtract))
                i_ = V_.tensor_tensor(dcol[dr][:, 8:10], BBC[:, dr, ends[dr]::CH], BBC[:, dr, mids[dr]::CH], ALU.subtract)
                if dr == 0:
                    ch.do(i_)
                else:
                    i_.then_inc(dif_made, 1)
            def rotate(u, t, e, a):
                tmp = ROT[e]
                dve.wait_ge(ga_out[e], h * 16 + 16)
                dve.wait_ge(aux_done, aux_at(h, a))
                V_.tensor_tensor(tmp[:, :], p(u)[:, :], SIN[:, :], ALU.mult).then_inc(ev(u), 1)
                ch.link(V_.tensor_tensor(t[:, :], t[:, :], COS[:, :], ALU.mult))
                dve.wait_ge(ev(u), evac_at(h, u))
                ch.link(V_.tensor_tensor(t[:, :], t[:, :], tmp[:, :], ALU.add))

            dve.wait_ge(exp_made, h * 5 + 5)
            dve.wait_ge(ev(5), evac_at(h, 5))
            ch.link(V_.tensor_tensor(KDC[:, 0, :], KDC[:, 0, :], KC[:, :], ALU.mult))
            V_.tensor_tensor(KDC[:, 1, :], KDC[:, 1, :], KC[:, :], ALU.mult).then_inc(kdc_made, 1)
            rotate(6, QT, 0, 5)
            V_.tensor_tensor(QD[0][:, :], QT[:, :], TT[1][:, :], ALU.mult).then_inc(qk_made, 1)
            rotate(8, KTt, 1, 7)
            dve.wait_ge(on_out[0], h * 16 + 16)
            V_.tensor_tensor(KD[0][:, :], KTt[:, :], TT[2][:, :], ALU.mult).then_inc(qk_made, 1)
            dve.wait_ge(qk_made, h * 4 + 2)
            V_.tensor_tensor(QD[1][:, :], QT[:, :], TT[0][:, :], ALU.mult).then_inc(qk_made, 1)
            V_.tensor_tensor(KD[1][:, :], KTt[:, :], TT[3][:, :], ALU.mult).then_inc(qk_made, 1)
            masks = [cc(m).unsqueeze(1).to_broadcast([P, NCH, CH]) for m in ("mask_f", "mask_b")]
            dve.wait_ge(qk_made, h * 4 + 4)
            for dr in range(2):
                dve.wait_ge(aux_done, aux_at(h, 12 + dr))
                V_.tensor_tensor(by_chunk(SCO[dr][:, :]), by_chunk(p(14 + dr)[:, :]), masks[dr], ALU.mult
                                 ).then_inc(ev(14 + dr), 1)
                dve.wait_ge(ev(14 + dr), evac_at(h, 14 + dr))
            V_.tensor_tensor(SCO[0][:, :], SCO[0][:, :], SCO[1][:, :], ALU.add).then_inc(sco_made, 1)
            dve.wait_ge(colexp, h * 8 + 8)
            dve.wait_ge(aux_done, aux_at(h, 14))
            for dr in range(2):
                S_, cl, tmp = SS[dr], col[dr], TT[2 + dr][:, 0:DV]
                for q, c in enumerate(((0, 1), (1, 0))[dr]):
                    U = p(16)[:, dr * 512 + c * DV:dr * 512 + (c + 1) * DV]
                    if q == 0:
                        ch.link(V_.tensor_scalar(S_[:, :], U, cl[:, 38 + c:39 + c], None, ALU.mult))
                    else:
                        i_ = V_.tensor_scalar(tmp, U, cl[:, 38 + c:39 + c], None, ALU.mult)
                        if dr:
                            i_.then_inc(ev(16), 1)
                            dve.wait_ge(ev(16), evac_at(h, 16))
                        else:
                            ch.link(i_)
                        ch.link(V_.scalar_tensor_tensor(out=S_[:, :], in0=S_[:, :], scalar=cl[:, 28 + c:29 + c], in1=tmp,
                                                        op0=ALU.mult, op1=ALU.add))
            for q in range(NCH):
                for dr in range(2):
                    c = (q, NCH - 1 - q)[dr]
                    if q:
                        ch.wait(1)
                    i_ = V_.tensor_scalar(SR[dr][:, c, :], SS[dr][:, :], col[dr][:, 10 + c:11 + c], None, ALU.mult)
                    if q == NCH - 1 and dr == 1:
                        i_.then_inc(state_made, 1)
                    else:
                        ch.do(i_)
                if q == NCH - 1:
                    break
                for dr in range(2):
                    c = (q, NCH - 1 - q)[dr]
                    for u, d_, chunks in STATE_JOBS:
                        if d_ == dr and c in chunks:
                            dve.wait_ge(ev(u), evac_at(h, u))
                    ch.wait(1)
                    ch.do(V_.scalar_tensor_tensor(out=SS[dr][:, :], in0=SS[dr][:, :], scalar=col[dr][:, 20 + c:21 + c],
                                                  in1=SR[dr][:, c + (1, -1)[dr], :], op0=ALU.mult, op1=ALU.add))
            ch.wait()
            dve.wait_ge(osq, h * 2 + 2)
            V_.tensor_tensor(TT[2][:, :], TT[2][:, :], TT[3][:, :], ALU.add).then_inc(osum, 1)
            dve.wait_ge(aux_done, aux_at(h, 21))
            v, r, q = nv[:, 0:8], nr[:, 0:8], nq[:, 0:8]
            V_.tensor_scalar(v, p(26)[:, 0:8], 1.0 / DV, EPS, ALU.mult, ALU.add).then_inc(o_var, 1)
            dve.wait_ge(o_r0, h + 1)
            ch.link(V_.tensor_tensor(q, r, r, ALU.mult))
            ch.link(V_.tensor_tensor(q, q, v, ALU.mult))
            ch.link(V_.tensor_scalar(q, q, -0.5, 1.5, ALU.mult, ALU.add))
            V_.tensor_tensor(r, r, q, ALU.mult).then_inc(o_r, 1)
            dve.wait_ge(o_rb, h + 1)
            for e in range(2):
                dve.wait_ge(ev(23 + e), evac_at(h, 23 + e))
                i_ = V_.scalar_tensor_tensor(out=OE[e][:, :], in0=OE[e][:, :],
                                             scalar=vec[:, VEC["gla_g"] + e:VEC["gla_g"] + e + 1],
                                             in1=p(26)[:, :], op0=ALU.mult, op1=ALU.mult)
                if e:
                    i_.then_inc(ev(26), 1)
                    dve.wait_ge(ev(26), evac_at(h, 26))
                else:
                    ch.link(i_)
                dve.wait_ge(ev(21 + e), evac_at(h, 21 + e))
                V_.tensor_tensor(OE[e][:, :], OE[e][:, :], SZA[e][:, :], ALU.mult).then_inc(on_made, 1)

        block = ctx.enter_context(nc.Block())

        @block.sync
        def _(sp):
            for t, n in ((feat, "feat"), (fw1, "fw1")):
                sp.dma_start(t[:, :], d[n]).then_inc(feat_in, 16)
            sp.dma_start(vec[:, :], d["vec"]).then_inc(vec_in, 16)
            xv = d["xT"].rearrange("(k p) t -> p k t", p=P)
            for k in range(4):
                sp.dma_start(X[:, 2 * k:2 * k + 2, :], xv[:, 2 * k:2 * k + 2, :]).then_inc(x_in[k], 16)
            sp.dma_start(cst[:, :], d["cst"]).then_inc(const_in, 16)
            for t, n in ((fw2, "fw2"), (fw3, "fw3")):
                sp.dma_start(t[:, :], d[n]).then_inc(filt_in, 16)

            def panel(n, s):
                sp.dma_start(wraw[:, s, :, :], d["panels"][ds(n, 1), :, :].rearrange("a p (k m) -> (a p) k m", k=8)
                             ).then_inc(raw_in[s], 16)

            def panels(lo, hi):
                assert lo >= 2 and (hi - lo) % 2 == 0
                with sp.Fori(0, (hi - lo) // 2) as i:
                    for u in range(2):
                        n = lo + u + i * 2
                        sp.wait_ge(split_made, n - 1)
                        panel(n, (lo + u) % 2)

            def modp(f, m):
                sp.dma_start(mw[m][:, :], d["modp"][ds(f, 1), :, :].rearrange("a p k -> (a p) k")).then_inc(mod_in[m], 16)

            for u in range(2):
                panel(u, u)
            sp.wait_ge(n1.h, KT)
            for t, n in ((wtap, "wtap"), (dec, "dec")):
                sp.dma_start(t[:, :], d[n]).then_inc(filt_in, 16)
            sp.dma_start(crep[:, :], d["cvec"].to_broadcast([P, 2 * D])).then_inc(filt_in, 16)
            for m in range(4):
                modp(m, m)
            panels(2, 6)
            with sp.Fori(0, 5) as i:
                for u in range(2):
                    sp.wait_ge(split_made, i * 2 + (u + 5))
                    panel(i * 2 + (u + 6), u)
                    for j in range(2):
                        m = 2 * u + j
                        sp.wait_ge(mod_used, i * 4 + (m + 1))
                        modp(i * 4 + (m + 4), m)
            panels(16, 24)
            with sp.Fori(0, N2 // 2) as i:
                for u in range(2):
                    s = slot("sfwd", 2 + u)
                    sp.wait_ge(evac[s], turn("sfwd", 2 + u, i, 4) + 1)
                    sp.dma_start(s1[:, ds(i * 2 + u, 1), :], sa[u][:, :].unsqueeze(1)).then_inc(s1_out[u], 16)
            for u in range(2):
                sp.wait_ge(g1_out[u], 16 * (N2 // 2 + 1))
                sp.wait_ge(s1_out[u], 16 * (N2 // 2 + 1))
            sp.wait_ge(ended["pe"], 1)
            sp.wait_ge(ended["act"], 1)
            g1r = g1.rearrange("p n t -> (p n) t")
            s1r = s1.rearrange("p n t -> (p n) t")

            def spec_load(g):
                u = g % 2
                for t, src in ((bg[u][:, :], g1r[g * P:(g + 1) * P, :]), (bs[u][:, :], s1r[g * P:(g + 1) * P, :])):
                    sp.dma_start(t, src).then_inc(spec_in[u], 16)

            def kfft_load(g):
                sp.dma_start(kf[g % 3][:, :, :].rearrange("p a m -> p (a m)"), d["kfft"][g, :, :]).then_inc(kf_in[g % 3], 16)

            for g in range(GROUPS):
                if g >= 2:
                    sp.wait_ge(spec_xm, 2 * g - 2)
                spec_load(g)
                if g >= 3:
                    sp.wait_ge(spec_inv, 2 * g - 4)
                kfft_load(g)
            sp.wait_ge(ended["pe"], 2)
            sp.wait_ge(ended["act"], 2)
            sp.wait_ge(ended["dve"], 2)
            sp.dma_start(X[:, :, :], xv).then_inc(xr_in, 16)
            panels(24, N0["up1"])
            sp.wait_ge(panel_done, N0["up0"] + 1)
            cxv = d["ctxT"].rearrange("(k p) t -> p k t", p=P)
            for u in range(2):
                sp.dma_start(CX[u][:, :, :], cxv[:, 4 * u:4 * u + 4, :]).then_inc(cx_in, 16)
            panels(N0["up1"], N0["lr"])
            sp.wait_ge(aux_done, A0["mix"] + 32)
            sp.dma_start(wup_h[:, :], d["wup"][:, 0:DK]).then_inc(wup_in, 16)
            n = N0["lr"]
            for q in range(2):
                sp.wait_ge(split_made, n + q - 1)
                panel(n + q, (n + q) % 2)
            sp.wait_ge(panel_done, n)
            sp.dma_start(COS[:, :], d["cos"]).then_inc(rot_in, 16)
            n = N0["heads"] + 1
            xsv = xs.rearrange("(k p) t -> p k t", p=P)
            for u in range(HP):
                sp.wait_ge(split_made, n + u - 1)
                panel(n + u, (n + u) % 2)
                if u == 1:
                    sp.wait_ge(nf1.h, KT)
                    sp.dma_start(xsv, X[:, :, :]).then_inc(x_spilled, 16)
                if u == 3:
                    sp.wait_ge(x_spilled, 16)
                    sp.dma_start(SIN[:, :], d["sin"]).then_inc(rot_in, 16)
            with sp.Fori(1, HEADS) as h:
                sp.wait_ge(aux_done, h * HA + (A0["heads"] + 3 - HA))
                sp.dma_start(wup_h[:, :], d["wup"][:, ds(h * DK, DK)]).then_inc(wup_in, 16)
                for u in range(HP):
                    sp.wait_ge(split_made, h * HP + (n + u - 1))
                    panel(h * HP + (n + u), (n + u) % 2)
            n += HP * HEADS
            sp.wait_ge(split_made, n - 1)
            panel(n, n % 2)
            sp.wait_ge(aux_done, aux_at(HEADS, 0))
            sp.wait_ge(on_out[0], 16 * 4)
            sp.wait_ge(on_out[1], 16 * 4)
            for q in range(4):
                sp.dma_start(TT[q][:, :], ond[O_ORDER[q], :, :]).then_inc(on_in[q], 16)
            panels(n + 1, NPANELS)

        @block.gpsimd
        def _(pool):
            for s in range(2):
                pool.wait_ge(raw_in[s], 16)
                nc.gpsimd.tensor_copy(whi[:, s, :, :], wraw[:, s, :, :]).then_inc(hi_made, 1)
                pool.wait_ge(hi_made, s + 1)
                nc.gpsimd.tensor_tensor(wlo[:, s, :, :], wraw[:, s, :, :], whi[:, s, :, :].bitcast(F32), ALU.subtract
                                        ).then_inc(split_made, 1)

            def rest(pairs_lo, pairs_hi):
                with pool.Fori(pairs_lo, pairs_hi) as i:
                    for s in range(2):
                        pool.wait_ge(raw_in[s], i * 16 + 16)
                        pool.wait_ge(panel_done, i * 2 + s - 1)
                        steady(pool)
                        nc.gpsimd.tensor_copy(whi[:, s, :, :], wraw[:, s, :, :]).then_inc(hi_made, 1)
                        pool.wait_ge(hi_made, i * 2 + s + 1)
                        nc.gpsimd.tensor_tensor(wlo[:, s, :, :], wraw[:, s, :, :], whi[:, s, :, :].bitcast(F32),
                                                ALU.subtract).then_inc(split_made, 1)

            rest(1, NPANELS // 2)
            if NPANELS % 2:
                n = NPANELS - 1
                pool.wait_ge(raw_in[0], (n // 2 + 1) * 16)
                pool.wait_ge(panel_done, n - 1)
                nc.gpsimd.tensor_copy(whi[:, 0, :, :], wraw[:, 0, :, :]).then_inc(hi_made, 1)
                pool.wait_ge(hi_made, n + 1)
                nc.gpsimd.tensor_tensor(wlo[:, 0, :, :], wraw[:, 0, :, :], whi[:, 0, :, :].bitcast(F32), ALU.subtract
                                        ).then_inc(split_made, 1)

        @block.tensor
        def _(pe):
            mm = nc.tensor.matmul

            def free(phase, u, i=0, per=0):
                q = turn(phase, u, i, per)
                if not (isinstance(q, int) and q == 0):
                    pe.wait_ge(evac[slot(phase, u)], q)

            def panel_mm(p, ws, act, width, nk, ready=None, order=range(KT)):
                last = None
                step = min(512, width)
                for q, k in enumerate(order[:nk]):
                    if ready is not None:
                        pe.wait_ge(ready[0], ready[1] + q + 1)
                    for w, a in ((whi, 0), (whi, 1), (wlo, 0)):
                        for c in range(width // step):
                            last = mm(p[:, c * step:(c + 1) * step], w[:, ws, k, :],
                                      operand(act, a, k, c * step, step),
start=(q == 0 and w is whi and a == 0), stop=(q == nk - 1 and w is wlo))
                return last

            def panel_jobs(phase, trips, act, nk=8, ready=None, per=4, order=range(KT)):
                n0 = N0[phase]
                with pe.Fori(0, trips) as i:
                    for u in range(per):
                        pe.wait_ge(split_made, i * per + (n0 + u + 1))
                        free(phase, u, i, per)
                        panel_mm(ps[slot(phase, u)], (n0 + u) % 2, act, T, nk, ready, order).then_inc(panel_done, 1)

            def norm_sums(phase, *accs, width=T):
                free(phase, 0)
                j = 0
                for acc, n, full in accs:
                    pe.wait_ge(n.acc, full)
                    for c in range(width // P):
                        last = mm(ps[slot(phase, 0)][:, j:j + 1], acc[:, c * P:(c + 1) * P], ones[:, 0:1],
                                  start=True, stop=True)
                        j += 1
                last.then_inc(aux_done, 1)

            def norm_spread(phase, n, r, width=T):
                pe.wait_ge(n.r, 1)
                for c in range(width // P):
                    last = mm(ps[slot(phase, 0)][:, c * P:(c + 1) * P], r[:, c:c + 1].to_broadcast([P, P]), ident,
                              start=True, stop=True)
                last.then_inc(n.rb, 1)

            def mlp(phase, u, w, src, ready):
                free(phase, u)
                pe.wait_ge(*ready)
                for c in range(2):
                    last = mm(ps[slot(phase, u)][:, c * 512:(c + 1) * 512], w[:, :], src[:, c * 512:(c + 1) * 512],
                              start=True, stop=True)
                last.then_inc(aux_done, 1)

            mlp("mlp0", 0, fw1, feat, (feat_in, 32))
            pe.wait_ge(const_in, 16)
            norm_sums("norm1", (TT[2], n1, KT + 2))
            norm_spread("norm1", n1, nr)

            def project(phase, u, ready=None):
                n = N0[phase] + u
                pe.wait_ge(split_made, n + 1)
                free(phase, u)
                panel_mm(ps[slot(phase, u)], n % 2, H, T, 8, ready).then_inc(panel_done, 1)

            project("zin0", 0, (n1.lo, 0))
            pe.wait_ge(filt_in, 80)
            mlp("mlp1", 0, fw2, fh, (sin_made, 1))
            project("zin1", 0)
            mlp("mlp2", 0, fw3, fh, (sin_made, 2))
            for u in range(2):
                project("zin2", u)
            panel_jobs("zin3", 3, H)
            with pe.Fori(0, 2) as i:
                for q in range(4):
                    o, g = 5 * q, i * 4 + q

                    def begin(u):
                        free("mix", o + u, i, 20)
                        return ps[slot("mix", o + u)]

                    pe.wait_ge(split_made, g + (N0["mix"] + 1))
                    panel_mm(begin(0), (N0["mix"] + q) % 2, H, T, 8).then_inc(panel_done, 1)
                    for u in range(2):
                        p = begin(1 + u)
                        pe.wait_ge(hbs_made, g * 2 + (u + 1))
                        for c in range(2):
                            last = mm(p[:, c * 512:(c + 1) * 512], hbs[u][:, :], wtap[:, c * 512:(c + 1) * 512],
                                      start=True, stop=True)
                        last.then_inc(aux_done, 1)
                    for u in range(2):
                        p = begin(3 + u)
                        pe.wait_ge(evac[slot("mix", o + 1 + u)], turn("mix", o + 1 + u, i, 20) + 1)
                        for c in range(2):
                            last = mm(p[:, c * 512:(c + 1) * 512], cc("dft_g"), tap[u][:, c * 512:(c + 1) * 512],
                                      start=True, stop=True)
                        last.then_inc(aux_done, 1)
            with pe.Fori(0, N2 // 2) as i:
                for u in range(2):
                    free("sfwd", u, i, 4)
                    pe.wait_ge(sn_made, i * 2 + u + 1)
                    steady(pe)
                    for e in range(KT):
                        last = nc.tensor.transpose(ps[slot("sfwd", u)][0:HALF, e * P:(e + 1) * P], sn[u][:, e, :], ident)
                    last.then_inc(aux_done, 1)
                for u in range(2):
                    free("sfwd", 2 + u, i, 4)
                    pe.wait_ge(evac[slot("sfwd", u)], turn("sfwd", u, i, 4) + 1)
                    for c in range(2):
                        last = mm(ps[slot("sfwd", 2 + u)][:, c * 512:(c + 1) * 512], cc("dft_s", HALF),
                                  st_[u][:, c * 512:(c + 1) * 512], start=True, stop=True)
                    last.then_inc(aux_done, 1)
            free("tapnorm", 0)
            pe.wait_ge(tap_sum, N2)
            for e in range(KT):
                last = mm(ps[slot("tapnorm", 0)][:, e:e + 1], gacc[:, e * P:(e + 1) * P], ones[:, 0:1],
                          start=True, stop=True)
            last.then_inc(aux_done, 1)
            barrier(pe, "pe", 1)
            def bank(c, b):
                s = 2 * c + b // 2
                return ps[s][:, (b % 2) * 512:(b % 2) * 512 + 512]

            def inverse(n):
                g, c = n // 2, n % 2
                if n >= 2:
                    pe.wait_ge(spec_ev, n - 1)
                for q, (m, src) in enumerate(((4, ya), (1, yb))):
                    pe.wait_ge(spec_y, 2 * n + q + 1)
                    last = mm(bank(c, 3), kf[g % 3][:, m, :], src[c][:, :], start=(q == 0), stop=(q == 1))
                last.then_inc(spec_inv, 1)

            for n in range(2 * GROUPS):
                g, c = n // 2, n % 2
                u = g % 2
                if c == 0:
                    pe.wait_ge(spec_in[u], 32 * (g // 2 + 1))
                    pe.wait_ge(kf_in[g % 3], 16 * (g // 3 + 1))
                if n >= 2:
                    pe.wait_ge(spec_g, 2 * n - 2)
                for m, b in ((2, 1), (3, 2)):
                    mm(bank(c, b), kf[g % 3][:, m, :], bg[u][:, c * 512:(c + 1) * 512], start=True, stop=True
                       ).then_inc(spec_gm, 1)
                mm(bank(c, 0), kf[g % 3][:, 0, :], bs[u][:, c * 512:(c + 1) * 512], start=True, stop=True
                   ).then_inc(spec_xm, 1)
                if n:
                    inverse(n - 1)
            inverse(2 * GROUPS - 1)
            barrier(pe, "pe", 2)
            for u in range(2):
                pe.wait_ge(yb_in[u], 16 * GROUPS)
            for e in range(KT):
                free("inv", e)
                for m in range(N2):
                    last = mm(ps[slot("inv", e)][:, m * HALF:(m + 1) * HALF], YB[:, m, e * P:(e + 1) * P], cc("idft"),
                              start=True, stop=True)
                last.then_inc(aux_done, 1)
            panel_jobs("wout", 2, A, ready=(y_lo, 0))
            norm_sums("norm2", (TT[2], n2, KT + 2))
            norm_spread("norm2", n2, nr)
            f0 = 0
            for p, nf in enumerate(FPARTS):
                for u, (up_, trips) in enumerate(UPS[p]):
                    panel_jobs(up_, trips, H, ready=(n2.lo, 0))
                    if len(UPS[p]) > 1:
                        if u == 0:
                            norm_sums("normc", (cxacc, ncx, KT + 2), width=TC)
                        else:
                            free("normcb", 0)
                            norm_spread("normcb", ncx, cr, TC)
                panel_jobs(f"down{p}", 2, A, nk=nf, ready=(ff_lo, f0))
                f0 += nf
            norm_sums("normf", (TT[2], nf1, KT + 1), (TT[3], n3, KT + 1))
            free("norm3", 0)
            norm_spread("norm3", n3, nr[:, 8:16])
            norm_spread("normf", nf1, nr[:, 0:8])
            pe.wait_ge(split_made, N0["lr"] + 1)
            free("lr", 0)
            ws = N0["lr"] % 2
            panel_mm(ps[slot("lr", 0)], ws, H, T, 8, (n3.lo, 0)).then_inc(aux_done, 1)
            free("lr", 1)
            pe.wait_ge(ncx.lo, KT)
            panel_mm(ps[slot("lr", 1)], ws, HC, TC, 8).then_inc(panel_done, 1)
            for u in range(2):
                pe.wait_ge(evac[slot("lr", u)], turn("lr", u) + 1)
            with pe.Fori(0, HEADS) as h:
                heads_pe(pe, h, free, panel_mm)
            panel_jobs("mixa", 2, A, ready=(za_lo, 0), order=O_ORDER)
            for g in range(4):
                for u in range(4):
                    n = N0["pool"] + 4 * g + u
                    pe.wait_ge(split_made, n + 1)
                    free("pool", 6 * g + u)
                    panel_mm(ps[slot("pool", 6 * g + u)], n % 2, H, T, 8).then_inc(panel_done, 1)
                pe.wait_ge(pool_in, 32 * (g + 1))
                for m in range(2):
                    free("pool", 6 * g + 4 + m)
                    for k in range(2):
                        pe.wait_ge(pd_made, 2 * g + k + 1)
                        for c in range(2):
                            last = mm(ps[slot("pool", 6 * g + 4 + m)][:, c * 512:(c + 1) * 512],
                                      wpl[:, k, m * P:(m + 1) * P], pd[k][:, c * 512:(c + 1) * 512],
                                      start=(k == 0), stop=(k == 1))
                    last.then_inc(aux_done, 1)
            panel_jobs("gb", 2, H)
            panel_jobs("mixb", 2, A, ready=(pb_lo, 0))
            panel_jobs("wout2", 2, H, ready=(m_lo, 0))
            norm_sums("norm4", (TT[2], n4, KT + 2))
            norm_spread("norm4", n4, nr)

        @block.scalar
        def _(act):
            A_ = nc.scalar.activation
            ch = Steps(act, act_chain)

            def square(n, src, k, ring=TT):
                act.wait_ge(n.acc, k + 1)
                A_(ring[k % 2][:, :], src, ACT.Square).then_inc(n.sq, 1)

            def rsqrt(n, w=8, v=nv, r=nr):
                act.wait_ge(n.var, 1)
                ch.link(A_(r[:, 0:w], v[:, 0:w], ACT.Ln))
                A_(r[:, 0:w], r[:, 0:w], ACT.Exp, scale=-0.5).then_inc(n.r0, 1)

            def norm_hi(n, hi, shift=None, ring=TT):
                for k in range(KT):
                    act.wait_ge(n.h, k + 1)
                    if shift is None:
                        A_(hi(k), ring[k % 2][:, :], ACT.Copy).then_inc(n.hi, 1)
                    else:
                        A_(hi(k), ring[k % 2][:, :], ACT.Identity, bias=shift(k)).then_inc(n.hi, 1)

            def h_hi(k):
                return H[:, 0, k, :]

            for k in range(KT):
                act.wait_ge(x_in[k // 2], 16)
                square(n1, X[:, k, :], k)
            rsqrt(n1)
            norm_hi(n1, h_hi)

            def sine(l):
                act.wait_ge(arg_made, l + 1)
                if l:
                    act.wait_ge(aux_done, A0["mlp1"] + 1)
                A_(fh[:, :], fu[:, :], ACT.Sin).then_inc(sin_made, 1)

            def z_tile(n, phase, u, f):
                s = slot(phase, u)
                act.wait_ge(panel_done, n + 1)
                act.wait_ge(z_used, n + 1)
                A_(zp[n % 2][:, 1:T + 1], ps[s][:, :], ACT.Identity, bias=vcol("b_in", f)).then_inc(evac[s], 1)

            sine(0)
            act.wait_ge(filt_in, 80)
            ch.link(A_(dec[:, :], dec[:, :], ACT.Abs))
            for u in range(2):
                act.sem_inc(g1_out[u], 16)
                act.sem_inc(s1_out[u], 16)
            act.wait_ge(zpad_zero, 1)
            z_tile(0, "zin0", 0, 8)
            sine(1)
            z_tile(1, "zin1", 0, 16)
            act.wait_ge(arg_made, 3)
            ch.link(A_(hb[:, :, :].rearrange("p a b -> p (a b)"), fu[:, :], ACT.Sin))
            A_(crep[:, :], crep[:, :], ACT.Silu).then_inc(silu_c, 1)
            for u in range(2):
                z_tile(2 + u, "zin2", u, 9 + 8 * u)
            with act.Fori(0, 3) as i:
                for u in range(4):
                    n0, s = N0["zin3"] + u, slot("zin3", u)
                    act.wait_ge(panel_done, i * 4 + (n0 + 1))
                    act.wait_ge(z_used, i * 4 + (n0 + 1))
                    steady(act)
                    A_(zp[u % 2][:, 1:T + 1], ps[s][:, :], ACT.Identity,
                       bias=vcol("b_in", i * 2 + (10 + 8 * (u % 2) + u // 2))).then_inc(evac[s], 1)

            def decays(n2, u):
                for r in (0, HALF):
                    i_ = A_(hbs[u][r:r + HALF, r:r + HALF], hb[r:r + HALF, ds(n2, 1), :].rearrange("p a b -> p (a b)"),
                            ACT.Copy)
                i_.then_inc(hbs_made, 1)
                A_(tap[u][:, :], dec[:, :], ACT.Exp, scale=cst[:, ds(n2 + CST["tneg"], 1)],
                   bias=cst[:, ds(n2 + CST["tmask"], 1)]).then_inc(decay_made, 1)

            act.wait_ge(const_in, 16)
            act.wait_ge(hb_zero, 1)
            act.wait_ge(mod_used, 24)
            for u in range(2):
                decays(u, u)

            def mixed(i, steps, tail):
                for q in steps:
                    o, g = 5 * q, i * 4 + q
                    act.wait_ge(panel_done, g + (N0["mix"] + 1))
                    act.wait_ge(z_used, g + (N0["mix"] + 1))
                    steady(act)
                    A_(zp[q % 2][:, 1:T + 1], ps[slot("mix", o)][:, :], ACT.Identity, bias=vcol("b_in", g)
                       ).then_inc(evac[slot("mix", o)], 1)
                    for u in range(2):
                        s = slot("mix", o + 3 + u)
                        act.wait_ge(aux_done, i * 16 + (A0["mix"] + 4 * q + 3 + u))
                        act.wait_ge(g1_out[u], g * 16 + 16)
                        A_(gsp[u][:, :], ps[s][:, :], ACT.Copy).then_inc(evac[s], 1)
                        act.wait_ge(evac[s], turn("mix", o + 3 + u, i, 20) + 1)
                        act.dma_start(g1[:, ds(g * 2 + u, 1), :], gsp[u][:, :].unsqueeze(1)).then_inc(g1_out[u], 16)
                        if q not in tail:
                            act.wait_ge(tap_sum, g * 2 + (u + 1))
                            steady(act)
                            decays(g * 2 + (u + 2), u)

            mixed(0, range(4), ())
            mixed(1, range(4), (3,))
            for u in range(2):
                act.wait_ge(g1_out[u], 16 * (N2 // 2 + 1))
            act.wait_ge(s_made, KT)
            Sv = S[:, :, :].rearrange("p k (a b) -> p k a b", b=N2)

            def gather(n, u):
                A_(sn[u][:, :, :], Sv[:, :, :, ds(n, 1)].rearrange("p k a b -> p k (a b)"), ACT.Copy
                   ).then_inc(sn_made, 1)

            def transposed(i):
                for u in range(2):
                    act.wait_ge(aux_done, i * 4 + (A0["sfwd"] + 1 + u))
                    A_(st_[u][:, :], ps[slot("sfwd", u)][0:HALF, :], ACT.Copy).then_inc(evac[slot("sfwd", u)], 1)

            gather(0, 0)
            gather(1, 1)
            with act.Fori(0, N2 // 2 - 1) as i:
                transposed(i)
                for u in range(2):
                    gather(i * 2 + u + 2, u)
            transposed(N2 // 2 - 1)
            barrier(act, "act", 1)

            def spec_inverse(n):
                c = n % 2
                act.wait_ge(spec_inv, n + 1)
                if n >= 2:
                    act.wait_ge(yb_in[c], 16 * (n // 2))
                A_(yi[c][:, :], ps[2 * c + 1][:, 512:1024], ACT.Copy).then_inc(spec_ev, 1)
                act.wait_ge(spec_ev, n + 1)
                act.dma_start(YB[8 * (n // 2):8 * (n // 2) + 8, :, 512 * c:512 * c + 512], yi[c][:, :]
                              ).then_inc(yb_in[c], 16)

            for n in range(2 * GROUPS):
                c = n % 2
                if n >= 2:
                    act.wait_ge(spec_y, 2 * n - 2)
                act.wait_ge(spec_gm, 2 * n + 1)
                A_(ga[c][:, :], ps[2 * c][:, 512:1024], ACT.Copy).then_inc(spec_g, 1)
                act.wait_ge(spec_gm, 2 * n + 2)
                A_(gb[c][:, :], ps[2 * c + 1][:, 0:512], ACT.Copy).then_inc(spec_g, 1)
                if n:
                    spec_inverse(n - 1)
            spec_inverse(2 * GROUPS - 1)
            barrier(act, "act", 2)

            def y_hi_of(e):
                act.wait_ge(y_made, e + 1)
                A_(A[:, 0, e, :], TT[2 + e % 2][:, :], ACT.Copy).then_inc(y_hi, 1)

            for e in range(KT):
                if e >= 2:
                    act.wait_ge(evac[slot("inv", e - 2)], turn("inv", e - 2) + 1)
                A_(TT[e % 2][:, :], S[:, e, :], ACT.Copy, scale=vcol("skip", e)).then_inc(skip_made, 1)
                if e:
                    y_hi_of(e - 1)
            y_hi_of(KT - 1)

            def residual_squares(ph, n, src):
                with act.Fori(0, 2) as i:
                    for u in range(4):
                        e = i * 4 + u
                        act.wait_ge(evac[slot(ph, u)], turn(ph, u, i, 4) + 1)
                        act.wait_ge(n.acc, e + 1)
                        steady(act)
                        A_(TT[u % 2][:, :], src[:, ds(e, 1), :].rearrange("p a t -> p (a t)"), ACT.Square
                           ).then_inc(n.sq, 1)

            residual_squares("wout", n2, X)
            rsqrt(n2)
            norm_hi(n2, h_hi)
            f0 = 0
            for p, nf in enumerate(FPARTS):
                last = p == len(FPARTS) - 1
                if last:
                    act.wait_ge(cx_in, 32)
                    for k in range(KT):
                        square(ncx, CX[k // 4][:, k % 4, :], k, SS)
                for q, (ph, trips) in enumerate(UPS[p]):
                    t0 = 2 * q
                    with act.Fori(0, trips) as i:
                        for u in range(2):
                            g, v = slot(ph, 2 * u), slot(ph, 2 * u + 1)
                            act.wait_ge(panel_done, i * 4 + (N0[ph] + 2 * u + 1))
                            A_(TT[0][:, :], ps[g][:, :], ACT.Silu).then_inc(evac[g], 1)
                            act.wait_ge(evac[v], turn(ph, 2 * u + 1, i, 4) + 1)
                            steady(act)
                            A_(A[:, 0, ds(i * 2 + (t0 + u), 1), :], TT[2][:, :], ACT.Copy).then_inc(ff_hi, 1)
                    if last:
                        if q == 0:
                            rsqrt(ncx, 2, cv, cr)
                        else:
                            norm_hi(ncx, lambda k: HC[0][:, k, :], lambda k: mod[:, k, 1:2], SS)
                f0 += nf
            with act.Fori(0, 2) as i:
                for u in range(4):
                    e = i * 4 + u
                    act.wait_ge(evac[slot("down2", u)], turn("down2", u, i, 4) + 1)
                    act.wait_ge(nf1.acc, e + 1)
                    steady(act)
                    x = X[:, ds(e, 1), :].rearrange("p a t -> p (a t)")
                    A_(TT[0][:, :], x, ACT.Square).then_inc(nf1.sq, 1)
                    act.wait_ge(n3.acc, e + 1)
                    steady(act)
                    A_(TT[1][:, :], x, ACT.Square, scale=vcol("norm_final", e)).then_inc(n3.sq, 1)
            rsqrt(n3, 16)
            norm_hi(n3, h_hi, lambda k: mod[:, k, 0:1])
            act.wait_ge(aux_done, A0["lr"] + 1)
            A_(LRT[0:48, 0:T], ps[slot("lr", 0)][0:48, :], ACT.Copy).then_inc(evac[slot("lr", 0)], 1)
            act.wait_ge(panel_done, N0["lr"] + 1)
            A_(LRT[0:48, T:T + TC], ps[slot("lr", 1)][0:48, 0:TC], ACT.Copy).then_inc(evac[slot("lr", 1)], 1)
            for u in range(2):
                act.sem_inc(on_out[u], 16)
                act.sem_inc(ga_out[u], 16)
            with act.Fori(0, HEADS) as h:
                ch.enter(h, HEAD_ACT_STEPS)
                heads_act(act, h, ch)
                ch.leave(HEADS, HEAD_ACT_STEPS)

            for u in range(2):
                act.wait_ge(ga_out[u], 16 * (HEADS + 1))
            for k in range(4):
                act.dma_start(X[:, 2 * k:2 * k + 2, :], gad[2 * k:2 * k + 2, :, :].rearrange("k p t -> p k t")
                              ).then_inc(ga_in, 16)
            for q, t in enumerate(O_ORDER):
                if t >= KT - 2:
                    src = OE[t % 2]
                else:
                    src = TT[q % 4 if q < 4 else q - 6]
                    act.wait_ge(on_in[q % 4 if q < 4 else q - 6], 16 if q < 4 else 32)
                if q >= 6:
                    act.wait_ge(za_lo, q - 1)
                    act.wait_ge(on_out[t % 2 if t == 1 else 0], 16 * (HEADS + 1))
                A_(A[:, 0, t, :], src[:, :], ACT.Copy).then_inc(za_hi, 1)
                if q in (3, 4):
                    r = q - 3
                    act.wait_ge(za_lo, r + 1)
                    act.dma_start(TT[r][:, :], ond[O_ORDER[6 + r], :, :]).then_inc(on_in[r], 16)
            with act.Fori(0, 2) as i:
                for u in range(4):
                    e = i * 4 + u
                    act.wait_ge(ma_made, e + 1)
                    act.dma_start(mad[ds(e, 1), :, :].rearrange("k p t -> (k p) t"),
                                  X[:, ds(e, 1), :].rearrange("p a t -> p (a t)")).then_inc(ma_out, 16)
            act.wait_ge(pool_pad, 1)
            for g in range(4):
                if g:
                    act.wait_ge(aux_done, A0["pool"] + 2 * g)
                act.dma_start(wpl[:, :, :], d["wpool"][g].rearrange("p (k m) -> p k m", k=2)).then_inc(pool_in, 16)
                act.dma_start(icnt[:, :], d["icnt"][g]).then_inc(pool_in, 16)
                for u in range(2):
                    s = slot("pool", 6 * g + u)
                    act.wait_ge(panel_done, N0["pool"] + 4 * g + u + 1)
                    A_(up[u][:, PAD:PAD + T], ps[s][:, :], ACT.Copy).then_inc(evac[s], 1)
                for m in range(2):
                    s = slot("pool", 6 * g + 2 + m)
                    act.wait_ge(panel_done, N0["pool"] + 4 * g + 2 + m + 1)
                    A_(TT[m][:, :], ps[s][:, :], ACT.Silu).then_inc(evac[s], 1)
                for m in range(2):
                    act.wait_ge(evac[slot("pool", 6 * g + 4 + m)], turn("pool", 6 * g + 4 + m) + 1)
                    A_(A[:, 0, 2 * g + m, :], TT[2 + m][:, :], ACT.Copy).then_inc(pb_hi, 1)
            with act.Fori(0, 2) as i:
                for u in range(4):
                    e = i * 4 + u
                    act.wait_ge(panel_done, e + (N0["gb"] + 1))
                    steady(act)
                    A_(X[:, ds(e, 1), :].rearrange("p a t -> p (a t)"), ps[slot("gb", u)][:, :], ACT.Sigmoid
                       ).then_inc(evac[slot("gb", u)], 1)

            def ma_load(e, u):
                act.dma_start(TT[2 + u][:, :], mad[ds(e, 1), :, :].rearrange("k p t -> (k p) t")).then_inc(ma_in[u], 16)

            def merged_hi(e, u):
                act.wait_ge(mb_made, e + 1)
                steady(act)
                A_(H[:, 0, ds(e, 1), :].rearrange("p a t -> p (a t)"), TT[u][:, :], ACT.Copy).then_inc(m_hi, 1)

            act.wait_ge(pb_lo, KT)
            for u in range(2):
                ma_load(u, u)
            with act.Fori(0, KT // 2 - 1) as i:
                for u in range(2):
                    merged_hi(i * 2 + u, u)
                    ma_load(i * 2 + u + 2, u)
            for u in range(2):
                merged_hi(KT - 2 + u, u)
            xsv = xs.rearrange("(k p) t -> p k t", p=P)
            for k in range(KT):
                act.dma_start(XN[:, k, :], xsv[:, k, :]).then_inc(xr2_in, 16)
            residual_squares("wout2", n4, XN)
            rsqrt(n4)
            for k in range(KT):
                act.wait_ge(n4.h, k + 1)
                act.dma_start(out[k * P:(k + 1) * P, :], XN[:, k, :]).then_inc(out_st, 16)
            act.wait_ge(out_st, 16 * KT)

        @block.vector
        def _(dve):
            V_ = nc.vector
            ch = Steps(dve, dve_chain)

            def sum_start(n, acc, tiles=2):
                ch.link(V_.memset(acc, 0.0))
                dve.sem_inc(n.acc, tiles)

            def add_square(n, k, acc, tile, tiles=2):
                dve.wait_ge(n.sq, k + 1)
                V_.tensor_tensor(acc, acc, tile, ALU.add).then_inc(n.acc, 1)
                dve.wait_ge(n.acc, k + (tiles + 1))

            def newton(n, v, r, q):
                dve.wait_ge(n.r0, 1)
                ch.link(V_.tensor_tensor(q, r, r, ALU.mult))
                ch.link(V_.tensor_tensor(q, q, v, ALU.mult))
                ch.link(V_.tensor_scalar(q, q, -0.5, 1.5, ALU.mult, ALU.add))
                V_.tensor_tensor(r, r, q, ALU.mult).then_inc(n.r, 1)

            def norm_rstd(n, phase, v, r, q):
                w = v.shape[1]
                dve.wait_ge(aux_done, A0[phase] + 1)
                V_.tensor_scalar(v, ps[slot(phase, 0)][:, 0:w], 1.0 / D, EPS, ALU.mult, ALU.add).then_inc(n.var, 1)
                newton(n, v, r, q)

            def norm_tiles(n, phase, src, gain, hi=None, lo=None, shift=None, ring=TT, width=T):
                r = ps[slot(phase, 0)][:, 0:width]

                def low(k):
                    dve.wait_ge(n.hi, k + 1)
                    t = ring[k % 2][:, :]
                    if shift is None:
                        i_ = V_.tensor_tensor(lo(k), t, hi(k).bitcast(F32), ALU.subtract)
                    else:
                        i_ = V_.scalar_tensor_tensor(out=lo(k), in0=t, scalar=shift(k), in1=hi(k).bitcast(F32),
                                                     op0=ALU.add, op1=ALU.subtract)
                    i_.then_inc(n.lo, 1)

                dve.wait_ge(n.rb, 1)
                for k in range(KT):
                    if k >= 2 and hi is not None:
                        dve.wait_ge(n.lo, k - 1)
                    V_.scalar_tensor_tensor(out=src(k) if hi is None else ring[k % 2][:, :], in0=src(k),
                                            scalar=gain(k), in1=r, op0=ALU.mult, op1=ALU.mult).then_inc(n.h, 1)
                    if k and hi is not None:
                        low(k - 1)
                dve.wait_ge(n.h, KT)
                dve.sem_inc(evac[slot(phase, 0)], 1)
                if hi is not None:
                    low(KT - 1)

            def h_hi(k):
                return H[:, 0, k, :]

            def h_lo(k):
                return H[:, 1, k, :]

            def x_tile(k):
                return X[:, k, :]

            def argument(l):
                phase, u = f"mlp{l}", 0
                s = slot(phase, u)
                dve.wait_ge(aux_done, A0[phase] + 1)
                if l:
                    dve.wait_ge(sin_made, l)
                V_.tensor_scalar(fa[:, :], ps[s][:, :], vcol(f"f_b{l + 1}"), vcol("f_freq"), ALU.add, ALU.mult
                                 ).then_inc(evac[s], 1)
                dve.wait_ge(evac[s], turn(phase, u) + 1)
                ch.link(V_.tensor_scalar(fu[:, :], fa[:, :], 1.0 / (2 * np.pi), MAGIC, ALU.mult, ALU.add))
                ch.link(V_.tensor_scalar(fu[:, :], fu[:, :], MAGIC, None, ALU.subtract))
                for cst_ in (C1, C2, C3):
                    ch.link(V_.scalar_tensor_tensor(out=fa[:, :], in0=fu[:, :], scalar=-cst_, in1=fa[:, :],
                                                    op0=ALU.mult, op1=ALU.add))
                V_.tensor_scalar(fu[:, :], fa[:, :], PI_LOW, -PI_LOW, ALU.min, ALU.max).then_inc(arg_made, 1)

            sum_start(n1, TT[2][:, :])
            dve.wait_ge(vec_in, 16)
            for k in range(KT):
                add_square(n1, k, TT[2][:, :], TT[k % 2][:, :])
            norm_rstd(n1, "norm1", nv[:, 0:8], nr[:, 0:8], nq[:, 0:8])
            norm_tiles(n1, "norm1", x_tile, lambda k: vcol("norm_mix", k), h_hi, h_lo)
            argument(0)
            for z in zp:
                ch.do(V_.memset(z[:, 0:1], 0.0))
                ch.do(V_.memset(z[:, T + 1:T + 2], 0.0))
            ch.wait()
            dve.sem_inc(zpad_zero, 1)
            dve.sem_inc(z_used, 2)
            for t in hbs:
                i_ = V_.memset(t[:, :], 0.0)
            i_.then_inc(hb_zero, 1)

            def conv(z, f, tmp, dst):
                ch.link(V_.tensor_scalar(tmp, z[:, 1:T + 1], vcol("cw1", f), vcol("cb", f), ALU.mult, ALU.add))
                ch.link(V_.scalar_tensor_tensor(out=tmp, in0=z[:, 0:T], scalar=vcol("cw0", f), in1=tmp,
                                                op0=ALU.mult, op1=ALU.add))
                V_.scalar_tensor_tensor(out=dst, in0=z[:, 2:T + 2], scalar=vcol("cw2", f), in1=tmp,
                                        op0=ALU.mult, op1=ALU.add).then_inc(z_used, 1)

            def s_tile(phase, u, i, per, n, e, h):
                dve.wait_ge(evac[slot(phase, u)], turn(phase, u, i, per) + 1)
                t = (ca, cb_)[h]
                conv(zp[h], e + (8 + 8 * h), t[:, :], t[:, :])
                dve.wait_ge(z_used, n + 3)
                if h:
                    V_.tensor_tensor(S[:, ds(e, 1), :].rearrange("p a t -> p (a t)"), ca[:, :], cb_[:, :],
                                     ALU.mult).then_inc(s_made, 1)
                    dve.wait_ge(s_made, e + 1)

            s_tile("zin0", 0, 0, 0, 0, 0, 0)
            argument(1)
            s_tile("zin1", 0, 0, 0, 1, 0, 1)
            argument(2)
            for u in range(2):
                s_tile("zin2", u, 0, 0, 2 + u, 1, u)
            dve.wait_ge(silu_c, 1)
            with dve.Fori(0, 3) as i:
                ch.enter(i, 8 + 8 + 1)
                for u in range(4):
                    for j in range(2):
                        m = 2 * u + j
                        dve.wait_ge(mod_in[m % 4], i * 32 + 16 * (m // 4 + 1))
                        for w in range(2):
                            i_ = V_.tensor_tensor_reduce(mprod[:, :], mw[m % 4][:, :], crep[:, w * D:(w + 1) * D], 1.0, 0.0,
                                                         ALU.mult, ALU.add, macc[:, m, w:w + 1])
                            if w:
                                i_.then_inc(mod_used, 1)
                                dve.wait_ge(mod_used, i * 8 + (m + 1))
                            else:
                                ch.link(i_)
                    s_tile("zin3", u, i, 4, i * 4 + (N0["zin3"] + u), i * 2 + (2 + u // 2), u % 2)
                ch.link(V_.tensor_tensor(mod[:, ds(i * 8, 8), :], macc[:, :, :],
                                         vec[:, ds(i * 8 + VEC["b_mod"], 8)].unsqueeze(2).to_broadcast([P, 8, 2]), ALU.add))
                ch.leave(3, 8 + 8 + 1)
            ch.link(V_.tensor_scalar(mgs[:, :, :], mod[:, 8:16, :], 1.0, None, ALU.add))
            ch.link(V_.tensor_tensor(mgs[:, :, :], mgs[:, :, :],
                                     vec[:, VEC["norm2"]:VEC["norm2"] + 8].unsqueeze(2).to_broadcast([P, 8, 2]), ALU.mult))
            ch.link(V_.memset(gacc[:, :], 0.0))
            with dve.Fori(0, 2) as i:
                ch.enter(i, 16)
                for q in range(4):
                    o, g = 5 * q, i * 4 + q
                    for u in range(2):
                        s = slot("mix", o + 1 + u)
                        dve.wait_ge(aux_done, i * 16 + (A0["mix"] + 4 * q + 1 + u))
                        dve.wait_ge(decay_made, g * 2 + (u + 1))
                        V_.tensor_tensor(tap[u][:, :], ps[s][:, :], tap[u][:, :], ALU.mult).then_inc(evac[s], 1)
                    for u in range(2):
                        s = slot("mix", o + 1 + u)
                        dve.wait_ge(evac[s], turn("mix", o + 1 + u, i, 20) + 1)
                        ch.link(V_.scalar_tensor_tensor(out=tabs[:, :], in0=tap[u][:, :], scalar=-1.0, in1=tap[u][:, :],
                                                        op0=ALU.mult, op1=ALU.max))
                        V_.tensor_tensor(gacc[:, :], tabs[:, :], gacc[:, :], ALU.add).then_inc(tap_sum, 1)
                        dve.wait_ge(tap_sum, g * 2 + (u + 1))
                    dve.wait_ge(evac[slot("mix", o)], turn("mix", o, i, 20) + 1)
                    conv(zp[q % 2], g, ca[:, :], G0[:, ds(g, 1), :].rearrange("p a t -> p (a t)"))
                    dve.wait_ge(z_used, g + (N0["mix"] + 3))
                ch.leave(2, 16)
            with dve.Fori(0, N2 // 2) as i:
                for u in range(2):
                    s = slot("sfwd", 2 + u)
                    dve.wait_ge(aux_done, i * 4 + (A0["sfwd"] + 3 + u))
                    dve.wait_ge(s1_out[u], i * 16 + 16)
                    V_.tensor_copy(sa[u][:, :], ps[s][:, :]).then_inc(evac[s], 1)
            for u in range(2):
                dve.wait_ge(s1_out[u], 16 * (N2 // 2 + 1))
            s = slot("tapnorm", 0)
            dve.wait_ge(aux_done, A0["tapnorm"] + 1)
            V_.reciprocal(rn[:, :], ps[s][:, 0:8]).then_inc(evac[s], 1)
            barrier(dve, "dve", 1)
            for n in range(2 * GROUPS):
                c = n % 2
                dve.wait_ge(spec_xm, n + 1)
                if n >= 2:
                    dve.wait_ge(spec_inv, n - 1)
                for q, (t, gg) in enumerate(((ya, ga), (yb, gb))):
                    dve.wait_ge(spec_g, 2 * n + q + 1)
                    V_.tensor_tensor(t[c][:, :], ps[2 * c][:, 0:512], gg[c][:, :], ALU.mult).then_inc(spec_y, 1)
            barrier(dve, "dve", 2)

            def y_lo_of(e):
                dve.wait_ge(y_hi, e + 1)
                V_.tensor_tensor(A[:, 1, e, :], TT[2 + e % 2][:, :], A[:, 0, e, :].bitcast(F32), ALU.subtract
                                 ).then_inc(y_lo, 1)

            for e in range(KT):
                s, y = slot("inv", e), TT[2 + e % 2]
                dve.wait_ge(skip_made, e + 1)
                if e >= 2:
                    dve.wait_ge(y_lo, e - 1)
                dve.wait_ge(aux_done, A0["inv"] + e + 1)
                V_.scalar_tensor_tensor(out=y[:, :].rearrange("p (a b) -> p a b", b=N2),
                                        in0=ps[s][:, :].rearrange("p (b a) -> p a b", a=HALF),
                                        scalar=rn[:, e:e + 1], in1=TT[e % 2][:, :].rearrange("p (a b) -> p a b", b=N2),
                                        op0=ALU.mult, op1=ALU.add).then_inc(evac[s], 1)
                dve.wait_ge(evac[s], turn("inv", e) + 1)
                V_.tensor_tensor(y[:, :], y[:, :], G0[:, e, :], ALU.mult).then_inc(y_made, 1)
                if e:
                    y_lo_of(e - 1)
            y_lo_of(KT - 1)

            dve.wait_ge(y_lo, KT)
            sum_start(n2, TT[2][:, :])
            dve.wait_ge(xr_in, 16)
            with dve.Fori(0, 2) as i:
                for u in range(4):
                    e = i * 4 + u
                    dve.wait_ge(panel_done, e + (N0["wout"] + 1))
                    x = X[:, ds(e, 1), :].rearrange("p a t -> p (a t)")
                    V_.scalar_tensor_tensor(out=x, in0=ps[slot("wout", u)][:, :], scalar=vcol("b_out", e), in1=x,
                                            op0=ALU.add, op1=ALU.add).then_inc(evac[slot("wout", u)], 1)
                    add_square(n2, e, TT[2][:, :], TT[u % 2][:, :])
            norm_rstd(n2, "norm2", nv[:, 0:8], nr[:, 0:8], nq[:, 0:8])
            norm_tiles(n2, "norm2", x_tile, lambda k: vcol("norm_ffn", k), h_hi, h_lo)
            ch.link(V_.tensor_tensor(gfm[:, :], mgs[:, :, 0], vec[:, VEC["norm_final"]:VEC["norm_final"] + 8], ALU.mult))
            f0 = 0
            for p, nf in enumerate(FPARTS):
                last = p == len(FPARTS) - 1
                if last:
                    sum_start(ncx, cxacc[:, :])
                    for k in range(KT):
                        add_square(ncx, k, cxacc[:, :], SS[k % 2][:, :])
                for q, (ph, trips) in enumerate(UPS[p]):
                    t0 = 2 * q
                    with dve.Fori(0, trips) as i:
                        for u in range(2):
                            g, v = slot(ph, 2 * u), slot(ph, 2 * u + 1)
                            t, f = i * 2 + (t0 + u), i * 2 + (f0 + t0 + u)
                            dve.wait_ge(panel_done, i * 4 + (N0[ph] + 2 * u + 2))
                            dve.wait_ge(evac[g], turn(ph, 2 * u, i, 4) + 1)
                            V_.tensor_tensor(TT[2][:, :], TT[0][:, :], ps[v][:, :], ALU.mult).then_inc(evac[v], 1)
                            dve.wait_ge(ff_hi, f + 1)
                            V_.tensor_tensor(A[:, 1, ds(t, 1), :].rearrange("p a t -> p (a t)"), TT[2][:, :],
                                             A[:, 0, ds(t, 1), :].rearrange("p a t -> p (a t)").bitcast(F32),
                                             ALU.subtract).then_inc(ff_lo, 1)
                            dve.wait_ge(ff_lo, f + 1)
                    if last:
                        if q == 0:
                            norm_rstd(ncx, "normc", cv[:, :], cr[:, :], cq[:, :])
                            dve.sem_inc(evac[slot("normc", 0)], 1)
                        else:
                            norm_tiles(ncx, "normcb", lambda k: CX[k // 4][:, k % 4, :], lambda k: mgs[:, k, 1:2],
                                       lambda k: HC[0][:, k, :], lambda k: HC[1][:, k, :], lambda k: mod[:, k, 1:2],
                                       SS, TC)
                f0 += nf
                ph = f"down{p}"
                if last:
                    dve.wait_ge(ncx.h, KT)
                    sum_start(nf1, TT[2][:, :], 1)
                    sum_start(n3, TT[3][:, :], 1)
                with dve.Fori(0, 2) as i:
                    for u in range(4):
                        e = i * 4 + u
                        dve.wait_ge(panel_done, e + (N0[ph] + 1))
                        x = X[:, ds(e, 1), :].rearrange("p a t -> p (a t)")
                        V_.tensor_tensor(x, ps[slot(ph, u)][:, :], x, ALU.add).then_inc(evac[slot(ph, u)], 1)
                        dve.wait_ge(evac[slot(ph, u)], turn(ph, u, i, 4) + 1)
                        if last:
                            add_square(nf1, e, TT[2][:, :], TT[0][:, :], 1)
                            add_square(n3, e, TT[3][:, :], TT[1][:, :], 1)
            sl = slot("normf", 0)
            dve.wait_ge(aux_done, A0["normf"] + 1)
            ch.link(V_.tensor_scalar(nv[:, 0:8], ps[sl][:, 0:8], 1.0 / D, EPS, ALU.mult, ALU.add))
            ch.link(V_.tensor_scalar(nv[:, 8:16], ps[sl][:, 8:16], 1.0 / D, None, ALU.mult))
            V_.scalar_tensor_tensor(out=nv[:, 8:16], in0=nv[:, 0:8], scalar=EPS, in1=nv[:, 8:16],
                                    op0=ALU.mult, op1=ALU.add).then_inc(n3.var, 1)
            newton(n3, nv[:, :], nr[:, :], nq[:, :])
            dve.wait_ge(n3.r, 1)
            dve.sem_inc(nf1.r, 1)
            norm_tiles(n3, "norm3", x_tile, lambda k: gfm[:, k:k + 1], h_hi, h_lo, lambda k: mod[:, k, 0:1])
            norm_tiles(nf1, "normf", x_tile, lambda k: vcol("norm_final", k))
            dve.wait_ge(rot_in, 32)
            with dve.Fori(0, HEADS) as h:
                ch.enter(h, HEAD_STEPS)
                heads_dve(dve, h, ch)
                ch.leave(HEADS, HEAD_STEPS)
            for u in range(2):
                dve.wait_ge(ga_out[u], 16 * (HEADS + 1))
            for q, t in enumerate(O_ORDER):
                src = OE[t % 2] if t >= KT - 2 else TT[q % 4 if q < 4 else q - 6]
                dve.wait_ge(za_hi, q + 1)
                V_.tensor_tensor(A[:, 1, t, :], src[:, :], A[:, 0, t, :].bitcast(F32), ALU.subtract).then_inc(za_lo, 1)
            dve.wait_ge(ga_in, 64)
            with dve.Fori(0, 2) as i:
                for u in range(4):
                    e, s = i * 4 + u, slot("mixa", u)
                    x = X[:, ds(e, 1), :].rearrange("p a t -> p (a t)")
                    dve.wait_ge(panel_done, e + (N0["mixa"] + 1))
                    V_.tensor_tensor(x, x, ps[s][:, :], ALU.mult).then_inc(evac[s], 1)
                    dve.wait_ge(evac[s], turn("mixa", u, i, 4) + 1)
                    dve.sem_inc(ma_made, 1)
            dve.wait_ge(ma_out, 16 * KT)
            for t in up:
                ch.do(V_.memset(t[:, 0:PAD], 0.0))
                ch.do(V_.memset(t[:, PAD + T:W_U], 0.0))
            ch.wait()
            dve.sem_inc(pool_pad, 1)
            for g, w in enumerate(POOL_WINDOWS):
                dve.wait_ge(pool_in, 32 * (g + 1))
                for u in range(2):
                    s = slot("pool", 6 * g + u)
                    dve.wait_ge(evac[s], turn("pool", 6 * g + u) + 1)
                    src, span, width, q = up[u], 1, W_U, 0
                    while span < w:
                        width -= span
                        dst = (wa, wb)[q % 2]
                        ch.link(V_.tensor_tensor(dst[:, 0:width], src[:, 0:width], src[:, span:span + width], ALU.add))
                        src, span, q = dst, span * 2, q + 1
                    lo = PAD - w // 2
                    ch.link(V_.tensor_tensor(pd[u][:, :], src[:, lo:lo + T], icnt[:, :], ALU.mult))
                    V_.tensor_tensor(pd[u][:, :], pd[u][:, :], up[u][:, PAD:PAD + T], ALU.subtract).then_inc(pd_made, 1)
                    dve.wait_ge(pd_made, 2 * g + u + 1)
                for m in range(2):
                    s = slot("pool", 6 * g + 4 + m)
                    dve.wait_ge(aux_done, A0["pool"] + 2 * g + m + 1)
                    dve.wait_ge(evac[slot("pool", 6 * g + 2 + m)], turn("pool", 6 * g + 2 + m) + 1)
                    V_.scalar_tensor_tensor(out=TT[2 + m][:, :], in0=ps[s][:, :], scalar=vcol("pool_scale", 2 * g + m),
                                            in1=TT[m][:, :], op0=ALU.mult, op1=ALU.mult).then_inc(evac[s], 1)
                    dve.wait_ge(pb_hi, 2 * g + m + 1)
                    V_.tensor_tensor(A[:, 1, 2 * g + m, :], TT[2 + m][:, :], A[:, 0, 2 * g + m, :].bitcast(F32),
                                     ALU.subtract).then_inc(pb_lo, 1)
                    dve.wait_ge(pb_lo, 2 * g + m + 1)
            with dve.Fori(0, KT // 4) as i:
                for u in range(4):
                    e, s, t = i * 4 + u, slot("mixb", u), TT[u % 2]
                    dve.wait_ge(panel_done, e + (N0["mixb"] + 1))
                    V_.tensor_tensor(t[:, :], X[:, ds(e, 1), :].rearrange("p a t -> p (a t)"), ps[s][:, :], ALU.mult
                                     ).then_inc(evac[s], 1)
                    dve.wait_ge(evac[s], turn("mixb", u, i, 4) + 1)
                    dve.wait_ge(ma_in[u % 2], i * 32 + 16 * (u // 2 + 1))
                    V_.tensor_tensor(t[:, :], t[:, :], TT[2 + u % 2][:, :], ALU.add).then_inc(mb_made, 1)
                    dve.wait_ge(m_hi, e + 1)
                    V_.tensor_tensor(H[:, 1, ds(e, 1), :].rearrange("p a t -> p (a t)"), t[:, :],
                                     H[:, 0, ds(e, 1), :].rearrange("p a t -> p (a t)").bitcast(F32), ALU.subtract
                                     ).then_inc(m_lo, 1)
                    dve.wait_ge(m_lo, e + 1)
            sum_start(n4, TT[2][:, :])
            dve.wait_ge(xr2_in, 16 * KT)
            with dve.Fori(0, 2) as i:
                for u in range(4):
                    e, s = i * 4 + u, slot("wout2", u)
                    dve.wait_ge(panel_done, e + (N0["wout2"] + 1))
                    x = XN[:, ds(e, 1), :].rearrange("p a t -> p (a t)")
                    V_.scalar_tensor_tensor(out=x, in0=ps[s][:, :],
                                            scalar=mod[:, ds(e + 16, 1), 0:1].rearrange("p a b -> p (a b)"), in1=x,
                                            op0=ALU.mult, op1=ALU.add).then_inc(evac[s], 1)
                    add_square(n4, e, TT[2][:, :], TT[u % 2][:, :])
            norm_rstd(n4, "norm4", nv[:, 0:8], nr[:, 0:8], nq[:, 0:8])
            norm_tiles(n4, "norm4", lambda k: XN[:, k, :], lambda k: vcol("final2", k))


def _constants():
    f8 = np.float64
    cst = np.zeros((P, NCST), np.float32)

    def put(name, a):
        cst[:a.shape[0], CST[name]:CST[name] + a.shape[1]] = a

    put("ident", np.eye(P))
    put("ones", np.ones((P, P)))
    j, i = np.meshgrid(np.arange(P), np.arange(P), indexing="ij")
    put("mask_f", (j <= i) * 1.0)
    put("mask_b", (j >= i) * 1.0)
    m = np.arange(P)
    swap = np.where(m % 64 < 32, m + 32, m - 32)
    perm = np.zeros((P, P))
    perm[swap, m] = 1
    put("perm", perm)
    n1, k1 = np.arange(N1, dtype=f8)[:, None], np.arange(HALF, dtype=f8)[None, :]
    th = 2 * np.pi * n1 * (k1 + 0.5) / N1
    dft = np.stack([np.cos(th), -np.sin(th)], -1).reshape(N1, P)
    put("dft_s", dft[:HALF])
    put("dft_g", dft * np.where(np.arange(N1) < HALF, 1.0, -1.0)[:, None])
    inv = np.stack([np.cos(th[:HALF]), -np.sin(th[:HALF])], -1).reshape(HALF, P).T / (N1 * N2 / 2)
    put("idft", inv)
    r, n2 = np.arange(P)[:, None], np.arange(N2)[None, :]
    tok = np.where(r < HALF, N2 * r + n2, N2 * (N1 - r) - n2)
    none = tok >= T
    tok = np.where(none, 0, tok)
    t = np.linspace(0.0, 1.0, T, dtype=np.float32)
    put("tneg", -t[tok])
    put("tmask", np.where(none, -1e30, 0.0))
    w = (np.float32(2.0 * np.pi) * np.arange(T, dtype=np.float32) / np.float32(T))[:, None]
    bands = np.linspace(1e-4, 15, 16, dtype=np.float32)[None, :]
    arg = (bands * w).astype(f8)
    ft = np.concatenate([t[:, None], np.cos(arg), -np.sin(arg)], -1).astype(np.float32)
    cols = tok.reshape(2, HALF, N2).transpose(0, 2, 1).reshape(2, T)
    feat = np.concatenate([ft[cols[0]].T, ft[cols[1]].T], 0)
    kf = np.zeros((GROUPS, P, 5, P))
    a, b = np.arange(N2, dtype=f8)[:, None], np.arange(N2, dtype=f8)[None, :]
    for k in range(HALF):
        g, o = k // 4, (k % 4) * 32
        th = 2 * np.pi * (a * (k + 0.5) / (N1 * N2) + a * b / N2)
        c, s = np.cos(th), np.sin(th)
        re, im = np.concatenate([c, s], 0), np.concatenate([-s, c], 0)
        blk = kf[g, o:o + 32]
        blk[:, 0, o:o + 32] = np.concatenate([re, im], 1)
        blk[:, 2, o:o + 32] = np.concatenate([re, re], 1)
        blk[:, 3, o:o + 32] = np.concatenate([im, -im], 1)
        blk[:, 4, o:o + 32] = np.block([[c.T, s.T], [-s.T, c.T]])
        blk[:, 1, o:o + 32] = np.block([[-s.T, c.T], [c.T, s.T]])
    tt = np.arange(T)
    fr = np.float32(10000.0) ** (-np.arange(32, dtype=np.float32) / np.float32(32))
    cos, sin = np.zeros((P, T)), np.zeros((P, T))
    for p in range(P):
        pos = (tt // 64 if p < 64 else tt % 64).astype(np.float32)
        an = (pos * fr[p % 32]).astype(f8)
        cos[p] = np.cos(an)
        sin[p] = np.sin(an) * (-1 if p % 64 < 32 else 1)
    icnt = np.zeros((4, P, T))
    for g, wd in enumerate(POOL_WINDOWS):
        lo = np.clip(tt - wd // 2, 0, T - 1)
        hi = np.clip(tt + (wd - 1 - wd // 2), 0, T - 1)
        icnt[g] = 1.0 / (hi - lo + 1)
    f4 = lambda x: np.ascontiguousarray(x, np.float32)
    return {"cst": cst, "feat": f4(feat), "kfft": f4(kf.reshape(GROUPS, P, 5 * P)), "cos": f4(cos), "sin": f4(sin),
            "icnt": f4(icnt)}


def _layout(x):
    g = {k: np.asarray(v) for k, v in x.items()}
    cols = lambda a: np.asarray(a).reshape(-1, P).T
    vec = np.zeros((P, NVEC), np.float32)
    for name, a in (("norm_mix", g["norm_mix"]), ("norm_ffn", g["norm_ffn"]), ("norm_final", g["norm_final"]),
                    ("b_in", g["hy_b_in"]), ("cw0", g["hy_conv_w"][0, 0]), ("cw1", g["hy_conv_w"][0, 1]),
                    ("cw2", g["hy_conv_w"][0, 2]), ("cb", g["hy_conv_b"]), ("skip", g["hy_skip"]),
                    ("b_out", g["hy_b_out"]), ("norm2", g["norm_g_2"]), ("b_mod", g["b_mod_2"]),
                    ("b_gf", g["b_gate_f_2"]), ("b_gb", g["b_gate_b_2"]), ("gla_g", g["gla_norm_g_2"]),
                    ("pool_scale", g["pool_scale_2"]), ("final2", g["final_norm_g_2"])):
        a = cols(a)
        vec[:, VEC[name]:VEC[name] + a.shape[1]] = a
    for name, key in (("f_b1", "hy_f_b1"), ("f_b2", "hy_f_b2"), ("f_b3", "hy_f_b3"), ("f_freq", "hy_f_freq")):
        vec[:HALF, VEC[name]] = vec[HALF:, VEC[name]] = g[key][0]
    w1, w2, w3, wo = g["hy_f_w1"][0], g["hy_f_w2"][0], g["hy_f_w3"][0], g["hy_f_wout"][0]

    def twice(w):
        a = np.zeros((2 * w.shape[0], 2 * w.shape[1]), np.float32)
        a[:w.shape[0], :w.shape[1]] = w
        a[w.shape[0]:, w.shape[1]:] = w
        return a

    wtap = np.concatenate([wo[:, :D], wo[:, D:]], 0)
    dec = np.concatenate([np.repeat(g["hy_decay"][0, :1], HALF, 0), np.repeat(g["hy_decay"][0, 1:], HALF, 0)], 0)

    def panel(w):
        a = np.zeros((D, P), np.float32)
        a[:w.shape[0], :w.shape[1]] = w
        return a.reshape(8, P, P).transpose(1, 0, 2).reshape(P, D)

    out = []

    def add(w, f, rows=slice(None)):
        out.append(panel(w[rows, f * P:(f + 1) * P]))

    win, wi2 = g["hy_w_in"][0], g["w_in_2"][0]
    q_, k_, v_, za, lr, ub, zb, ga, gb = np.cumsum([0, 512, 512, 1024, 1024, 32, 1024, 1024, 1024])
    for f in range(8, 16):
        add(win, f)
        add(win, 8 + f)
    for f in range(8):
        add(win, f)
    for f in range(8):
        add(g["hy_w_out"][0], f)
    f0 = 0
    for nf in FPARTS:
        for f in range(f0, f0 + nf):
            add(g["ffn_w_gate"][0], f)
            add(g["ffn_w_up"][0], f)
        for f in range(8):
            add(g["ffn_w_down"][0], f, slice(f0 * P, (f0 + nf) * P))
        f0 += nf
    low = np.zeros((D, 48), np.float32)
    low[:, 0:16] = wi2[:, lr:lr + 16]
    low[:, 32:48] = wi2[:, lr + 16:lr + 32]
    out.append(panel(low))
    for h in range(HEADS):
        add(wi2[:, q_:k_], h)
        add(wi2[:, k_:v_], h)
        first = (N0["heads"] + 2) % 2
        for e in (first, 1 - first):
            add(wi2[:, v_:za], 2 * h + e)
        for w0 in (za, ga):
            for e in range(2):
                add(wi2[:, w0:w0 + D], 2 * h + e)
    for f in range(8):
        add(g["w_branch_a_2"][0], f)
    for q in range(4):
        for w0 in (ub, zb):
            for u in range(2):
                add(wi2[:, w0:w0 + D], 2 * q + u)
    for w, w0 in ((wi2, gb), (g["w_branch_b_2"][0], 0), (g["w_out_2"][0], 0)):
        for f in range(8):
            add(w[:, w0:w0 + D], f)
    assert len(out) == NPANELS
    modp = np.ascontiguousarray(g["w_mod_2"][0].T).reshape(24, P, D)
    cvec = np.concatenate([g["c_2"].reshape(-1), g["c_ctx_2"].reshape(-1)])[None]
    wup = np.zeros((48, HEADS * DK), np.float32)
    wup[0:16] = g["w_gate_up_f_2"][0]
    wup[32:48] = g["w_gate_up_b_2"][0]
    wpool = g["w_pool_2"][0].reshape(4, 2, P, 256).transpose(0, 2, 1, 3).reshape(4, P, 512)
    c = np.ascontiguousarray
    return {"vec": vec, "xT": c(g["x"][0].T), "ctxT": c(g["ctx_2"][0].T), "panels": np.stack(out), "modp": modp, "cvec": cvec,
            "fw1": twice(w1), "fw2": twice(w2), "fw3": twice(w3), "wtap": c(wtap), "dec": c(dec), "wup": wup,
            "wpool": c(wpool)}


def kernel(**inputs):
    import concourse.bacc as _bacc
    from concourse.bass_utils import run_bass_kernel_spmd as _run

    arrays = {**_layout(inputs), **_constants()}
    nc = _bacc.Bacc("TRN2", target_bir_lowering=False, num_devices=1)
    args = {n: nc.dram_tensor(f"in_{n}", a.shape, F32, kind="ExternalInput").ap() for n, a in arrays.items()}
    out = nc.dram_tensor("out_T", (D, T), F32, kind="ExternalOutput").ap()
    program(nc, args, out)
    r = _run(nc, [{f"in_{n}": a for n, a in arrays.items()}], core_ids=[0])
    return np.ascontiguousarray(r.results[0]["out_T"].T)[None]
```

```python
from contextlib import ExitStack

import numpy as np
import concourse.bass as bass
from concourse import mybir

F32 = mybir.dt.float32
F32R = mybir.dt.float32r
ACT = mybir.ActivationFunctionType
ALU = mybir.AluOpType
ds = bass.ds

P = 128
D = 1024
T = 1024
KT = D // P
TC = 256
F = 2816
FPARTS = (8, 8, 6)
EPS = 1e-6
HEADS, DK, DV = 4, 128, 256
CH = 128
NCH = T // CH
NCC = TC // CH
GATE_NORM = 16.0
CLAMP = 40.0 * GATE_NORM
N1, N2 = 128, 16
HALF = N1 // 2
GROUPS = 16
POOL_WINDOWS = (2, 4, 8, 16)
PAD = 8
MAGIC = 1.5 * 2.0 ** 23
C1 = 6.28125
C2 = float(np.float32(np.round((2 * np.pi - C1) * 2 ** 20) / 2 ** 20))
C3 = float(np.float32(2 * np.pi - C1 - C2))
PI_LOW = 3.1415925

VEC = {}
_c = 0
for _n, _w in (("norm_mix", 8), ("norm_ffn", 8), ("norm_final", 8), ("b_in", 24), ("cw0", 24), ("cw1", 24),
               ("cw2", 24), ("cb", 24), ("skip", 8), ("b_out", 8), ("norm2", 8), ("b_mod", 24), ("b_gf", 4),
               ("b_gb", 4), ("gla_g", 2), ("pool_scale", 8), ("final2", 8), ("f_b1", 1), ("f_b2", 1),
               ("f_b3", 1), ("f_freq", 1)):
    VEC[_n] = _c
    _c += _w
NVEC = _c
CST = {}
_c = 0
for _n, _w in (("ident", 128), ("ones", 128), ("mask_f", 128), ("mask_b", 128), ("dft_g", 128),
               ("dft_s", 128), ("idft", 64), ("tneg", 16), ("tmask", 16)):
    CST[_n] = _c
    _c += _w
NCST = _c

INV = [("rows", 0, 512, n2) for n2 in range(0, N2, 2)]
for _e in range(4):
    INV += [("rows", 512, 256, 4 * _e), ("tile", _e)]
INV += [("rows", 768, 256, 0), ("tile", 4)] + [("rows", 768, 256, _n2) for _n2 in (4, 8, 12)]
INV += [("tile", _e) for _e in (5, 6, 7)]


def inv_rows(e):
    return max(o for o, j in enumerate(INV) if j[0] == "rows" and j[1] <= 128 * e < j[1] + j[2])


PHASES = [("mlp0", 1, 0), ("zin0", 1, 1), ("norm1", 1, 0), ("zin1", 1, 1), ("mlp1", 1, 0), ("zin2", 1, 1),
          ("mlp2", 1, 0), ("zin3", 1, 1), ("zin4", 12, 12), ("mix", 40, 8), ("sfwd", 32, 0), ("tapnorm", 1, 0),
          ("spec", 0, GROUPS), ("inv", len(INV), 0), ("wout", 8, 8), ("first", 1, 1), ("norm2", 1, 0), ("second", 3, 3)]
UPS = [[(f"up{_p}", _n // 2)] for _p, _n in enumerate(FPARTS)]
UPS[0] = [("up0", FPARTS[0] // 2 - 1)]
UPS[-1] = [("up2", 1), ("up2b", FPARTS[-1] // 2 - 1)]
for _p, _ups in enumerate(UPS):
    for _u, (_name, _trips) in enumerate(_ups):
        PHASES += [(_name, 4 * _trips, 4 * _trips)]
        if len(_ups) > 1:
            PHASES += [(("normc", "normcb")[_u], 1, 0)]
    PHASES += [(f"down{_p}", 8, 8)]
HJ, HP, HA = 28, 8, 19
PHASES += [("normf", 1, 0), ("lr", 1, 0), ("norm3", 1, 0), ("lrx", 1, 1), ("heads", HJ * HEADS, HP * HEADS), ("mixa", 8, 8),
           ("pool", 24, 16), ("gb", 8, 8), ("mixb", 8, 8), ("wout2", 8, 8), ("norm4", 1, 0)]
J0, N0, A0 = {}, {}, {}
_j = _n_ = 0
for _name, _jobs, _pan in PHASES:
    J0[_name], N0[_name] = _j, _n_
    _j += _jobs
    _n_ += _pan
NPANELS = _n_
V_PANEL = N0["heads"] + 3
assert V_PANEL % 2 == 0 and HP % 2 == 0
_a = 0
AUX = {"norm1": 1, "mlp0": 1, "mlp1": 1, "mlp2": 1, "mix": 32, "tapnorm": 1, "sfwd": 32, "inv": len(INV), "norm2": 1,
       "normf": 1, "normc": 1, "lr": 1, "heads": HA * HEADS, "pool": 8, "norm4": 1}
for _name, _, _ in PHASES:
    A0[_name] = _a
    _a += AUX.get(_name, 0)


class Steps:

    def __init__(self, eng, sem):
        self.eng, self.sem, self.n, self.base = eng, sem, 0, 0

    def do(self, ins):
        ins.then_inc(self.sem, 1)
        self.n += 1

    def wait(self, but=0):
        self.eng.wait_ge(self.sem, self.base + (self.n - but))

    def link(self, ins):
        self.do(ins)
        self.wait()

    def enter(self, i, per):
        self.base, self.start = i * per, self.n

    def leave(self, trips, per):
        assert self.n - self.start == per, (self.n - self.start, per)
        self.base, self.n = 0, self.start + trips * per


def program(nc, d, out):
    ctx = ExitStack()
    with ctx:
        base = -(-nc.sbuf_base // 64) * 64

        def at(name, shape, offset, dt=F32):
            return nc.alloc_sbuf_tensor_at(name, shape, dt, offset=offset)

        def sem(name):
            return ctx.enter_context(nc.semaphore(name))

        o_vec = base
        o_cst = o_vec + NVEC * 4 + 8
        o_small = o_cst + NCST * 4
        o_raw = base + 5504
        o_wh = o_raw + 8192
        o_wl = o_wh + 8192
        RH = o_wl + 8192
        RA = RH + 65536
        RX = RA + 65536
        RT = RX + 32768
        assert o_small + 568 <= o_raw and RT + 18880 <= nc.sbuf_usable_end
        K = 1024
        vec = at("vec", [P, NVEC], o_vec)
        cst = at("cst", [P, NCST], o_cst)
        rn = at("rn", [P, 8], o_small)
        mod = at("mod", [P, 24, 2], o_small + 32)
        mgs = at("mgs", [P, 8, 2], o_small + 224)
        macc = at("macc", [P, 8, 2], o_small + 288)
        nv, nr, nq = (at(f"n{x}", [P, 16], o_small + 352 + 64 * k) for k, x in enumerate("vrq"))
        nc_ = at("nctx", [P, 3, 2], o_small + 544)
        cv, cr, cq = (nc_[:, k, :] for k in range(3))
        gfm = at("gfm", [P, 8], o_small)
        wraw = at("wraw", [P, 2, 8, P], o_raw)
        whi = at("whi", [P, 2, 8, P], o_wh, F32R)
        wlo = at("wlo", [P, 2, 8, P], o_wl, F32R)
        H = at("H", [P, 2, KT, T], RH, F32R)
        A = at("A", [P, 2, KT, T], RA, F32R)
        X = at("X", [P, KT, T], RX)
        TT = [at(f"T{i}", [P, T], RT + 4 * K * i) for i in range(4)]
        feat = at("feat", [66, T], RA + 32 * K)
        fa = at("fa", [P, T], RA + 36 * K)
        fu = at("fu", [P, T], RA + 40 * K)
        fh = at("fh", [P, T], RA + 44 * K)
        fw1 = at("fw1", [66, P], RA + 8 * K)
        fw2 = at("fw2", [P, P], RA + 8 * K + 512)
        fw3 = at("fw3", [P, P], RA + 9 * K)
        crep = at("crep", [P, 2 * D], RX + 20 * K)
        mw = [at(f"mw{m}", [P, D], RA + 48 * K + 4 * K * m) for m in range(4)]
        mprod = at("mprod", [P, D], RX + 28 * K)
        wtap = at("wtap", [P, T], RX)
        dec = at("dec", [P, T], RX + 4 * K)
        hb = at("hb", [P, N2, HALF], RX + 8 * K)
        tap = [at(f"tap{u}", [P, T], RX + 12 * K + 4 * K * u) for u in range(2)]
        gsp = [at(f"gsp{u}", [P, T], RX + 20 * K + 4 * K * u) for u in range(2)]
        gacc = at("gacc", [P, T], RX + 28 * K)
        hbs = [at(f"hbs{u}", [P, N1], RT + 16896 + 512 * u) for u in range(2)]
        S = at("S", [P, KT, T], RA)
        G0 = at("G0", [P, KT, T], RA + 32 * K)
        zp = at("zp", [P, T + 2], RT)
        R1 = at("R1", [P, T], RT + 4128)
        ca = at("ca", [P, T], RT + 8256)
        cb_ = at("cb_", [P, T], RT + 8256 + 4 * K)
        tabs = at("tabs", [P, T], RT + 8256 + 4 * K)
        sn = [at(f"sn{u}", [P, KT, HALF], RH + 2 * K * u) for u in range(2)]
        st_ = [at(f"st{u}", [HALF, T], RH + 4 * K + 4 * K * u) for u in range(2)]
        sa = [at(f"sa{u}", [P, T], RH + 12 * K + 4 * K * u) for u in range(2)]
        kf = [at(f"kf{u}", [P, 5, P], RX + 2560 * u) for u in range(3)]
        kh = [at(f"kh{u}", [P, 3, P], RX + 7680 + 1536 * u, F32R) for u in range(2)]
        kl = [at(f"kl{u}", [P, 3, P], (RX + 10752, RT + 16 * K)[u], F32R) for u in range(2)]
        bs = [at(f"bs{u}", [P, T], RX + 12 * K + 4 * K * u) for u in range(2)]
        bh = [at(f"bh{u}", [P, 512], RX + 20 * K + 2 * K * u, F32R) for u in range(2)]
        bl = [at(f"bl{u}", [P, 512], RT + 8 * K + 2 * K * u, F32R) for u in range(2)]
        ga = [at(f"ga{u}", [P, 512], RX + 24 * K + 2 * K * u) for u in range(2)]
        gb = [at(f"gb{u}", [P, 512], RX + 28 * K + 2 * K * u) for u in range(2)]
        ya = [at(f"ya{u}", [P, 512], RT + 2 * K * u) for u in range(2)]
        yb = [at(f"yb{u}", [P, 512], RT + 4 * K + 2 * K * u) for u in range(2)]
        yi = [at(f"yi{u}", [P, 512], RT + 12 * K + 2 * K * u) for u in range(2)]
        YB = at("YB", [P, N2, T], RH)
        CX = at("CX", [P, KT, TC], RA + 56 * K)
        cxacc = at("cxacc", [P, TC], RA + 31 * K)
        HC = [at("HCH", [P, KT, TC], RA + 24 * K, F32R), at("HCL", [P, KT, TC], RA + 56 * K, F32R)]
        QT = at("QT", [P, T], RA)
        KTt = at("KT", [P, T], RA + 4 * K)
        BB = [at("BF", [P, T], RA + 8 * K), at("BB", [P, T], RA + 12 * K)]
        QD = [at("QF", [P, T], RA + 16 * K), QT]
        KD = [at("KF", [P, T], RA + 20 * K), KTt]
        KDT = [at("KFT", [P, NCH, P], RA + 32 * K), at("KBT", [P, NCH, P], RA + 36 * K)]
        ROT = [at("ROTQ", [P, T], RA + 32 * K), at("ROTK", [P, T], RA + 36 * K)]
        KDTC = at("KDTC", [P, 2, NCC, P], RA + 40 * K)
        KC = at("KC", [P, TC], RA + 42 * K)
        BBC = at("BBC", [P, 2, TC], RA + 43 * K)
        KDC = at("KDC", [P, 2, TC], RA + 45 * K)
        COS = at("COS", [P, T], RA + 47 * K)
        LRT = at("LRT", [48, T + TC], RA + 51 * K)
        wup_h = at("wup_h", [48, DK], o_cst + CST["dft_g"] * 4)
        SIN = at("SIN", [P, T], RX)
        V = at("V", [P, NCH, DV], RX + 4 * K)
        VC = at("VC", [P, NCC, DV], RX + 12 * K)
        SR = [at("SRF", [P, NCH, DV], RX + 16 * K), at("SRB", [P, NCH, DV], RX + 24 * K)]
        SCO = TT[0:2]
        OE, SZA, SGA = [KD[0], KD[1]], BB, ROT
        SS = [at("SF", [P, DV], RT + 16 * K), at("SB", [P, DV], RT + 17 * K)]
        o_col = RT + 18 * K
        col = [at("colf", [P, 40], o_col), at("colb", [P, 40], o_col + 160)]
        dcol = [at("dcolf", [P, 10], o_col + 320), at("dcolb", [P, 10], o_col + 384)]
        W_U = T + 2 * PAD
        up = [at(f"up{u}", [P, W_U], RX + 4224 * u) for u in range(2)]
        wa = at("wa", [P, W_U], RX + 8448)
        wb = at("wb", [P, W_U], RX + 12672)
        pd = [at(f"pd{u}", [P, T], RX + 16896 + 4 * K * u) for u in range(2)]
        icnt = at("icnt", [P, T], RX + 16896 + 8 * K)
        wpl = at("wpl", [P, 2, 256], RX + 16896 + 12 * K)
        assert 16896 + 14 * K <= 32 * K
        XN = at("XN", [P, KT, T], RA)

        ps = [ctx.enter_context(nc.psum_tensor(f"ps{s}", [P, 2 * 512], F32)) for s in range(4)]

        def dram(name, shape):
            return nc.dram_tensor(name, shape, F32, kind="Internal").ap()

        g1 = dram("g1", [P, N2, T])
        s1 = dram("s1", [P, N2, T])
        xs = dram("xs", [D, T])
        ond = dram("ond", [KT, P, T])
        gad = dram("gad", [KT, P, T])
        mad = dram("mad", [KT, P, T])

        const_in, vec_in, feat_in, filt_in = (sem(f"{x}_in") for x in ("const", "vec", "feat", "filt"))
        x_in = [sem(f"x_in{k}") for k in range(4)]
        raw_in = [sem("raw_in0"), sem("raw_in1")]
        hi_made, split_made = sem("hi_made"), sem("split_made")
        panel_done, aux_done = sem("panel_done"), sem("aux_done")
        evac = [sem(f"evac{s}") for s in range(4)]
        act_chain, dve_chain = sem("act_chain"), sem("dve_chain")
        ended = {e: sem(f"ended_{e}") for e in ("pe", "act", "dve")}

        def slot(phase, u):
            return (J0[phase] + u) % 4

        def turn(phase, u, i=0, per=0):
            return (J0[phase] + u) // 4 + i * (per // 4)

        def barrier(eng, name):
            eng.drain().then_inc(ended[name], 1)
            for other in ("pe", "act", "dve"):
                if other != name:
                    eng.wait_ge(ended[other], 1)

        waited = sem("waited")

        def steady(eng):
            eng.sem_inc(waited, 1)

        class NormSems:

            def __init__(self, tag, chain=True, split=True, tiles=True):
                self.sq, self.acc, self.r, self.rb = (sem(f"{x}_{tag}") for x in ("sq", "acc", "r", "rb"))
                if chain:
                    self.var, self.r0 = sem(f"var_{tag}"), sem(f"r0_{tag}")
                if tiles:
                    self.h = sem(f"h_{tag}")
                if split:
                    self.hi, self.lo = sem(f"hi_{tag}"), sem(f"lo_{tag}")

        n1, n2 = NormSems("mix", tiles=False), NormSems("ffn", tiles=False)
        n3, ncx, n4 = NormSems("x2"), NormSems("ctx"), NormSems("fin2", split=False)
        nf1 = NormSems("fin", chain=False, split=False)
        arg_made, sin_made, hb_zero = sem("arg_made"), sem("sin_made"), sem("hb_zero")
        hbs_made, decay_made, tap_sum = sem("hbs_made"), sem("decay_made"), sem("tap_sum")
        g1_out = [sem("g1_out0"), sem("g1_out1")]
        c_made, s_made = sem("c_made"), sem("s_made")
        sn_made = sem("sn_made")
        s1_out = [sem("s1_out0"), sem("s1_out1")]
        silu_c = sem("silu_c")
        mod_in = [sem(f"mod_in{m}") for m in range(4)]
        mod_used = sem("mod_used")
        spec_in = [sem("spec_in0"), sem("spec_in1")]
        spec_hi, spec_lo = sem("spec_hi"), sem("spec_lo")

        def rows_made(n):
            return n + 2 + n // 2

        def mats_made(g):
            return 3 * g + 1

        spec_gm, spec_xm, spec_g, spec_y, spec_inv, spec_ev = (
            sem(f"spec_{x}") for x in ("gm", "xm", "g", "y", "inv", "ev"))
        yb_in = [sem("yb_in0"), sem("yb_in1")]
        kg_in = mod_in[0:3]
        skip_made, y_made, y_hi, y_lo = sem("skip_made"), sem("y_made"), sem("y_hi"), sem("y_lo")
        xr_in = sem("xr_in")
        sg_made, ff_prod, ff_hi, ff_lo = (sem(x) for x in ("sg_made", "ff_prod", "ff_hi", "ff_lo"))
        x_spilled, rot_in, cx_in = sem("x_spilled"), sem("rot_in"), sem("cx_in")
        gate_abs, gate_ln, wup_in = sem("gate_abs"), sem("gate_ln"), sem("wup_in")
        dif_made, exp_made, qk_made = sem("dif_made"), sem("exp_made"), sem("qk_made")
        kdc_made, colexp = sem("kdc_made"), sem("colexp")
        state_made, sco_made = sem("state_made"), sem("sco_made")
        osq, osum, o_var, o_r0, o_r, o_rb, on_made = (
            sem(x) for x in ("osq", "osum", "o_var", "o_r0", "o_r", "o_rb", "on_made"))
        on_out = [sem("on_out0"), sem("on_out1")]
        ga_out = [sem("ga_out0"), sem("ga_out1")]
        on_in = [sem(f"on_in{k}") for k in range(4)]
        ga_in = sem("ga_in")
        za_hi, za_lo = sem("za_hi"), sem("za_lo")
        ma_out, ma_made = sem("ma_out"), sem("ma_made")
        ma_in = [sem(f"ma_in{k}") for k in range(2)]
        pool_in, pool_pad, pd_made, pb_hi, pb_lo = (
            sem(x) for x in ("pool_in", "pool_pad", "pd_made", "pb_hi", "pb_lo"))
        mb_made, m_hi, m_lo = sem("mb_made"), sem("m_hi"), sem("m_lo")
        xr2_in = sem("xr2_in")
        out_st = sem("out_st")
        swapped = sem("swapped")

        def vcol(name, j=0):
            return vec[:, ds(VEC[name] + j, 1)]

        def cc(name, rows=P):
            w = {"idft": 64, "tneg": 16, "tmask": 16}.get(name, 128)
            return cst[0:rows, CST[name]:CST[name] + w]

        ident, ones = cc("ident"), cc("ones")

        def operand(act, a, k, t0, w):
            return act[a][:, k, t0:t0 + w] if isinstance(act, list) else act[:, a, k, t0:t0 + w]

        def chunk(t, c):
            return t[:, c * CH:(c + 1) * CH]


        def aux_at(h, a):
            return h * HA + (A0["heads"] + a)

        def evac_at(h, u):
            return h * (HJ // 4) + (turn("heads", u) + 1)

        O_ORDER = (0, 4, 2, 3, 7, 6, 1, 5)
        STATE_JOBS = ((17, 0, range(0, 4)), (18, 1, range(4, NCH)), (19, 0, range(4, NCH - 1)), (20, 1, range(1, 4)))

        def heads_pe(pe, h, free, panel_mm):
            mm = nc.tensor.matmul

            def p(u):
                return ps[slot("heads", u)]

            def begin(u):
                free("heads", u, h, HJ)

            n0 = N0["heads"]
            pe.wait_ge(wup_in, h * 16 + 16)
            for u in range(2):
                begin(u)
                for c in range(2):
                    last = mm(p(u)[:, c * 512:(c + 1) * 512], wup_h[32 * u:32 * u + 16, :],
                              LRT[32 * u:32 * u + 16, c * 512:(c + 1) * 512], start=True, stop=True)
                last.then_inc(aux_done, 1)
            begin(2)
            for u in range(2):
                last = mm(p(2)[:, u * 512:u * 512 + TC], wup_h[32 * u:32 * u + 16, :],
                          LRT[32 * u:32 * u + 16, T:T + TC], start=True, stop=True)
            last.then_inc(aux_done, 1)
            pe.wait_ge(split_made, h * HP + (n0 + 1))
            begin(3)
            panel_mm(p(3), n0 % 2, H, T, 8).then_inc(panel_done, 1)
            pe.wait_ge(split_made, h * HP + (n0 + 2))
            begin(4)
            panel_mm(p(4), (n0 + 1) % 2, H, T, 8).then_inc(aux_done, 1)
            begin(5)
            panel_mm(p(5), (n0 + 1) % 2, HC, TC, 8).then_inc(panel_done, 1)

            def values(u, act, tiles, t0):
                begin(u)
                for pair in (((0, 2), (1, 3)) if tiles == 4 else ((0,), (1,))):
                    for parts in (((0, whi), (1, whi)), ((0, wlo),)):
                        if u == 8 and parts[0][1] is wlo:
                            pe.wait_ge(split_made, h * HP + (n0 + 4))
                        for t in pair:
                            for k in range(KT):
                                for a, w in parts:
                                    last = mm(p(u)[:, t * DV:(t + 1) * DV], operand(act, a, k, (t0 + t) * P, P),
                                              w[:, :, k, :], start=(k == 0 and a == 0 and w is whi),
                                              stop=(k == KT - 1 and w is wlo))
                return last

            pe.wait_ge(hi_made, h * HP + (n0 + 4))
            values(8, H, 4, 0).then_inc(aux_done, 1)
            values(9, H, 4, 4).then_inc(aux_done, 1)
            values(10, HC, 2, 0).then_inc(panel_done, 2)
            begin(11)
            pe.wait_ge(kdc_made, h + 1)
            for dr in range(2):
                for c in range(NCC):
                    last = nc.tensor.transpose(p(11)[:, dr * 512 + c * CH:dr * 512 + (c + 1) * CH],
                                               chunk(KDC[:, dr, :], c), ident)
            last.then_inc(aux_done, 1)
            for dr in range(2):
                begin(12 + dr)
                pe.wait_ge(qk_made, h * 4 + 2 * dr + 2)
                for c in range(NCH):
                    last = nc.tensor.transpose(chunk(p(12 + dr), c), chunk(KD[dr], c), ident)
                last.then_inc(aux_done, 1)
            for dr in range(2):
                begin(14 + dr)
                for c in range(NCH):
                    last = mm(chunk(p(14 + dr), c), chunk(KD[dr], c), chunk(QD[dr], c), start=True, stop=True)
                last.then_inc(aux_done, 1)
            for u in (10, 11):
                pe.wait_ge(evac[slot("heads", u)], evac_at(h, u))
            begin(16)
            for dr in range(2):
                for c in range(NCC):
                    last = mm(p(16)[:, dr * 512 + c * DV:dr * 512 + (c + 1) * DV], KDTC[:, dr, c, :], VC[:, c, :],
                              start=True, stop=True)
            last.then_inc(aux_done, 1)
            pe.wait_ge(evac[slot("heads", 12)], evac_at(h, 12))
            for u, dr, chunks in STATE_JOBS:
                begin(u)
                if u == 18:
                    pe.wait_ge(evac[slot("heads", 13)], evac_at(h, 13))
                for c in chunks:
                    last = mm(p(u)[:, (c % 4) * DV:(c % 4 + 1) * DV], KDT[dr][:, c, :], V[:, c, :],
                              start=True, stop=True)
                last.then_inc(aux_done, 1)

            def projection(u, n):
                pe.wait_ge(split_made, h * HP + (n0 + n + 1))
                begin(u)
                panel_mm(p(u), (n0 + n) % 2, H, T, 8).then_inc(panel_done, 1)

            projection(21, 4)
            projection(22, 5)
            pe.wait_ge(sco_made, h + 1)
            pe.wait_ge(state_made, h + 1)
            for e in range(2):
                begin(23 + e)
                for c in range(NCH):
                    o = chunk(p(23 + e), c)
                    mm(o, V[:, c, e * P:(e + 1) * P], chunk(SCO[0], c), start=True, stop=False)
                    mm(o, SR[0][:, c, e * P:(e + 1) * P], chunk(QD[0], c), start=False, stop=False)
                    last = mm(o, SR[1][:, c, e * P:(e + 1) * P], chunk(QD[1], c), start=False, stop=True)
                last.then_inc(aux_done, 1)
            projection(25, 6)
            begin(26)
            pe.wait_ge(osum, h + 1)
            for c in range(NCH):
                last = mm(p(26)[:, c:c + 1], chunk(TT[2], c), ones[:, 0:1], start=True, stop=True)
            last.then_inc(aux_done, 1)
            pe.wait_ge(split_made, h * HP + (n0 + HP))
            begin(27)
            panel_mm(p(27), (n0 + HP - 1) % 2, H, T, 8, part=range(KT // 2))
            pe.wait_ge(o_r, h + 1)
            for c in range(NCH):
                last = mm(chunk(p(26), c), nr[:, c:c + 1].to_broadcast([P, P]), ident, start=True, stop=True)
            last.then_inc(o_rb, 1)
            panel_mm(p(27), (n0 + HP - 1) % 2, H, T, 8, part=range(KT // 2, KT)).then_inc(panel_done, 1)

        def heads_act(act, h, ch):
            A_ = nc.scalar.activation
            inv = 1.0 / GATE_NORM

            def p(u):
                return ps[slot("heads", u)]

            def copied(u, out_, in_, **kw):
                A_(out_, in_, ACT.Copy, **kw).then_inc(evac[slot("heads", u)], 1)

            for u, t in ((0, TT[0]), (1, TT[2])):
                act.wait_ge(aux_done, aux_at(h, u + 1))
                steady(act)
                A_(t[:, :], p(u)[:, :], ACT.Abs, bias=vcol(("b_gf", "b_gb")[u], h)).then_inc(gate_abs, 1)
                act.wait_ge(gate_abs, h * 4 + u + 1)
                ch.link(A_(t[:, :], t[:, :], ACT.Exp, scale=-1.0))
                A_(t[:, :], t[:, :], ACT.Ln, bias=1.0).then_inc(gate_ln, 1)
            act.wait_ge(aux_done, aux_at(h, 3))
            steady(act)
            for u in range(2):
                A_(KDC[:, u, :], p(2)[:, u * 512:u * 512 + TC], ACT.Abs, bias=vcol(("b_gf", "b_gb")[u], h)
                   ).then_inc(gate_abs, 1)
            act.wait_ge(gate_abs, h * 4 + 4)
            ch.link(A_(KDC[:, :, :], KDC[:, :, :], ACT.Exp, scale=-1.0))
            A_(KDC[:, :, :], KDC[:, :, :], ACT.Ln, bias=1.0).then_inc(gate_ln, 1)
            act.wait_ge(panel_done, h * HP + (N0["heads"] + 1))
            copied(3, QT[:, :], p(3)[:, :], scale=DK ** -0.5)

            def swap(e, src):
                act.wait_ge(ga_out[e], h * 16 + 16)
                act.wait_ge(evac[slot("heads", 3 + e)], evac_at(h, 3 + e))
                for o in range(0, P, 64):
                    A_(ROT[e][o:o + 32, :], src[o + 32:o + 64, :], ACT.Copy)
                    i_ = A_(ROT[e][o + 32:o + 64, :], src[o:o + 32, :], ACT.Copy)
                i_.then_inc(swapped, 1)

            swap(0, QT)
            act.wait_ge(aux_done, aux_at(h, 4))
            act.wait_ge(on_out[1], h * 16 + 16)
            copied(4, KTt[:, :], p(4)[:, :])
            act.wait_ge(panel_done, h * HP + (N0["heads"] + 2))
            act.wait_ge(split_made, h * HP + V_PANEL)
            act.wait_ge(raw_in[V_PANEL % 2], h * (HP // 2 * 16) + (V_PANEL // 2 + 1) * 16)
            steady(act)
            A_(whi[:, V_PANEL % 2, :, :], wraw[:, V_PANEL % 2, :, :], ACT.Copy).then_inc(hi_made, 1)
            copied(5, KC[:, :], p(5)[:, 0:TC])
            act.wait_ge(dif_made, h * 4 + 1)
            A_(TT[1][:, :], TT[0][:, :], ACT.Exp, scale=inv).then_inc(exp_made, 1)
            A_(TT[2][:, :], TT[0][:, :], ACT.Exp, scale=-inv).then_inc(exp_made, 1)
            act.wait_ge(exp_made, h * 5 + 2)
            act.wait_ge(dif_made, h * 4 + 2)
            A_(TT[0][:, :], TT[3][:, :], ACT.Exp, scale=inv).then_inc(exp_made, 1)
            act.wait_ge(exp_made, h * 5 + 3)
            A_(TT[3][:, :], TT[3][:, :], ACT.Exp, scale=-inv).then_inc(exp_made, 1)
            act.wait_ge(dif_made, h * 4 + 3)
            A_(KDC[:, :, :], KDC[:, :, :], ACT.Exp, scale=-inv).then_inc(exp_made, 1)
            swap(1, KTt)
            act.wait_ge(dif_made, h * 4 + 4)
            for dr in range(2):
                mid, end = ((CH // 2 - 1, CH - 1), (CH // 2, 0))[dr]
                A_(col[dr][:, 10:18], BB[dr][:, mid::CH], ACT.Exp, scale=inv).then_inc(colexp, 1)
                A_(col[dr][:, 20:28], BB[dr][:, end::CH], ACT.Exp, scale=inv).then_inc(colexp, 1)
                A_(col[dr][:, 28:30], BBC[:, dr, end::CH], ACT.Exp, scale=inv).then_inc(colexp, 1)
                A_(col[dr][:, 30:40], dcol[dr][:, :], ACT.Exp, scale=inv).then_inc(colexp, 1)
            act.wait_ge(aux_done, aux_at(h, 5))
            act.wait_ge(x_spilled, 16)
            copied(8, V[:, 0:4, :].rearrange("p c v -> p (c v)"), p(8)[:, :])
            act.wait_ge(aux_done, aux_at(h, 6))
            copied(9, V[:, 4:8, :].rearrange("p c v -> p (c v)"), p(9)[:, :])
            act.wait_ge(panel_done, h * HP + (N0["heads"] + 4))
            copied(10, VC[:, :, :].rearrange("p c v -> p (c v)"), p(10)[:, 0:2 * DV])
            act.wait_ge(aux_done, aux_at(h, 7))
            copied(11, KDTC[:, :, :, :].rearrange("p a c k -> p a (c k)"),
                   p(11)[:, :].rearrange("p (a b) -> p a b", a=2)[:, :, 0:TC])
            for dr in range(2):
                act.wait_ge(aux_done, aux_at(h, 8 + dr))
                copied(12 + dr, KDT[dr][:, :, :].rearrange("p c k -> p (c k)"), p(12 + dr)[:, :])
            for u, dr, chunks in STATE_JOBS:
                act.wait_ge(aux_done, aux_at(h, u - 4))
                for c in chunks:
                    i_ = A_(SR[dr][:, c + (1, -1)[dr], :], p(u)[:, (c % 4) * DV:(c % 4 + 1) * DV], ACT.Copy,
                            scale=col[dr][:, 30 + c:31 + c])
                i_.then_inc(evac[slot("heads", u)], 1)
            for e in range(2):
                act.wait_ge(panel_done, h * HP + (N0["heads"] + 5 + e))
                A_(SZA[e][:, :], p(21 + e)[:, :], ACT.Silu).then_inc(evac[slot("heads", 21 + e)], 1)
            for e in range(2):
                act.wait_ge(aux_done, aux_at(h, 17 + e))
                if e == 0:
                    act.wait_ge(state_made, h + 1)
                A_(TT[2 + e][:, :], p(23 + e)[:, :], ACT.Square).then_inc(osq, 1)
                copied(23 + e, OE[e][:, :], p(23 + e)[:, :])

            def gate_a(e):
                u = 25 + 2 * e
                act.wait_ge(panel_done, h * HP + (N0["heads"] + 7 + e))
                A_(SGA[e][:, :], p(u)[:, :], ACT.Sigmoid).then_inc(evac[slot("heads", u)], 1)
                act.wait_ge(evac[slot("heads", u)], evac_at(h, u))
                act.dma_start(gad[ds(h * 2 + e, 1), :, :].rearrange("k p t -> (k p) t"), SGA[e][:, :]
                              ).then_inc(ga_out[e], 16)

            gate_a(0)
            act.wait_ge(o_var, h + 1)
            ch.link(A_(nr[:, 0:8], nv[:, 0:8], ACT.Ln))
            A_(nr[:, 0:8], nr[:, 0:8], ACT.Exp, scale=-0.5).then_inc(o_r0, 1)
            gate_a(1)

        HEAD_STEPS = 78
        HEAD_ACT_STEPS = 4

        def heads_dve(dve, h, ch):
            V_ = nc.vector

            def p(u):
                return ps[slot("heads", u)]

            def ev(u):
                return evac[slot("heads", u)]

            def by_chunk(t):
                return t.rearrange("p (c j) -> p c j", j=CH)

            def at_col(t, j):
                v = by_chunk(t)
                return v[:, :, j:j + 1].to_broadcast([P, v.shape[1], CH])

            dve.wait_ge(gate_abs, h * 4 + 1)
            V_.tensor_scalar(TT[1][:, :], p(0)[:, :], vcol("b_gf", h), 0.0, ALU.add, ALU.min).then_inc(ev(0), 1)
            dve.wait_ge(ev(0), evac_at(h, 0))
            dve.wait_ge(gate_ln, h * 3 + 1)
            ch.link(V_.tensor_tensor(TT[1][:, :], TT[1][:, :], TT[0][:, :], ALU.subtract))
            for c in range(NCH):
                ch.do(V_.tensor_tensor_scan(chunk(BB[0], c), ones, chunk(TT[1], c), 0.0, ALU.mult, ALU.add))
            dve.wait_ge(gate_abs, h * 4 + 2)
            V_.tensor_scalar(TT[3][:, :], p(1)[:, :], vcol("b_gb", h), 0.0, ALU.add, ALU.min).then_inc(ev(1), 1)
            dve.wait_ge(ev(1), evac_at(h, 1))
            dve.wait_ge(gate_ln, h * 3 + 2)
            ch.link(V_.tensor_tensor(TT[3][:, :], TT[3][:, :], TT[2][:, :], ALU.subtract))
            for c in range(NCH):
                ch.do(V_.tensor_tensor_scan(chunk(TT[2], c), ones, chunk(TT[3], c), 0.0, ALU.mult, ALU.add))
            ch.wait()
            ch.link(V_.tensor_tensor(TT[3][:, :], TT[3][:, :], TT[2][:, :], ALU.subtract))
            ch.link(V_.tensor_tensor(by_chunk(BB[1][:, :]), by_chunk(TT[3][:, :]), at_col(TT[2][:, :], CH - 1), ALU.add))
            dve.wait_ge(gate_abs, h * 4 + 4)
            for u in range(2):
                i_ = V_.tensor_scalar(BBC[:, u, :], p(2)[:, u * 512:u * 512 + TC], vcol(("b_gf", "b_gb")[u], h), 0.0,
                                      ALU.add, ALU.min)
                if u:
                    i_.then_inc(ev(2), 1)
            dve.wait_ge(ev(2), evac_at(h, 2))
            dve.wait_ge(gate_ln, h * 3 + 3)
            ch.link(V_.tensor_tensor(BBC[:, :, :], BBC[:, :, :], KDC[:, :, :], ALU.subtract))
            for u in range(2):
                for c in range(NCC):
                    ch.do(V_.tensor_tensor_scan(chunk(KDC[:, u, :], c), ones, chunk(BBC[:, u, :], c), 0.0,
                                                ALU.mult, ALU.add))
            ch.wait()
            ch.do(V_.tensor_copy(BBC[:, 0, :], KDC[:, 0, :]))
            ch.link(V_.tensor_tensor(BBC[:, 1, :], BBC[:, 1, :], KDC[:, 1, :], ALU.subtract))
            ch.link(V_.tensor_tensor(by_chunk(BBC[:, 1, :]), by_chunk(BBC[:, 1, :]), at_col(KDC[:, 1, :], CH - 1), ALU.add))
            mids = (CH // 2 - 1, CH // 2)
            ends = (CH - 1, 0)
            for dr, t in ((0, TT[0]), (1, TT[3])):
                ch.link(V_.tensor_tensor(by_chunk(t[:, :]), by_chunk(BB[dr][:, :]), at_col(BB[dr][:, :], mids[dr]),
                                         ALU.subtract))
                V_.tensor_scalar(t[:, :], t[:, :], CLAMP, -CLAMP, ALU.min, ALU.max).then_inc(dif_made, 1)
            for dr in range(2):
                ch.do(V_.tensor_tensor(by_chunk(KDC[:, dr, :]), by_chunk(BBC[:, dr, :]), at_col(BBC[:, dr, :], mids[dr]),
                                       ALU.subtract))
            ch.wait()
            V_.tensor_scalar(KDC[:, :, :], KDC[:, :, :], CLAMP, -CLAMP, ALU.min, ALU.max).then_inc(dif_made, 1)
            for dr in range(2):
                ch.do(V_.tensor_tensor(dcol[dr][:, 0:8], BB[dr][:, ends[dr]::CH], BB[dr][:, mids[dr]::CH], ALU.subtract))
                i_ = V_.tensor_tensor(dcol[dr][:, 8:10], BBC[:, dr, ends[dr]::CH], BBC[:, dr, mids[dr]::CH], ALU.subtract)
                if dr == 0:
                    ch.do(i_)
                else:
                    i_.then_inc(dif_made, 1)
            def rotate(u, t, e):
                tmp = ROT[e]
                dve.wait_ge(swapped, h * 2 + (e + 1))
                V_.tensor_tensor(tmp[:, :], tmp[:, :], SIN[:, :], ALU.mult).then_inc(ev(u), 1)
                ch.link(V_.tensor_tensor(t[:, :], t[:, :], COS[:, :], ALU.mult))
                dve.wait_ge(ev(u), evac_at(h, u))
                ch.link(V_.tensor_tensor(t[:, :], t[:, :], tmp[:, :], ALU.add))

            dve.wait_ge(exp_made, h * 5 + 5)
            dve.wait_ge(ev(5), evac_at(h, 5))
            ch.link(V_.tensor_tensor(KDC[:, 0, :], KDC[:, 0, :], KC[:, :], ALU.mult))
            V_.tensor_tensor(KDC[:, 1, :], KDC[:, 1, :], KC[:, :], ALU.mult).then_inc(kdc_made, 1)
            dve.wait_ge(rot_in, 32)
            rotate(6, QT, 0)
            V_.tensor_tensor(QD[0][:, :], QT[:, :], TT[1][:, :], ALU.mult).then_inc(qk_made, 1)
            rotate(7, KTt, 1)
            dve.wait_ge(on_out[0], h * 16 + 16)
            V_.tensor_tensor(KD[0][:, :], KTt[:, :], TT[2][:, :], ALU.mult).then_inc(qk_made, 1)
            dve.wait_ge(qk_made, h * 4 + 2)
            V_.tensor_tensor(QD[1][:, :], QT[:, :], TT[0][:, :], ALU.mult).then_inc(qk_made, 1)
            V_.tensor_tensor(KD[1][:, :], KTt[:, :], TT[3][:, :], ALU.mult).then_inc(qk_made, 1)
            masks = [cc(m).unsqueeze(1).to_broadcast([P, NCH, CH]) for m in ("mask_f", "mask_b")]
            dve.wait_ge(qk_made, h * 4 + 4)
            for dr in range(2):
                dve.wait_ge(aux_done, aux_at(h, 10 + dr))
                V_.tensor_tensor(by_chunk(SCO[dr][:, :]), by_chunk(p(14 + dr)[:, :]), masks[dr], ALU.mult
                                 ).then_inc(ev(14 + dr), 1)
                dve.wait_ge(ev(14 + dr), evac_at(h, 14 + dr))
            V_.tensor_tensor(SCO[0][:, :], SCO[0][:, :], SCO[1][:, :], ALU.add).then_inc(sco_made, 1)
            dve.wait_ge(colexp, h * 8 + 8)
            dve.wait_ge(aux_done, aux_at(h, 12))
            for dr in range(2):
                S_, cl, tmp = SS[dr], col[dr], TT[2 + dr][:, 0:DV]
                for q, c in enumerate(((0, 1), (1, 0))[dr]):
                    U = p(16)[:, dr * 512 + c * DV:dr * 512 + (c + 1) * DV]
                    if q == 0:
                        ch.link(V_.tensor_scalar(S_[:, :], U, cl[:, 38 + c:39 + c], None, ALU.mult))
                    else:
                        i_ = V_.tensor_scalar(tmp, U, cl[:, 38 + c:39 + c], None, ALU.mult)
                        if dr:
                            i_.then_inc(ev(16), 1)
                            dve.wait_ge(ev(16), evac_at(h, 16))
                        else:
                            ch.link(i_)
                        ch.link(V_.scalar_tensor_tensor(out=S_[:, :], in0=S_[:, :], scalar=cl[:, 28 + c:29 + c], in1=tmp,
                                                        op0=ALU.mult, op1=ALU.add))
            for q in range(NCH):
                for dr in range(2):
                    c = (q, NCH - 1 - q)[dr]
                    if q:
                        ch.wait(1)
                    i_ = V_.tensor_scalar(SR[dr][:, c, :], SS[dr][:, :], col[dr][:, 10 + c:11 + c], None, ALU.mult)
                    if q == NCH - 1 and dr == 1:
                        i_.then_inc(state_made, 1)
                    else:
                        ch.do(i_)
                if q == NCH - 1:
                    break
                for dr in range(2):
                    c = (q, NCH - 1 - q)[dr]
                    for u, d_, chunks in STATE_JOBS:
                        if d_ == dr and c in chunks:
                            dve.wait_ge(ev(u), evac_at(h, u))
                    ch.wait(1)
                    ch.do(V_.scalar_tensor_tensor(out=SS[dr][:, :], in0=SS[dr][:, :], scalar=col[dr][:, 20 + c:21 + c],
                                                  in1=SR[dr][:, c + (1, -1)[dr], :], op0=ALU.mult, op1=ALU.add))
            ch.wait()
            dve.wait_ge(osq, h * 2 + 2)
            V_.tensor_tensor(TT[2][:, :], TT[2][:, :], TT[3][:, :], ALU.add).then_inc(osum, 1)
            dve.wait_ge(aux_done, aux_at(h, 19))
            v, r, q = nv[:, 0:8], nr[:, 0:8], nq[:, 0:8]
            V_.tensor_scalar(v, p(26)[:, 0:8], 1.0 / DV, EPS, ALU.mult, ALU.add).then_inc(o_var, 1)
            dve.wait_ge(o_r0, h + 1)
            ch.link(V_.tensor_tensor(q, r, r, ALU.mult))
            ch.link(V_.tensor_tensor(q, q, v, ALU.mult))
            ch.link(V_.tensor_scalar(q, q, -0.5, 1.5, ALU.mult, ALU.add))
            V_.tensor_tensor(r, r, q, ALU.mult).then_inc(o_r, 1)
            dve.wait_ge(o_rb, h + 1)
            for e in range(2):
                dve.wait_ge(ev(23 + e), evac_at(h, 23 + e))
                i_ = V_.scalar_tensor_tensor(out=OE[e][:, :], in0=OE[e][:, :],
                                             scalar=vec[:, VEC["gla_g"] + e:VEC["gla_g"] + e + 1],
                                             in1=p(26)[:, :], op0=ALU.mult, op1=ALU.mult)
                if e:
                    i_.then_inc(ev(26), 1)
                    dve.wait_ge(ev(26), evac_at(h, 26))
                else:
                    ch.link(i_)
                dve.wait_ge(ev(21 + e), evac_at(h, 21 + e))
                V_.tensor_tensor(OE[e][:, :], OE[e][:, :], SZA[e][:, :], ALU.mult).then_inc(on_made, 1)

        block = ctx.enter_context(nc.Block())

        @block.sync
        def _(sp):
            for t, n in ((feat, "feat"), (fw1, "fw1")):
                sp.dma_start(t[:, :], d[n]).then_inc(feat_in, 16)

            skipped = 0

            def panel(n, s):
                sp.dma_start(wraw[:, s, :, :], d["panels"][ds(n - skipped, 1), :, :].rearrange("a p (k m) -> (a p) k m", k=8)
                             ).then_inc(raw_in[s], 16)

            panel(0, 0)
            sp.dma_start(vec[:, :], d["vec"]).then_inc(vec_in, 16)
            xv = d["xT"].rearrange("(k p) t -> p k t", p=P)
            for k in range(4):
                sp.dma_start(X[:, 2 * k:2 * k + 2, :], xv[:, 2 * k:2 * k + 2, :]).then_inc(x_in[k], 16)
            panel(1, 1)
            sp.dma_start(cst[:, :], d["cst"]).then_inc(const_in, 16)
            for t, n in ((fw2, "fw2"), (fw3, "fw3")):
                sp.dma_start(t[:, :], d[n]).then_inc(filt_in, 16)

            def panels(lo, hi):
                assert lo >= 2 and (hi - lo) % 2 == 0
                with sp.Fori(0, (hi - lo) // 2) as i:
                    for u in range(2):
                        n = lo + u + i * 2
                        sp.wait_ge(split_made, n - 1)
                        panel(n, (lo + u) % 2)

            def modp(f, m):
                sp.dma_start(mw[m][:, :], d["modp"][ds(f, 1), :, :].rearrange("a p k -> (a p) k")).then_inc(mod_in[m], 16)

            panels(2, 4)
            sp.wait_ge(n1.lo, KT)
            sp.wait_ge(n1.acc, KT + 2)
            for t, n in ((wtap, "wtap"), (dec, "dec")):
                sp.dma_start(t[:, :], d[n]).then_inc(filt_in, 16)
            sp.dma_start(crep[:, :], d["cvec"].to_broadcast([P, 2 * D])).then_inc(filt_in, 16)
            for m in range(4):
                modp(m, m)
            panels(4, 6)
            with sp.Fori(0, 5) as i:
                for u in range(2):
                    sp.wait_ge(split_made, i * 2 + (u + 5))
                    panel(i * 2 + (u + 6), u)
                    for j in range(2):
                        m = 2 * u + j
                        sp.wait_ge(mod_used, i * 4 + (m + 1))
                        modp(i * 4 + (m + 4), m)
            panels(16, 24)
            g1r = g1.rearrange("p n t -> (p n) t")
            s1r = s1.rearrange("p n t -> (p n) t")

            def filter_rows(g):
                n = N0["spec"] + g
                sp.wait_ge(split_made, n - 1)
                sp.dma_start(wraw[:, n % 2, :, :].rearrange("p k m -> p (k m)"), g1r[g * P:(g + 1) * P, :]
                             ).then_inc(raw_in[n % 2], 16)

            def matrices(g):
                if g >= 3:
                    sp.wait_ge(spec_inv, 2 * g - 4)
                sp.dma_start(kf[g % 3][:, :, :].rearrange("p a m -> p (a m)"), d["kfft"][g, :, :]).then_inc(kg_in[g % 3], 16)

            for u in range(2):
                sp.wait_ge(g1_out[u], 16 * (N2 // 2 + 1))
            for g in range(2):
                filter_rows(g)
            sp.wait_ge(tap_sum, N2)
            for g in range(2):
                matrices(g)
            with sp.Fori(0, N2 // 2) as i:
                for u in range(2):
                    s = slot("sfwd", 2 + u)
                    sp.wait_ge(evac[s], turn("sfwd", 2 + u, i, 4) + 1)
                    sp.dma_start(s1[:, ds(i * 2 + u, 1), :], sa[u][:, :].unsqueeze(1)).then_inc(s1_out[u], 16)
            for u in range(2):
                sp.wait_ge(s1_out[u], 16 * (N2 // 2 + 1))
            for g in range(GROUPS):
                if g >= 2:
                    filter_rows(g)
                    sp.wait_ge(spec_lo, rows_made(2 * g - 3))
                sp.dma_start(bs[g % 2][:, :], s1r[g * P:(g + 1) * P, :]).then_inc(spec_in[g % 2], 16)
                if g >= 2:
                    matrices(g)
            skipped = GROUPS
            panels(N0["wout"], N0["wout"] + 2)
            sp.wait_ge(ended["pe"], 1)
            sp.wait_ge(ended["act"], 1)
            sp.wait_ge(ended["dve"], 1)
            sp.dma_start(X[:, :, :], xv).then_inc(xr_in, 16)
            panels(N0["wout"] + 2, N0["up2"] + 2)
            sp.wait_ge(panel_done, N0["up2"])
            sp.dma_start(CX[:, :, :], d["ctxT"].rearrange("(k p) t -> p k t", p=P)).then_inc(cx_in, 16)
            panels(N0["up2"] + 2, N0["lrx"])
            sp.wait_ge(aux_done, A0["mix"] + 32)
            sp.dma_start(wup_h[:, :], d["wup"][:, 0:DK]).then_inc(wup_in, 16)
            n = N0["lrx"]
            for q in range(2):
                sp.wait_ge(split_made, n + q - 1)
                panel(n + q, (n + q) % 2)
            sp.wait_ge(panel_done, n)
            sp.dma_start(COS[:, :], d["cos"]).then_inc(rot_in, 16)
            n = N0["heads"] + 1
            xsv = xs.rearrange("(k p) t -> p k t", p=P)
            def head_stores(h):
                sp.wait_ge(aux_done, aux_at(h, 3))
                sp.dma_start(wup_h[:, :], d["wup"][:, ds(h * DK + DK, DK)]).then_inc(wup_in, 16)
                for e in range(2):
                    sp.wait_ge(on_made, h * 2 + (e + 1))
                    sp.dma_start(ond[ds(h * 2 + e, 1), :, :].rearrange("k p t -> (k p) t"), OE[e][:, :]
                                 ).then_inc(on_out[e], 16)

            for u in range(HP):
                sp.wait_ge(split_made, n + u - 1)
                panel(n + u, (n + u) % 2)
                if u == 2:
                    sp.wait_ge(nf1.h, KT)
                    sp.dma_start(xsv, X[:, :, :]).then_inc(x_spilled, 16)
                    sp.wait_ge(x_spilled, 16)
                    sp.dma_start(SIN[:, :], d["sin"]).then_inc(rot_in, 16)
            head_stores(0)
            with sp.Fori(1, HEADS - 1) as h:
                for u in range(HP):
                    sp.wait_ge(split_made, h * HP + (n + u - 1))
                    panel(h * HP + (n + u), (n + u) % 2)
                head_stores(h)
            n += HP * (HEADS - 1)
            panels(n, n + HP)
            n += HP
            sp.wait_ge(split_made, n - 1)
            panel(n, n % 2)
            sp.wait_ge(aux_done, aux_at(HEADS, 0))
            sp.wait_ge(on_out[0], 16 * 4)
            sp.wait_ge(on_out[1], 16 * 4)
            for q in range(4):
                sp.dma_start(TT[q][:, :], ond[O_ORDER[q], :, :]).then_inc(on_in[q], 16)
            panels(n + 1, NPANELS)

        @block.gpsimd
        def _(pool):
            for s in range(2):
                pool.wait_ge(raw_in[s], 16)
                nc.gpsimd.tensor_copy(whi[:, s, :, :], wraw[:, s, :, :]).then_inc(hi_made, 1)
                pool.wait_ge(hi_made, s + 1)
                nc.gpsimd.tensor_tensor(wlo[:, s, :, :], wraw[:, s, :, :], whi[:, s, :, :].bitcast(F32), ALU.subtract
                                        ).then_inc(split_made, 1)

            def pair(i, quick=False):
                for s in range(2):
                    pool.wait_ge(raw_in[s], i * 16 + 16)
                    pool.wait_ge(panel_done, i * 2 + s - 1)
                    steady(pool)
                    if not (quick and s == 0):
                        nc.gpsimd.tensor_copy(whi[:, s, :, :], wraw[:, s, :, :]).then_inc(hi_made, 1)
                    pool.wait_ge(hi_made, i * 2 + s + 1)
                    nc.gpsimd.tensor_tensor(wlo[:, s, :, :], wraw[:, s, :, :], whi[:, s, :, :].bitcast(F32),
                                            ALU.subtract).then_inc(split_made, 1)

            def rest(pairs_lo, pairs_hi):
                with pool.Fori(pairs_lo, pairs_hi) as i:
                    pair(i)

            rest(1, V_PANEL // 2)
            with pool.Fori(0, HEADS) as h:
                for q in range(HP // 2):
                    pair(h * (HP // 2) + (V_PANEL // 2 + q), quick=(q == 0))
            rest(V_PANEL // 2 + HEADS * HP // 2, NPANELS // 2)
            if NPANELS % 2:
                n = NPANELS - 1
                pool.wait_ge(raw_in[0], (n // 2 + 1) * 16)
                pool.wait_ge(panel_done, n - 1)
                nc.gpsimd.tensor_copy(whi[:, 0, :, :], wraw[:, 0, :, :]).then_inc(hi_made, 1)
                pool.wait_ge(hi_made, n + 1)
                nc.gpsimd.tensor_tensor(wlo[:, 0, :, :], wraw[:, 0, :, :], whi[:, 0, :, :].bitcast(F32), ALU.subtract
                                        ).then_inc(split_made, 1)

        @block.tensor
        def _(pe):
            mm = nc.tensor.matmul

            def free(phase, u, i=0, per=0):
                q = turn(phase, u, i, per)
                if not (isinstance(q, int) and q == 0):
                    pe.wait_ge(evac[slot(phase, u)], q)

            def panel_mm(p, ws, act, width, nk, ready=None, order=range(KT), part=range(KT)):
                last = None
                step = min(512, width)
                for q, k in enumerate(order[:nk]):
                    if q not in part:
                        continue
                    if ready is not None:
                        pe.wait_ge(ready[0], ready[1] + q + 1)
                    for w, a in ((whi, 0), (whi, 1), (wlo, 0)):
                        for c in range(width // step):
                            last = mm(p[:, c * step:(c + 1) * step], w[:, ws, k, :],
                                      operand(act, a, k, c * step, step),
start=(q == 0 and w is whi and a == 0), stop=(q == nk - 1 and w is wlo))
                return last

            def panel_jobs(phase, trips, act, nk=8, ready=None, per=4, order=range(KT)):
                n0 = N0[phase]
                with pe.Fori(0, trips) as i:
                    for u in range(per):
                        pe.wait_ge(split_made, i * per + (n0 + u + 1))
                        free(phase, u, i, per)
                        panel_mm(ps[slot(phase, u)], (n0 + u) % 2, act, T, nk, ready, order).then_inc(panel_done, 1)

            def norm_sums(phase, *accs, width=T):
                free(phase, 0)
                j = 0
                for acc, n, full in accs:
                    pe.wait_ge(n.acc, full)
                    for c in range(width // P):
                        last = mm(ps[slot(phase, 0)][:, j:j + 1], acc[:, c * P:(c + 1) * P], ones[:, 0:1],
                                  start=True, stop=True)
                        j += 1
                last.then_inc(aux_done, 1)

            def norm_spread(phase, n, r, width=T):
                pe.wait_ge(n.r, 1)
                for c in range(width // P):
                    last = mm(ps[slot(phase, 0)][:, c * P:(c + 1) * P], r[:, c:c + 1].to_broadcast([P, P]), ident,
                              start=True, stop=True)
                last.then_inc(n.rb, 1)

            def mlp(phase, u, w, src, ready):
                free(phase, u)
                pe.wait_ge(*ready)
                for c in range(2):
                    last = mm(ps[slot(phase, u)][:, c * 512:(c + 1) * 512], w[:, :], src[:, c * 512:(c + 1) * 512],
                              start=True, stop=True)
                last.then_inc(aux_done, 1)

            mlp("mlp0", 0, fw1, feat, (feat_in, 32))

            def project(phase, u, ready=None):
                n = N0[phase] + u
                pe.wait_ge(split_made, n + 1)
                free(phase, u)
                panel_mm(ps[slot(phase, u)], n % 2, H, T, 8, ready).then_inc(panel_done, 1)

            project("zin0", 0, (n1.lo, 0))
            pe.wait_ge(const_in, 16)
            norm_sums("norm1", (TT[2], n1, KT + 2))
            project("zin1", 0)
            norm_spread("norm1", n1, nr)
            pe.wait_ge(filt_in, 80)
            mlp("mlp1", 0, fw2, fh, (sin_made, 1))
            project("zin2", 0)
            mlp("mlp2", 0, fw3, fh, (sin_made, 2))
            project("zin3", 0)
            panel_jobs("zin4", 3, H)
            with pe.Fori(0, 2) as i:
                for q in range(4):
                    o, g = 5 * q, i * 4 + q

                    def begin(u):
                        free("mix", o + u, i, 20)
                        return ps[slot("mix", o + u)]

                    pe.wait_ge(split_made, g + (N0["mix"] + 1))
                    panel_mm(begin(0), (N0["mix"] + q) % 2, H, T, 8).then_inc(panel_done, 1)
                    for u in range(2):
                        p = begin(1 + u)
                        pe.wait_ge(hbs_made, g * 2 + (u + 1))
                        for c in range(2):
                            last = mm(p[:, c * 512:(c + 1) * 512], hbs[u][:, :], wtap[:, c * 512:(c + 1) * 512],
                                      start=True, stop=True)
                        last.then_inc(aux_done, 1)
                    for u in range(2):
                        p = begin(3 + u)
                        pe.wait_ge(evac[slot("mix", o + 1 + u)], turn("mix", o + 1 + u, i, 20) + 1)
                        for c in range(2):
                            last = mm(p[:, c * 512:(c + 1) * 512], cc("dft_g"), tap[u][:, c * 512:(c + 1) * 512],
                                      start=True, stop=True)
                        last.then_inc(aux_done, 1)
            with pe.Fori(0, N2 // 2) as i:
                for u in range(2):
                    free("sfwd", u, i, 4)
                    pe.wait_ge(sn_made, i * 2 + u + 1)
                    steady(pe)
                    for e in range(KT):
                        last = nc.tensor.transpose(ps[slot("sfwd", u)][0:HALF, e * P:(e + 1) * P], sn[u][:, e, :], ident)
                    last.then_inc(aux_done, 1)
                for u in range(2):
                    free("sfwd", 2 + u, i, 4)
                    pe.wait_ge(evac[slot("sfwd", u)], turn("sfwd", u, i, 4) + 1)
                    for c in range(2):
                        last = mm(ps[slot("sfwd", 2 + u)][:, c * 512:(c + 1) * 512], cc("dft_s", HALF),
                                  st_[u][:, c * 512:(c + 1) * 512], start=True, stop=True)
                    last.then_inc(aux_done, 1)
            free("tapnorm", 0)
            pe.wait_ge(tap_sum, N2)
            for e in range(KT):
                last = mm(ps[slot("tapnorm", 0)][:, e:e + 1], gacc[:, e * P:(e + 1) * P], ones[:, 0:1],
                          start=True, stop=True)
            last.then_inc(aux_done, 1)
            for u in range(N2 * 2 - 3, N2 * 2):
                pe.wait_ge(evac[slot("sfwd", u)], turn("sfwd", u) + 1)
            pe.wait_ge(evac[slot("tapnorm", 0)], turn("tapnorm", 0) + 1)
            def bank(c, b):
                s = 2 * c + b // 2
                return ps[s][:, (b % 2) * 512:(b % 2) * 512 + 512]

            def inverse(n):
                g, c = n // 2, n % 2
                if n >= 2:
                    pe.wait_ge(spec_ev, n - 1)
                for q, (m, src) in enumerate(((3, ya), (4, yb))):
                    pe.wait_ge(spec_y, 2 * n + q + 1)
                    last = mm(bank(c, 3), kf[g % 3][:, m, :], src[c][:, :], start=(q == 0), stop=(q == 1))
                    if c == 0 and q == 0:
                        last.then_inc(panel_done, 1)
                last.then_inc(spec_inv, 1)

            def three(bank_, g, m, hi, lo):
                mm(bank_, kh[g % 2][:, m, :], hi, start=True, stop=False)
                mm(bank_, kh[g % 2][:, m, :], lo, start=False, stop=False)
                return mm(bank_, kl[g % 2][:, m, :], hi, start=False, stop=True)

            def filter_spectra(n):
                g, c = n // 2, n % 2
                if c == 0:
                    pe.wait_ge(spec_lo, mats_made(g))
                    pe.wait_ge(split_made, N0["spec"] + g + 1)
                if n >= 2:
                    pe.wait_ge(spec_g, 2 * n - 2)
                w = (N0["spec"] + g) % 2
                hi, lo = (t[:, w, 4 * c:4 * c + 4, :].rearrange("p k m -> p (k m)") for t in (whi, wlo))
                for m, b in ((1, 1), (2, 2)):
                    three(bank(c, b), g, m, hi, lo).then_inc(spec_gm, 1)

            filter_spectra(0)
            filter_spectra(1)
            for n in range(2 * GROUPS):
                g, c = n // 2, n % 2
                if n >= 2:
                    filter_spectra(n)
                pe.wait_ge(spec_lo, rows_made(n))
                three(bank(c, 0), g, 0, bh[c][:, :], bl[c][:, :]).then_inc(spec_xm, 1)
                if n:
                    inverse(n - 1)
            inverse(2 * GROUPS - 1)
            pe.drain().then_inc(ended["pe"], 1)
            pe.wait_ge(spec_ev, 2 * GROUPS)
            for o, (kind, *j) in enumerate(INV):
                p = ps[slot("inv", o)]
                free("inv", o)
                if kind == "rows":
                    c0, w, m0 = j
                    if m0 == 0:
                        pe.wait_ge(yb_in[c0 // 512], 16 * GROUPS)
                    for u in range(T // w):
                        last = mm(p[0:HALF, u * w:(u + 1) * w], cc("idft"), YB[:, m0 + u, c0:c0 + w], start=True, stop=True)
                else:
                    e, q = j[0], inv_rows(j[0])
                    pe.wait_ge(evac[slot("inv", q)], turn("inv", q) + 1)
                    for m in range(N2):
                        last = nc.tensor.transpose(p[:, m * HALF:(m + 1) * HALF], YB[0:HALF, m, e * P:(e + 1) * P],
                                                   ident[0:HALF, 0:HALF])
                last.then_inc(aux_done, 1)
            panel_jobs("wout", 2, A, ready=(y_lo, 0))
            project("first", 0, (n2.lo, 0))
            norm_sums("norm2", (TT[2], n2, KT + 2))
            project("second", 0)
            norm_spread("norm2", n2, nr)
            for u in range(1, 3):
                project("second", u)
            f0 = 0
            for p, nf in enumerate(FPARTS):
                for u, (up_, trips) in enumerate(UPS[p]):
                    panel_jobs(up_, trips, H)
                    if len(UPS[p]) > 1:
                        if u == 0:
                            norm_sums("normc", (cxacc, ncx, KT + 2), width=TC)
                        else:
                            free("normcb", 0)
                            norm_spread("normcb", ncx, cr, TC)
                panel_jobs(f"down{p}", 2, A, nk=nf, ready=(ff_lo, f0))
                f0 += nf
            norm_sums("normf", (TT[2], nf1, KT + 1), (TT[3], n3, KT + 1))
            pe.wait_ge(split_made, N0["lrx"] + 1)
            free("lr", 0)
            ws = N0["lrx"] % 2
            pe.wait_ge(ncx.lo, KT)
            panel_mm(ps[slot("lr", 0)], ws, HC, TC, 8).then_inc(aux_done, 1)
            free("norm3", 0)
            norm_spread("norm3", n3, nr[:, 8:16])
            norm_spread("normf", nf1, nr[:, 0:8])
            free("lrx", 0)
            panel_mm(ps[slot("lrx", 0)], ws, H, T, 8, (n3.lo, 0)).then_inc(panel_done, 1)
            for q in ("lr", "lrx"):
                pe.wait_ge(evac[slot(q, 0)], turn(q, 0) + 1)
            with pe.Fori(0, HEADS) as h:
                heads_pe(pe, h, free, panel_mm)
            panel_jobs("mixa", 2, A, ready=(za_lo, 0), order=O_ORDER)
            for g in range(4):
                for u in range(4):
                    n = N0["pool"] + 4 * g + u
                    pe.wait_ge(split_made, n + 1)
                    free("pool", 6 * g + u)
                    panel_mm(ps[slot("pool", 6 * g + u)], n % 2, H, T, 8).then_inc(panel_done, 1)
                pe.wait_ge(pool_in, 32 * (g + 1))
                for m in range(2):
                    free("pool", 6 * g + 4 + m)
                    for k in range(2):
                        pe.wait_ge(pd_made, 2 * g + k + 1)
                        for c in range(2):
                            last = mm(ps[slot("pool", 6 * g + 4 + m)][:, c * 512:(c + 1) * 512],
                                      wpl[:, k, m * P:(m + 1) * P], pd[k][:, c * 512:(c + 1) * 512],
                                      start=(k == 0), stop=(k == 1))
                    last.then_inc(aux_done, 1)
            panel_jobs("gb", 2, H)
            panel_jobs("mixb", 2, A, ready=(pb_lo, 0))
            panel_jobs("wout2", 2, H, ready=(m_lo, 0))
            norm_sums("norm4", (TT[2], n4, KT + 2))
            norm_spread("norm4", n4, nr)

        @block.scalar
        def _(act):
            A_ = nc.scalar.activation
            ch = Steps(act, act_chain)

            def square(n, src, k, ring=TT):
                act.wait_ge(n.acc, k + 1)
                A_(ring[k % 2][:, :], src, ACT.Square).then_inc(n.sq, 1)

            def rsqrt(n, w=8, v=nv, r=nr):
                act.wait_ge(n.var, 1)
                ch.link(A_(r[:, 0:w], v[:, 0:w], ACT.Ln))
                A_(r[:, 0:w], r[:, 0:w], ACT.Exp, scale=-0.5).then_inc(n.r0, 1)

            def norm_hi(n, hi, shift, ring=TT):
                for k in range(KT):
                    act.wait_ge(n.h, k + 1)
                    A_(hi(k), ring[k % 2][:, :], ACT.Identity, bias=shift(k)).then_inc(n.hi, 1)

            def h_hi(k):
                return H[:, 0, k, :]

            def gained_hi(n, src, dst, gain):
                A_(dst, src, ACT.Copy, scale=gain).then_inc(n.hi, 1)

            act.wait_ge(vec_in, 16)
            for k in range(KT):
                act.wait_ge(x_in[k // 2], 16)
                gained_hi(n1, X[:, k, :], H[:, 0, k, :], vcol("norm_mix", k))
                square(n1, X[:, k, :], k)
            rsqrt(n1)

            def sine(l):
                act.wait_ge(arg_made, l + 1)
                if l:
                    act.wait_ge(aux_done, A0["mlp1"] + 1)
                A_(fh[:, :], fu[:, :], ACT.Sin).then_inc(sin_made, 1)

            def middle(slot_, count, n, t, f):
                act.wait_ge(evac[slot_], count)
                steady(act)
                A_(t[:, :], zp[:, 1:T + 1], ACT.Identity, scale=vcol("cw1", f), bias=vcol("cb", f)).then_inc(c_made, 1)

            def first_z(phase, n, f):
                middle(slot(phase, 0), turn(phase, 0) + 1, n, (ca, cb_)[n % 2], f)

            sine(0)
            act.wait_ge(n1.rb, 1)
            A_(R1[:, :], ps[slot("norm1", 0)][:, :], ACT.Copy).then_inc(evac[slot("norm1", 0)], 1)
            act.wait_ge(filt_in, 80)
            ch.link(A_(dec[:, :], dec[:, :], ACT.Abs))
            for u in range(2):
                act.sem_inc(g1_out[u], 16)
                act.sem_inc(s1_out[u], 16)
            first_z("zin0", 0, 8)
            sine(1)
            first_z("zin1", 1, 16)
            act.wait_ge(arg_made, 3)
            ch.link(A_(hb[:, :, :].rearrange("p a b -> p (a b)"), fu[:, :], ACT.Sin))
            A_(crep[:, :], crep[:, :], ACT.Silu).then_inc(silu_c, 1)
            first_z("zin2", 2, 9)
            first_z("zin3", 3, 17)
            with act.Fori(0, 3) as i:
                for u in range(4):
                    middle(slot("zin4", u), turn("zin4", u, i, 4) + 1, i * 4 + u, (ca, cb_)[u % 2],
                           i * 2 + (10 + 8 * (u % 2) + u // 2))

            def decays(n2, u):
                for r in (0, HALF):
                    i_ = A_(hbs[u][r:r + HALF, r:r + HALF], hb[r:r + HALF, ds(n2, 1), :].rearrange("p a b -> p (a b)"),
                            ACT.Copy)
                i_.then_inc(hbs_made, 1)
                A_(tap[u][:, :], dec[:, :], ACT.Exp, scale=cst[:, ds(n2 + CST["tneg"], 1)],
                   bias=cst[:, ds(n2 + CST["tmask"], 1)]).then_inc(decay_made, 1)

            act.wait_ge(const_in, 16)
            act.wait_ge(hb_zero, 1)
            for u in range(2):
                decays(u, u)
            act.wait_ge(mod_used, 24)

            Sv = S[:, :, :].rearrange("p k (a b) -> p k a b", b=N2)

            def gather(n, u):
                A_(sn[u][:, :, :], Sv[:, :, :, ds(n, 1)].rearrange("p k a b -> p k (a b)"), ACT.Copy
                   ).then_inc(sn_made, 1)

            def mixed(i, steps, tail):
                for q in steps:
                    o, g = 5 * q, i * 4 + q
                    middle(slot("mix", o), turn("mix", o, i, 20) + 1, g, ca, g)
                    if q in tail:
                        act.wait_ge(s_made, KT)
                        gather(0, 0)
                        gather(1, 1)
                    for u in range(2):
                        s = slot("mix", o + 3 + u)
                        act.wait_ge(aux_done, i * 16 + (A0["mix"] + 4 * q + 3 + u))
                        act.wait_ge(g1_out[u], g * 16 + 16)
                        A_(gsp[u][:, :], ps[s][:, :], ACT.Copy).then_inc(evac[s], 1)
                        act.wait_ge(evac[s], turn("mix", o + 3 + u, i, 20) + 1)
                        act.dma_start(g1[:, ds(g * 2 + u, 1), :], gsp[u][:, :].unsqueeze(1)).then_inc(g1_out[u], 16)
                        if q not in tail:
                            act.wait_ge(tap_sum, g * 2 + (u + 1))
                            steady(act)
                            decays(g * 2 + (u + 2), u)

            mixed(0, range(4), ())
            mixed(1, range(4), (3,))

            def transposed(i):
                for u in range(2):
                    act.wait_ge(aux_done, i * 4 + (A0["sfwd"] + 1 + u))
                    A_(st_[u][:, :], ps[slot("sfwd", u)][0:HALF, :], ACT.Copy).then_inc(evac[slot("sfwd", u)], 1)

            with act.Fori(0, N2 // 2 - 1) as i:
                transposed(i)
                for u in range(2):
                    gather(i * 2 + u + 2, u)
            transposed(N2 // 2 - 1)

            def spec_inverse(n):
                c = n % 2
                act.wait_ge(spec_inv, n + 1)
                if n >= 2:
                    act.wait_ge(yb_in[c], 16 * (n // 2))
                A_(yi[c][:, :], ps[2 * c + 1][:, 512:1024], ACT.Copy).then_inc(spec_ev, 1)
                act.wait_ge(spec_ev, n + 1)
                act.dma_start(YB[8 * (n // 2):8 * (n // 2) + 8, :, 512 * c:512 * c + 512], yi[c][:, :]
                              ).then_inc(yb_in[c], 16)

            def mats_hi(g):
                act.wait_ge(kg_in[g % 3], 16 * 6 + 16 * (g // 3 + 1))
                if g >= 2:
                    act.wait_ge(spec_xm, 2 * g - 2)
                A_(kh[g % 2][:, :, :], kf[g % 3][:, 0:3, :], ACT.Copy).then_inc(spec_hi, 1)

            def rows_hi(n):
                g, c = n // 2, n % 2
                act.wait_ge(spec_in[g % 2], 16 * (g // 2 + 1))
                if n >= 2:
                    act.wait_ge(spec_xm, n - 1)
                A_(bh[c][:, :], bs[g % 2][:, c * 512:(c + 1) * 512], ACT.Copy).then_inc(spec_hi, 1)

            mats_hi(0)
            rows_hi(0)
            for n in range(2 * GROUPS):
                c = n % 2
                if n >= 2:
                    act.wait_ge(spec_y, 2 * n - 2)
                act.wait_ge(spec_gm, 2 * n + 1)
                A_(ga[c][:, :], ps[2 * c][:, 512:1024], ACT.Copy).then_inc(spec_g, 1)
                act.wait_ge(spec_gm, 2 * n + 2)
                A_(gb[c][:, :], ps[2 * c + 1][:, 0:512], ACT.Copy).then_inc(spec_g, 1)
                if n + 1 < 2 * GROUPS:
                    rows_hi(n + 1)
                if c == 0 and n // 2 + 1 < GROUPS:
                    mats_hi(n // 2 + 1)
                if n:
                    spec_inverse(n - 1)
            spec_inverse(2 * GROUPS - 1)
            barrier(act, "act")

            def y_hi_of(e):
                act.wait_ge(y_made, e + 1)
                A_(A[:, 0, e, :], TT[2 + e % 2][:, :], ACT.Copy).then_inc(y_hi, 1)

            def skip_of(e):
                if e >= 2:
                    o = INV.index(("tile", e - 2))
                    act.wait_ge(evac[slot("inv", o)], turn("inv", o) + 1)
                A_(TT[e % 2][:, :], S[:, e, :], ACT.Copy, scale=vcol("skip", e)).then_inc(skip_made, 1)

            def around(e):
                if e:
                    y_hi_of(e - 1)
                    if e + 1 < KT:
                        skip_of(e + 1)

            skip_of(0)
            skip_of(1)
            for o, (kind, *j) in enumerate(INV):
                if kind == "rows":
                    c0, w, m0 = j
                    act.wait_ge(aux_done, A0["inv"] + o + 1)
                    A_(YB[0:HALF, m0:m0 + T // w, c0:c0 + w], ps[slot("inv", o)][0:HALF, :].rearrange("p (a b) -> p a b", b=w),
                       ACT.Copy).then_inc(evac[slot("inv", o)], 1)
                    if o and INV[o - 1][0] == "tile":
                        around(INV[o - 1][1])
                elif o + 1 == len(INV) or INV[o + 1][0] == "tile":
                    around(j[0])
            y_hi_of(KT - 1)

            def residual_squares(ph, n, src, gain=None):
                with act.Fori(0, 2) as i:
                    for u in range(4):
                        e = i * 4 + u
                        x = src[:, ds(e, 1), :].rearrange("p a t -> p (a t)")
                        act.wait_ge(evac[slot(ph, u)], turn(ph, u, i, 4) + 1)
                        steady(act)
                        if gain is not None:
                            gained_hi(n, x, H[:, 0, ds(e, 1), :].rearrange("p a t -> p (a t)"), vcol(gain, e))
                        act.wait_ge(n.acc, e + 1)
                        steady(act)
                        A_(TT[u % 2][:, :], x, ACT.Square).then_inc(n.sq, 1)

            residual_squares("wout", n2, X, "norm_ffn")
            rsqrt(n2)
            act.wait_ge(n2.rb, 1)
            A_(TT[3][:, :], ps[slot("norm2", 0)][:, :], ACT.Copy).then_inc(evac[slot("norm2", 0)], 1)

            def ff_act(f, t, g, gturn):
                act.wait_ge(evac[g], gturn + 1)
                steady(act)
                A_(TT[0][:, :], TT[0][:, :], ACT.Silu).then_inc(sg_made, 1)
                act.wait_ge(ff_prod, f + 1)
                steady(act)
                A_(A[:, 0, ds(t, 1), :].rearrange("p a t -> p (a t)"), TT[2][:, :], ACT.Copy).then_inc(ff_hi, 1)

            ff_act(0, 0, slot("first", 0), turn("first", 0))
            ff_act(1, 1, slot("second", 1), turn("second", 1))
            f0 = 0
            for p, nf in enumerate(FPARTS):
                last = p == len(FPARTS) - 1
                if last:
                    act.wait_ge(cx_in, 16)
                    for k in range(KT):
                        square(ncx, CX[:, k, :], k, SS)
                for q, (ph, trips) in enumerate(UPS[p]):
                    t0 = 2 * q if p else 2
                    with act.Fori(0, trips) as i:
                        for u in range(2):
                            g = slot(ph, 2 * u)
                            ff_act(i * 2 + (f0 + t0 + u), i * 2 + (t0 + u), g, turn(ph, 2 * u, i, 4))
                    if last:
                        if q == 0:
                            rsqrt(ncx, 2, cv, cr)
                        else:
                            norm_hi(ncx, lambda k: HC[0][:, k, :], lambda k: mod[:, k, 1:2], SS)
                f0 += nf
            with act.Fori(0, 2) as i:
                for u in range(4):
                    e = i * 4 + u
                    act.wait_ge(evac[slot("down2", u)], turn("down2", u, i, 4) + 1)
                    act.wait_ge(nf1.acc, e + 1)
                    steady(act)
                    x = X[:, ds(e, 1), :].rearrange("p a t -> p (a t)")
                    A_(TT[0][:, :], x, ACT.Square).then_inc(nf1.sq, 1)
                    act.wait_ge(n3.acc, e + 1)
                    steady(act)
                    A_(TT[1][:, :], x, ACT.Square, scale=vcol("norm_final", e)).then_inc(n3.sq, 1)
            rsqrt(n3, 16)
            act.wait_ge(nf1.rb, 1)
            A_(TT[3][:, :], ps[slot("normf", 0)][:, :], ACT.Copy).then_inc(evac[slot("normf", 0)], 1)
            norm_hi(n3, h_hi, lambda k: mod[:, k, 0:1])
            act.wait_ge(aux_done, A0["lr"] + 1)
            A_(LRT[0:48, T:T + TC], ps[slot("lr", 0)][0:48, 0:TC], ACT.Copy).then_inc(evac[slot("lr", 0)], 1)
            act.wait_ge(panel_done, N0["lrx"] + 1)
            A_(LRT[0:48, 0:T], ps[slot("lrx", 0)][0:48, :], ACT.Copy).then_inc(evac[slot("lrx", 0)], 1)
            for u in range(2):
                act.sem_inc(on_out[u], 16)
                act.sem_inc(ga_out[u], 16)
            with act.Fori(0, HEADS) as h:
                ch.enter(h, HEAD_ACT_STEPS)
                heads_act(act, h, ch)
                ch.leave(HEADS, HEAD_ACT_STEPS)

            for q, t in enumerate(O_ORDER):
                if q == 2:
                    act.wait_ge(on_made, 2 * HEADS)
                if t >= KT - 2:
                    src = OE[t % 2]
                else:
                    src = TT[q % 4 if q < 4 else q - 6]
                    act.wait_ge(on_in[q % 4 if q < 4 else q - 6], 16 if q < 4 else 32)
                if q >= 6:
                    act.wait_ge(za_lo, q - 1)
                A_(A[:, 0, t, :], src[:, :], ACT.Copy).then_inc(za_hi, 1)
                if q in (2, 3):
                    r = q - 2
                    act.wait_ge(za_lo, r + 1)
                    act.dma_start(TT[r][:, :], ond[O_ORDER[6 + r], :, :]).then_inc(on_in[r], 16)
                if q == 3:
                    for u in range(2):
                        act.wait_ge(ga_out[u], 16 * (HEADS + 1))
                    for k in range(4):
                        act.dma_start(X[:, 2 * k:2 * k + 2, :], gad[2 * k:2 * k + 2, :, :].rearrange("k p t -> p k t")
                                      ).then_inc(ga_in, 16)
            with act.Fori(0, 2) as i:
                for u in range(4):
                    e = i * 4 + u
                    act.wait_ge(ma_made, e + 1)
                    act.dma_start(mad[ds(e, 1), :, :].rearrange("k p t -> (k p) t"),
                                  X[:, ds(e, 1), :].rearrange("p a t -> p (a t)")).then_inc(ma_out, 16)
            act.wait_ge(pool_pad, 1)
            for g in range(4):
                if g:
                    act.wait_ge(aux_done, A0["pool"] + 2 * g)
                act.dma_start(wpl[:, :, :], d["wpool"][g].rearrange("p (k m) -> p k m", k=2)).then_inc(pool_in, 16)
                act.dma_start(icnt[:, :], d["icnt"][g]).then_inc(pool_in, 16)
                for u in range(2):
                    s = slot("pool", 6 * g + u)
                    act.wait_ge(panel_done, N0["pool"] + 4 * g + u + 1)
                    A_(up[u][:, PAD:PAD + T], ps[s][:, :], ACT.Copy).then_inc(evac[s], 1)
                for m in range(2):
                    s = slot("pool", 6 * g + 2 + m)
                    act.wait_ge(panel_done, N0["pool"] + 4 * g + 2 + m + 1)
                    A_(TT[m][:, :], ps[s][:, :], ACT.Silu).then_inc(evac[s], 1)
                for m in range(2):
                    act.wait_ge(evac[slot("pool", 6 * g + 4 + m)], turn("pool", 6 * g + 4 + m) + 1)
                    A_(A[:, 0, 2 * g + m, :], TT[2 + m][:, :], ACT.Copy).then_inc(pb_hi, 1)
            with act.Fori(0, 2) as i:
                for u in range(4):
                    e = i * 4 + u
                    act.wait_ge(panel_done, e + (N0["gb"] + 1))
                    steady(act)
                    A_(X[:, ds(e, 1), :].rearrange("p a t -> p (a t)"), ps[slot("gb", u)][:, :], ACT.Sigmoid
                       ).then_inc(evac[slot("gb", u)], 1)

            def ma_load(e, u):
                act.dma_start(TT[2 + u][:, :], mad[ds(e, 1), :, :].rearrange("k p t -> (k p) t")).then_inc(ma_in[u], 16)

            def merged_hi(e, u):
                act.wait_ge(mb_made, e + 1)
                steady(act)
                A_(H[:, 0, ds(e, 1), :].rearrange("p a t -> p (a t)"), TT[u][:, :], ACT.Copy).then_inc(m_hi, 1)

            act.wait_ge(pb_lo, KT)
            for u in range(2):
                ma_load(u, u)
            with act.Fori(0, KT // 2 - 1) as i:
                for u in range(2):
                    merged_hi(i * 2 + u, u)
                    ma_load(i * 2 + u + 2, u)
            for u in range(2):
                merged_hi(KT - 2 + u, u)
            xsv = xs.rearrange("(k p) t -> p k t", p=P)
            for k in range(KT):
                act.dma_start(XN[:, k, :], xsv[:, k, :]).then_inc(xr2_in, 16)
            residual_squares("wout2", n4, XN)
            rsqrt(n4)
            for k in range(KT):
                act.wait_ge(n4.h, k + 1)
                act.dma_start(out[k * P:(k + 1) * P, :], XN[:, k, :]).then_inc(out_st, 16)
            act.wait_ge(out_st, 16 * KT)

        @block.vector
        def _(dve):
            V_ = nc.vector
            ch = Steps(dve, dve_chain)

            def sum_start(n, acc, tiles=2):
                ch.link(V_.memset(acc, 0.0))
                dve.sem_inc(n.acc, tiles)

            def add_square(n, k, acc, tile, tiles=2):
                dve.wait_ge(n.sq, k + 1)
                V_.tensor_tensor(acc, acc, tile, ALU.add).then_inc(n.acc, 1)
                dve.wait_ge(n.acc, k + (tiles + 1))

            def newton(n, v, r, q):
                dve.wait_ge(n.r0, 1)
                ch.link(V_.tensor_tensor(q, r, r, ALU.mult))
                ch.link(V_.tensor_tensor(q, q, v, ALU.mult))
                ch.link(V_.tensor_scalar(q, q, -0.5, 1.5, ALU.mult, ALU.add))
                V_.tensor_tensor(r, r, q, ALU.mult).then_inc(n.r, 1)

            def norm_rstd(n, phase, v, r, q):
                w = v.shape[1]
                dve.wait_ge(aux_done, A0[phase] + 1)
                V_.tensor_scalar(v, ps[slot(phase, 0)][:, 0:w], 1.0 / D, EPS, ALU.mult, ALU.add).then_inc(n.var, 1)
                newton(n, v, r, q)

            def norm_tiles(n, phase, src, gain, hi=None, lo=None, shift=None, ring=TT, width=T):
                r = ps[slot(phase, 0)][:, 0:width]

                def low(k):
                    dve.wait_ge(n.hi, k + 1)
                    V_.scalar_tensor_tensor(out=lo(k), in0=ring[k % 2][:, :], scalar=shift(k), in1=hi(k).bitcast(F32),
                                            op0=ALU.add, op1=ALU.subtract).then_inc(n.lo, 1)

                dve.wait_ge(n.rb, 1)
                for k in range(KT):
                    if k >= 2 and hi is not None:
                        dve.wait_ge(n.lo, k - 1)
                    V_.scalar_tensor_tensor(out=src(k) if hi is None else ring[k % 2][:, :], in0=src(k),
                                            scalar=gain(k), in1=r, op0=ALU.mult, op1=ALU.mult).then_inc(n.h, 1)
                    if k and hi is not None:
                        low(k - 1)
                dve.wait_ge(n.h, KT)
                dve.sem_inc(evac[slot(phase, 0)], 1)
                if hi is not None:
                    low(KT - 1)

            def h_hi(k):
                return H[:, 0, k, :]

            def h_lo(k):
                return H[:, 1, k, :]

            def x_tile(k):
                return X[:, k, :]

            def argument(l):
                phase, u = f"mlp{l}", 0
                s = slot(phase, u)
                dve.wait_ge(aux_done, A0[phase] + 1)
                if l:
                    dve.wait_ge(sin_made, l)
                V_.tensor_scalar(fa[:, :], ps[s][:, :], vcol(f"f_b{l + 1}"), vcol("f_freq"), ALU.add, ALU.mult
                                 ).then_inc(evac[s], 1)
                dve.wait_ge(evac[s], turn(phase, u) + 1)
                ch.link(V_.tensor_scalar(fu[:, :], fa[:, :], 1.0 / (2 * np.pi), MAGIC, ALU.mult, ALU.add))
                ch.link(V_.tensor_scalar(fu[:, :], fu[:, :], MAGIC, None, ALU.subtract))
                for cst_ in (C1, C2, C3):
                    ch.link(V_.scalar_tensor_tensor(out=fa[:, :], in0=fu[:, :], scalar=-cst_, in1=fa[:, :],
                                                    op0=ALU.mult, op1=ALU.add))
                V_.tensor_scalar(fu[:, :], fa[:, :], PI_LOW, -PI_LOW, ALU.min, ALU.max).then_inc(arg_made, 1)

            def gained_lo(n, e, src, lo, hi, gain):
                dve.wait_ge(n.hi, e + 1)
                V_.scalar_tensor_tensor(out=lo, in0=src, scalar=gain, in1=hi.bitcast(F32), op0=ALU.mult, op1=ALU.subtract
                                        ).then_inc(n.lo, 1)

            sum_start(n1, TT[2][:, :])
            dve.wait_ge(vec_in, 16)
            for k in range(KT):
                gained_lo(n1, k, X[:, k, :], H[:, 1, k, :], H[:, 0, k, :], vcol("norm_mix", k))
                add_square(n1, k, TT[2][:, :], TT[k % 2][:, :])

            def v24(name):
                return vec[:, VEC[name]:VEC[name] + 24]

            t24 = TT[3][:, 0:24]
            ch.link(V_.tensor_tensor(t24, v24("cw0"), v24("cw1"), ALU.add))
            ch.link(V_.tensor_tensor(t24, t24, v24("cw2"), ALU.add))
            ch.link(V_.tensor_tensor(t24, t24, v24("b_in"), ALU.mult))
            ch.link(V_.tensor_tensor(v24("cb"), v24("cb"), t24, ALU.add))
            ch.link(V_.tensor_scalar(v24("b_in"), v24("b_in"), -1.0, None, ALU.mult))
            for t in hbs:
                i_ = V_.memset(t[:, :], 0.0)
            i_.then_inc(hb_zero, 1)
            argument(0)
            norm_rstd(n1, "norm1", nv[:, 0:8], nr[:, 0:8], nq[:, 0:8])
            dve.wait_ge(const_in, 16)
            dve.wait_ge(evac[slot("norm1", 0)], turn("norm1", 0) + 1)

            def z_tile(slot_, count, n, f):
                dve.wait_ge(panel_done, n + 1)
                V_.tensor_scalar(zp[:, 0:T + 2:T + 1], ones[:, 0:2], vcol("b_in", f), None, ALU.mult)
                V_.tensor_tensor(zp[:, 1:T + 1], ps[slot_][:, :], R1[:, :], ALU.mult).then_inc(evac[slot_], 1)
                dve.wait_ge(evac[slot_], count)

            def conv(n, f, t, dst):
                dve.wait_ge(c_made, n + 1)
                ch.link(V_.scalar_tensor_tensor(out=t, in0=zp[:, 0:T], scalar=vcol("cw0", f), in1=t,
                                                op0=ALU.mult, op1=ALU.add))
                ch.link(V_.scalar_tensor_tensor(out=dst, in0=zp[:, 2:T + 2], scalar=vcol("cw2", f), in1=t,
                                                op0=ALU.mult, op1=ALU.add))

            def s_conv(n, e, h):
                t = (ca, cb_)[h]
                conv(n, e + (8 + 8 * h), t[:, :], t[:, :])
                if h:
                    V_.tensor_tensor(S[:, ds(e, 1), :].rearrange("p a t -> p (a t)"), ca[:, :], cb_[:, :],
                                     ALU.mult).then_inc(s_made, 1)
                    dve.wait_ge(s_made, e + 1)

            for n in range(4):
                ph = f"zin{n}"
                z_tile(slot(ph, 0), turn(ph, 0) + 1, n, n // 2 + 8 + 8 * (n % 2))
                s_conv(n, n // 2, n % 2)
                if n < 2:
                    argument(n + 1)
            dve.wait_ge(silu_c, 1)
            with dve.Fori(0, 3) as i:
                ch.enter(i, 8 + 8 + 1)
                for u in range(4):
                    z_tile(slot("zin4", u), turn("zin4", u, i, 4) + 1, i * 4 + (N0["zin4"] + u),
                           i * 2 + (10 + 8 * (u % 2) + u // 2))
                    for j in range(2):
                        m = 2 * u + j
                        dve.wait_ge(mod_in[m % 4], i * 32 + 16 * (m // 4 + 1))
                        for w in range(2):
                            i_ = V_.tensor_tensor_reduce(mprod[:, :], mw[m % 4][:, :], crep[:, w * D:(w + 1) * D], 1.0, 0.0,
                                                         ALU.mult, ALU.add, macc[:, m, w:w + 1])
                            if w:
                                i_.then_inc(mod_used, 1)
                                dve.wait_ge(mod_used, i * 8 + (m + 1))
                            else:
                                ch.link(i_)
                    n, e = i * 4 + (N0["zin4"] + u), i * 2 + (2 + u // 2)
                    s_conv(n, e, u % 2)
                ch.link(V_.tensor_tensor(mod[:, ds(i * 8, 8), :], macc[:, :, :],
                                         vec[:, ds(i * 8 + VEC["b_mod"], 8)].unsqueeze(2).to_broadcast([P, 8, 2]), ALU.add))
                ch.leave(3, 8 + 8 + 1)
            ch.link(V_.tensor_scalar(mgs[:, :, :], mod[:, 8:16, :], 1.0, None, ALU.add))
            ch.link(V_.tensor_tensor(mgs[:, :, :], mgs[:, :, :],
                                     vec[:, VEC["norm2"]:VEC["norm2"] + 8].unsqueeze(2).to_broadcast([P, 8, 2]), ALU.mult))
            ch.link(V_.memset(gacc[:, :], 0.0))
            with dve.Fori(0, 2) as i:
                ch.enter(i, 16)
                for q in range(4):
                    o, g = 5 * q, i * 4 + q
                    z_tile(slot("mix", o), turn("mix", o, i, 20) + 1, g + N0["mix"], g)
                    for u in range(2):
                        s = slot("mix", o + 1 + u)
                        dve.wait_ge(aux_done, i * 16 + (A0["mix"] + 4 * q + 1 + u))
                        dve.wait_ge(decay_made, g * 2 + (u + 1))
                        V_.tensor_tensor(tap[u][:, :], ps[s][:, :], tap[u][:, :], ALU.mult).then_inc(evac[s], 1)
                    for u in range(2):
                        s = slot("mix", o + 1 + u)
                        dve.wait_ge(evac[s], turn("mix", o + 1 + u, i, 20) + 1)
                        ch.link(V_.scalar_tensor_tensor(out=tabs[:, :], in0=tap[u][:, :], scalar=-1.0, in1=tap[u][:, :],
                                                        op0=ALU.mult, op1=ALU.max))
                        V_.tensor_tensor(gacc[:, :], tabs[:, :], gacc[:, :], ALU.add).then_inc(tap_sum, 1)
                        dve.wait_ge(tap_sum, g * 2 + (u + 1))
                    conv(g + N0["mix"], g, ca[:, :], G0[:, ds(g, 1), :].rearrange("p a t -> p (a t)"))
                ch.leave(2, 16)
            with dve.Fori(0, N2 // 2) as i:
                for u in range(2):
                    s = slot("sfwd", 2 + u)
                    dve.wait_ge(aux_done, i * 4 + (A0["sfwd"] + 3 + u))
                    dve.wait_ge(s1_out[u], i * 16 + 16)
                    V_.tensor_copy(sa[u][:, :], ps[s][:, :]).then_inc(evac[s], 1)
            for u in range(2):
                dve.wait_ge(s1_out[u], 16 * (N2 // 2 + 1))
            s = slot("tapnorm", 0)
            dve.wait_ge(aux_done, A0["tapnorm"] + 1)
            V_.reciprocal(rn[:, :], ps[s][:, 0:8]).then_inc(evac[s], 1)
            def mats_lo(g):
                dve.wait_ge(spec_hi, mats_made(g))
                V_.tensor_tensor(kl[g % 2][:, :, :], kf[g % 3][:, 0:3, :], kh[g % 2][:, :, :].bitcast(F32), ALU.subtract
                                 ).then_inc(spec_lo, 1)

            def rows_lo(n):
                g, c = n // 2, n % 2
                dve.wait_ge(spec_hi, rows_made(n))
                V_.tensor_tensor(bl[c][:, :], bs[g % 2][:, c * 512:(c + 1) * 512], bh[c][:, :].bitcast(F32), ALU.subtract
                                 ).then_inc(spec_lo, 1)

            mats_lo(0)
            rows_lo(0)
            for n in range(2 * GROUPS):
                c = n % 2
                dve.wait_ge(spec_xm, n + 1)
                if n >= 2:
                    dve.wait_ge(spec_inv, n - 1)
                for q, (t, gg) in enumerate(((ya, ga), (yb, gb))):
                    dve.wait_ge(spec_g, 2 * n + q + 1)
                    V_.tensor_tensor(t[c][:, :], ps[2 * c][:, 0:512], gg[c][:, :], ALU.mult).then_inc(spec_y, 1)
                if n + 1 < 2 * GROUPS:
                    rows_lo(n + 1)
                if c == 0 and n // 2 + 1 < GROUPS:
                    mats_lo(n // 2 + 1)
            barrier(dve, "dve")

            def y_lo_of(e):
                dve.wait_ge(y_hi, e + 1)
                V_.tensor_tensor(A[:, 1, e, :], TT[2 + e % 2][:, :], A[:, 0, e, :].bitcast(F32), ALU.subtract
                                 ).then_inc(y_lo, 1)

            for e in range(KT):
                o = INV.index(("tile", e))
                s, y = slot("inv", o), TT[2 + e % 2]
                dve.wait_ge(skip_made, e + 1)
                if e >= 2:
                    dve.wait_ge(y_lo, e - 1)
                dve.wait_ge(aux_done, A0["inv"] + o + 1)
                V_.scalar_tensor_tensor(out=y[:, :].rearrange("p (a b) -> p a b", b=N2),
                                        in0=ps[s][:, :].rearrange("p (b a) -> p a b", a=HALF),
                                        scalar=rn[:, e:e + 1], in1=TT[e % 2][:, :].rearrange("p (a b) -> p a b", b=N2),
                                        op0=ALU.mult, op1=ALU.add).then_inc(evac[s], 1)
                dve.wait_ge(evac[s], turn("inv", o) + 1)
                V_.tensor_tensor(y[:, :], y[:, :], G0[:, e, :], ALU.mult).then_inc(y_made, 1)
                if e:
                    y_lo_of(e - 1)
            y_lo_of(KT - 1)

            dve.wait_ge(y_lo, KT)
            sum_start(n2, TT[2][:, :])
            dve.wait_ge(xr_in, 16)
            with dve.Fori(0, 2) as i:
                for u in range(4):
                    e = i * 4 + u
                    dve.wait_ge(panel_done, e + (N0["wout"] + 1))
                    x = X[:, ds(e, 1), :].rearrange("p a t -> p (a t)")
                    V_.scalar_tensor_tensor(out=x, in0=ps[slot("wout", u)][:, :], scalar=vcol("b_out", e), in1=x,
                                            op0=ALU.add, op1=ALU.add).then_inc(evac[slot("wout", u)], 1)
                    dve.wait_ge(evac[slot("wout", u)], turn("wout", u, i, 4) + 1)
                    gained_lo(n2, e, x, H[:, 1, ds(e, 1), :].rearrange("p a t -> p (a t)"),
                              H[:, 0, ds(e, 1), :].rearrange("p a t -> p (a t)"), vcol("norm_ffn", e))
                    add_square(n2, e, TT[2][:, :], TT[u % 2][:, :])
            norm_rstd(n2, "norm2", nv[:, 0:8], nr[:, 0:8], nq[:, 0:8])
            dve.wait_ge(evac[slot("norm2", 0)], turn("norm2", 0) + 1)

            def ff_dve(f, t, pg, pu, gs, gturn, us, uturn):
                dve.wait_ge(panel_done, pg)
                V_.tensor_tensor(TT[0][:, :], ps[gs][:, :], TT[3][:, :], ALU.mult).then_inc(evac[gs], 1)
                dve.wait_ge(panel_done, pu)
                V_.tensor_tensor(TT[2][:, :], ps[us][:, :], TT[3][:, :], ALU.mult).then_inc(evac[us], 1)
                dve.wait_ge(evac[us], uturn + 1)
                dve.wait_ge(sg_made, f + 1)
                V_.tensor_tensor(TT[2][:, :], TT[2][:, :], TT[0][:, :], ALU.mult).then_inc(ff_prod, 1)
                dve.wait_ge(ff_hi, f + 1)
                V_.tensor_tensor(A[:, 1, ds(t, 1), :].rearrange("p a t -> p (a t)"), TT[2][:, :],
                                 A[:, 0, ds(t, 1), :].rearrange("p a t -> p (a t)").bitcast(F32),
                                 ALU.subtract).then_inc(ff_lo, 1)
                dve.wait_ge(ff_lo, f + 1)

            def jobs2(a, u, b, v):
                return (N0[a] + u + 1, N0[b] + v + 1, slot(a, u), turn(a, u), slot(b, v), turn(b, v))

            ff_dve(0, 0, *jobs2("first", 0, "second", 0))
            ff_dve(1, 1, *jobs2("second", 1, "second", 2))
            ch.link(V_.tensor_tensor(gfm[:, :], mgs[:, :, 0], vec[:, VEC["norm_final"]:VEC["norm_final"] + 8], ALU.mult))
            f0 = 0
            for p, nf in enumerate(FPARTS):
                last = p == len(FPARTS) - 1
                if last:
                    sum_start(ncx, cxacc[:, :])
                    for k in range(KT):
                        add_square(ncx, k, cxacc[:, :], SS[k % 2][:, :])
                for q, (ph, trips) in enumerate(UPS[p]):
                    t0 = 2 * q if p else 2
                    with dve.Fori(0, trips) as i:
                        for u in range(2):
                            g, v = 2 * u, 2 * u + 1
                            ff_dve(i * 2 + (f0 + t0 + u), i * 2 + (t0 + u), i * 4 + (N0[ph] + g + 1),
                                   i * 4 + (N0[ph] + v + 1), slot(ph, g), turn(ph, g, i, 4), slot(ph, v),
                                   turn(ph, v, i, 4))
                    if last:
                        if q == 0:
                            norm_rstd(ncx, "normc", cv[:, :], cr[:, :], cq[:, :])
                            dve.sem_inc(evac[slot("normc", 0)], 1)
                        else:
                            norm_tiles(ncx, "normcb", lambda k: CX[:, k, :], lambda k: mgs[:, k, 1:2],
                                       lambda k: HC[0][:, k, :], lambda k: HC[1][:, k, :], lambda k: mod[:, k, 1:2],
                                       SS, TC)
                f0 += nf
                ph = f"down{p}"
                if last:
                    dve.wait_ge(ncx.h, KT)
                    sum_start(nf1, TT[2][:, :], 1)
                    sum_start(n3, TT[3][:, :], 1)
                with dve.Fori(0, 2) as i:
                    for u in range(4):
                        e = i * 4 + u
                        dve.wait_ge(panel_done, e + (N0[ph] + 1))
                        x = X[:, ds(e, 1), :].rearrange("p a t -> p (a t)")
                        V_.tensor_tensor(x, ps[slot(ph, u)][:, :], x, ALU.add).then_inc(evac[slot(ph, u)], 1)
                        dve.wait_ge(evac[slot(ph, u)], turn(ph, u, i, 4) + 1)
                        if last:
                            add_square(nf1, e, TT[2][:, :], TT[0][:, :], 1)
                            add_square(n3, e, TT[3][:, :], TT[1][:, :], 1)
            sl = slot("normf", 0)
            dve.wait_ge(aux_done, A0["normf"] + 1)
            ch.link(V_.tensor_scalar(nv[:, 0:8], ps[sl][:, 0:8], 1.0 / D, EPS, ALU.mult, ALU.add))
            ch.link(V_.tensor_scalar(nv[:, 8:16], ps[sl][:, 8:16], 1.0 / D, None, ALU.mult))
            V_.scalar_tensor_tensor(out=nv[:, 8:16], in0=nv[:, 0:8], scalar=EPS, in1=nv[:, 8:16],
                                    op0=ALU.mult, op1=ALU.add).then_inc(n3.var, 1)
            newton(n3, nv[:, :], nr[:, :], nq[:, :])
            dve.wait_ge(n3.r, 1)
            dve.sem_inc(nf1.r, 1)
            norm_tiles(n3, "norm3", x_tile, lambda k: gfm[:, k:k + 1], h_hi, h_lo, lambda k: mod[:, k, 0:1])
            dve.wait_ge(evac[slot("normf", 0)], turn("normf", 0) + 1)
            for k in range(KT):
                V_.scalar_tensor_tensor(out=X[:, k, :], in0=X[:, k, :], scalar=vcol("norm_final", k), in1=TT[3][:, :],
                                        op0=ALU.mult, op1=ALU.mult).then_inc(nf1.h, 1)
            dve.wait_ge(nf1.h, KT)
            with dve.Fori(0, HEADS) as h:
                ch.enter(h, HEAD_STEPS)
                heads_dve(dve, h, ch)
                ch.leave(HEADS, HEAD_STEPS)
            for q, t in enumerate(O_ORDER):
                if t < 2:
                    dve.wait_ge(ga_out[t], 16 * (HEADS + 1))
                src = OE[t % 2] if t >= KT - 2 else TT[q % 4 if q < 4 else q - 6]
                dve.wait_ge(za_hi, q + 1)
                V_.tensor_tensor(A[:, 1, t, :], src[:, :], A[:, 0, t, :].bitcast(F32), ALU.subtract).then_inc(za_lo, 1)
            dve.wait_ge(ga_in, 64)
            with dve.Fori(0, 2) as i:
                for u in range(4):
                    e, s = i * 4 + u, slot("mixa", u)
                    x = X[:, ds(e, 1), :].rearrange("p a t -> p (a t)")
                    dve.wait_ge(panel_done, e + (N0["mixa"] + 1))
                    V_.tensor_tensor(x, x, ps[s][:, :], ALU.mult).then_inc(evac[s], 1)
                    dve.wait_ge(evac[s], turn("mixa", u, i, 4) + 1)
                    dve.sem_inc(ma_made, 1)
            dve.wait_ge(ma_out, 16 * KT)
            for t in up:
                ch.do(V_.memset(t[:, 0:PAD], 0.0))
                ch.do(V_.memset(t[:, PAD + T:W_U], 0.0))
            ch.wait()
            dve.sem_inc(pool_pad, 1)
            for g, w in enumerate(POOL_WINDOWS):
                dve.wait_ge(pool_in, 32 * (g + 1))
                for u in range(2):
                    s = slot("pool", 6 * g + u)
                    dve.wait_ge(evac[s], turn("pool", 6 * g + u) + 1)
                    src, span, width, q = up[u], 1, W_U, 0
                    while span < w:
                        width -= span
                        dst = (wa, wb)[q % 2]
                        ch.link(V_.tensor_tensor(dst[:, 0:width], src[:, 0:width], src[:, span:span + width], ALU.add))
                        src, span, q = dst, span * 2, q + 1
                    lo = PAD - w // 2
                    ch.link(V_.tensor_tensor(pd[u][:, :], src[:, lo:lo + T], icnt[:, :], ALU.mult))
                    V_.tensor_tensor(pd[u][:, :], pd[u][:, :], up[u][:, PAD:PAD + T], ALU.subtract).then_inc(pd_made, 1)
                    dve.wait_ge(pd_made, 2 * g + u + 1)
                for m in range(2):
                    s = slot("pool", 6 * g + 4 + m)
                    dve.wait_ge(aux_done, A0["pool"] + 2 * g + m + 1)
                    dve.wait_ge(evac[slot("pool", 6 * g + 2 + m)], turn("pool", 6 * g + 2 + m) + 1)
                    V_.scalar_tensor_tensor(out=TT[2 + m][:, :], in0=ps[s][:, :], scalar=vcol("pool_scale", 2 * g + m),
                                            in1=TT[m][:, :], op0=ALU.mult, op1=ALU.mult).then_inc(evac[s], 1)
                    dve.wait_ge(pb_hi, 2 * g + m + 1)
                    V_.tensor_tensor(A[:, 1, 2 * g + m, :], TT[2 + m][:, :], A[:, 0, 2 * g + m, :].bitcast(F32),
                                     ALU.subtract).then_inc(pb_lo, 1)
                    dve.wait_ge(pb_lo, 2 * g + m + 1)
            with dve.Fori(0, KT // 4) as i:
                for u in range(4):
                    e, s, t = i * 4 + u, slot("mixb", u), TT[u % 2]
                    dve.wait_ge(panel_done, e + (N0["mixb"] + 1))
                    V_.tensor_tensor(t[:, :], X[:, ds(e, 1), :].rearrange("p a t -> p (a t)"), ps[s][:, :], ALU.mult
                                     ).then_inc(evac[s], 1)
                    dve.wait_ge(evac[s], turn("mixb", u, i, 4) + 1)
                    dve.wait_ge(ma_in[u % 2], i * 32 + 16 * (u // 2 + 1))
                    V_.tensor_tensor(t[:, :], t[:, :], TT[2 + u % 2][:, :], ALU.add).then_inc(mb_made, 1)
                    dve.wait_ge(m_hi, e + 1)
                    V_.tensor_tensor(H[:, 1, ds(e, 1), :].rearrange("p a t -> p (a t)"), t[:, :],
                                     H[:, 0, ds(e, 1), :].rearrange("p a t -> p (a t)").bitcast(F32), ALU.subtract
                                     ).then_inc(m_lo, 1)
                    dve.wait_ge(m_lo, e + 1)
            sum_start(n4, TT[2][:, :])
            dve.wait_ge(xr2_in, 16 * KT)
            with dve.Fori(0, 2) as i:
                for u in range(4):
                    e, s = i * 4 + u, slot("wout2", u)
                    dve.wait_ge(panel_done, e + (N0["wout2"] + 1))
                    x = XN[:, ds(e, 1), :].rearrange("p a t -> p (a t)")
                    V_.scalar_tensor_tensor(out=x, in0=ps[s][:, :],
                                            scalar=mod[:, ds(e + 16, 1), 0:1].rearrange("p a b -> p (a b)"), in1=x,
                                            op0=ALU.mult, op1=ALU.add).then_inc(evac[s], 1)
                    add_square(n4, e, TT[2][:, :], TT[u % 2][:, :])
            norm_rstd(n4, "norm4", nv[:, 0:8], nr[:, 0:8], nq[:, 0:8])
            norm_tiles(n4, "norm4", lambda k: XN[:, k, :], lambda k: vcol("final2", k))


def _constants():
    f8 = np.float64
    cst = np.zeros((P, NCST), np.float32)

    def put(name, a):
        cst[:a.shape[0], CST[name]:CST[name] + a.shape[1]] = a

    put("ident", np.eye(P))
    put("ones", np.ones((P, P)))
    j, i = np.meshgrid(np.arange(P), np.arange(P), indexing="ij")
    put("mask_f", (j <= i) * 1.0)
    put("mask_b", (j >= i) * 1.0)
    n1, k1 = np.arange(N1, dtype=f8)[:, None], np.arange(HALF, dtype=f8)[None, :]
    th = 2 * np.pi * n1 * (k1 + 0.5) / N1
    dft = np.stack([np.cos(th), -np.sin(th)], -1).reshape(N1, P)
    put("dft_s", dft[:HALF])
    put("dft_g", dft * np.where(np.arange(N1) < HALF, 1.0, -1.0)[:, None])
    inv = np.stack([np.cos(th[:HALF]), -np.sin(th[:HALF])], -1).reshape(HALF, P).T / (N1 * N2 / 2)
    put("idft", inv)
    r, n2 = np.arange(P)[:, None], np.arange(N2)[None, :]
    tok = np.where(r < HALF, N2 * r + n2, N2 * (N1 - r) - n2)
    none = tok >= T
    tok = np.where(none, 0, tok)
    t = np.linspace(0.0, 1.0, T, dtype=np.float32)
    put("tneg", -t[tok])
    put("tmask", np.where(none, -1e30, 0.0))
    w = (np.float32(2.0 * np.pi) * np.arange(T, dtype=np.float32) / np.float32(T))[:, None]
    bands = np.linspace(1e-4, 15, 16, dtype=np.float32)[None, :]
    arg = (bands * w).astype(f8)
    ft = np.concatenate([t[:, None], np.cos(arg), -np.sin(arg)], -1).astype(np.float32)
    cols = tok.reshape(2, HALF, N2).transpose(0, 2, 1).reshape(2, T)
    feat = np.concatenate([ft[cols[0]].T, ft[cols[1]].T], 0)
    kf = np.zeros((GROUPS, P, 5, P))
    a, b = np.arange(N2, dtype=f8)[:, None], np.arange(N2, dtype=f8)[None, :]
    for k in range(HALF):
        g, o = k // 4, (k % 4) * 32
        th = 2 * np.pi * (a * (k + 0.5) / (N1 * N2) + a * b / N2)
        c, s = np.cos(th), np.sin(th)
        re, im = np.concatenate([c, s], 0), np.concatenate([-s, c], 0)
        blk = kf[g, o:o + 32]
        blk[:, 0, o:o + 32] = np.concatenate([re, im], 1)
        blk[:, 1, o:o + 32] = np.concatenate([re, re], 1)
        blk[:, 2, o:o + 32] = np.concatenate([im, -im], 1)
        blk[:, 3, o:o + 32] = np.block([[c.T, s.T], [-s.T, c.T]])
        blk[:, 4, o:o + 32] = np.block([[-s.T, c.T], [c.T, s.T]])
    tt = np.arange(T)
    fr = np.float32(10000.0) ** (-np.arange(32, dtype=np.float32) / np.float32(32))
    cos, sin = np.zeros((P, T)), np.zeros((P, T))
    for p in range(P):
        pos = (tt // 64 if p < 64 else tt % 64).astype(np.float32)
        an = (pos * fr[p % 32]).astype(f8)
        cos[p] = np.cos(an)
        sin[p] = np.sin(an) * (-1 if p % 64 < 32 else 1)
    icnt = np.zeros((4, P, T))
    for g, wd in enumerate(POOL_WINDOWS):
        lo = np.clip(tt - wd // 2, 0, T - 1)
        hi = np.clip(tt + (wd - 1 - wd // 2), 0, T - 1)
        icnt[g] = 1.0 / (hi - lo + 1)
    f4 = lambda x: np.ascontiguousarray(x, np.float32)
    return {"cst": cst, "feat": f4(feat), "kfft": f4(kf.reshape(GROUPS, P, 5 * P)), "cos": f4(cos), "sin": f4(sin),
            "icnt": f4(icnt)}


def _layout(x):
    g = {k: np.asarray(v) for k, v in x.items()}
    cols = lambda a: np.asarray(a).reshape(-1, P).T
    vec = np.zeros((P, NVEC), np.float32)
    for name, a in (("norm_mix", g["norm_mix"]), ("norm_ffn", g["norm_ffn"]), ("norm_final", g["norm_final"]),
                    ("b_in", g["hy_b_in"]), ("cw0", g["hy_conv_w"][0, 0]), ("cw1", g["hy_conv_w"][0, 1]),
                    ("cw2", g["hy_conv_w"][0, 2]), ("cb", g["hy_conv_b"]), ("skip", g["hy_skip"]),
                    ("b_out", g["hy_b_out"]), ("norm2", g["norm_g_2"]), ("b_mod", g["b_mod_2"]),
                    ("b_gf", g["b_gate_f_2"]), ("b_gb", g["b_gate_b_2"]), ("gla_g", g["gla_norm_g_2"]),
                    ("pool_scale", g["pool_scale_2"]), ("final2", g["final_norm_g_2"])):
        a = cols(a)
        vec[:, VEC[name]:VEC[name] + a.shape[1]] = a
    for name, key in (("f_b1", "hy_f_b1"), ("f_b2", "hy_f_b2"), ("f_b3", "hy_f_b3"), ("f_freq", "hy_f_freq")):
        vec[:HALF, VEC[name]] = vec[HALF:, VEC[name]] = g[key][0]
    w1, w2, w3, wo = g["hy_f_w1"][0], g["hy_f_w2"][0], g["hy_f_w3"][0], g["hy_f_wout"][0]

    def twice(w):
        a = np.zeros((2 * w.shape[0], 2 * w.shape[1]), np.float32)
        a[:w.shape[0], :w.shape[1]] = w
        a[w.shape[0]:, w.shape[1]:] = w
        return a

    wtap = np.concatenate([wo[:, :D], wo[:, D:]], 0)
    dec = np.concatenate([np.repeat(g["hy_decay"][0, :1], HALF, 0), np.repeat(g["hy_decay"][0, 1:], HALF, 0)], 0)

    def panel(w):
        a = np.zeros((D, P), np.float32)
        a[:w.shape[0], :w.shape[1]] = w
        return a.reshape(8, P, P).transpose(1, 0, 2).reshape(P, D)

    out = []

    def add(w, f, rows=slice(None)):
        out.append(panel(w[rows, f * P:(f + 1) * P]))

    win, wi2 = g["hy_w_in"][0], g["w_in_2"][0]
    q_, k_, v_, za, lr, ub, zb, ga, gb = np.cumsum([0, 512, 512, 1024, 1024, 32, 1024, 1024, 1024])
    for f in range(8, 16):
        add(win, f)
        add(win, 8 + f)
    for f in range(8):
        add(win, f)
    for f in range(8):
        add(g["hy_w_out"][0], f)
    f0 = 0
    for nf in FPARTS:
        for f in range(f0, f0 + nf):
            add(g["ffn_w_gate"][0], f)
            add(g["ffn_w_up"][0], f)
        for f in range(8):
            add(g["ffn_w_down"][0], f, slice(f0 * P, (f0 + nf) * P))
        f0 += nf
    low = np.zeros((D, 48), np.float32)
    low[:, 0:16] = wi2[:, lr:lr + 16]
    low[:, 32:48] = wi2[:, lr + 16:lr + 32]
    out.append(panel(low))
    for h in range(HEADS):
        add(wi2[:, q_:k_], h)
        add(wi2[:, k_:v_], h)
        first = (N0["heads"] + 2) % 2
        for e in (first, 1 - first):
            add(wi2[:, v_:za], 2 * h + e)
        for w0 in (za, ga):
            for e in range(2):
                add(wi2[:, w0:w0 + D], 2 * h + e)
    for f in range(8):
        add(g["w_branch_a_2"][0], f)
    for q in range(4):
        for w0 in (ub, zb):
            for u in range(2):
                add(wi2[:, w0:w0 + D], 2 * q + u)
    for w, w0 in ((wi2, gb), (g["w_branch_b_2"][0], 0), (g["w_out_2"][0], 0)):
        for f in range(8):
            add(w[:, w0:w0 + D], f)
    assert len(out) == NPANELS - GROUPS
    modp = np.ascontiguousarray(g["w_mod_2"][0].T).reshape(24, P, D)
    cvec = np.concatenate([g["c_2"].reshape(-1), g["c_ctx_2"].reshape(-1)])[None]
    wup = np.zeros((48, HEADS * DK + DK), np.float32)
    wup[0:16, 0:HEADS * DK] = g["w_gate_up_f_2"][0]
    wup[32:48, 0:HEADS * DK] = g["w_gate_up_b_2"][0]
    wpool = g["w_pool_2"][0].reshape(4, 2, P, 256).transpose(0, 2, 1, 3).reshape(4, P, 512)
    c = np.ascontiguousarray
    return {"vec": vec, "xT": c(g["x"][0].T), "ctxT": c(g["ctx_2"][0].T), "panels": np.stack(out), "modp": modp, "cvec": cvec,
            "fw1": twice(w1), "fw2": twice(w2), "fw3": twice(w3), "wtap": c(wtap), "dec": c(dec), "wup": wup,
            "wpool": c(wpool)}


def kernel(**inputs):
    import concourse.bacc as _bacc
    from concourse.bass_utils import run_bass_kernel_spmd as _run

    arrays = {**_layout(inputs), **_constants()}
    nc = _bacc.Bacc("TRN2", target_bir_lowering=False, num_devices=1)
    args = {n: nc.dram_tensor(f"in_{n}", a.shape, F32, kind="ExternalInput").ap() for n, a in arrays.items()}
    out = nc.dram_tensor("out_T", (D, T), F32, kind="ExternalOutput").ap()
    program(nc, args, out)
    r = _run(nc, [{f"in_{n}": a for n, a in arrays.items()}], core_ids=[0])
    return np.ascontiguousarray(r.results[0]["out_T"].T)[None]
```
